# Optimizing a Trainium2 kernel written in Bass

```python
import math
import jax, jax.numpy as jnp
from jax import lax
import numpy as np
import jax
import jax.numpy as jnp

D_MODEL = 1024
BATCH = 1
SEQ = 256
DEPTH = 2

HEAD_DIM = 64
D_ATTN = D_MODEL // 2
ATTN_HEADS = D_ATTN // HEAD_DIM
Q_BLOCK = 128
D_CONV = D_MODEL // 4
CONV_K = 3
D_POOL = D_MODEL // 4
POOL_WINDOWS = (2, 4, 8, 16)
POOL_GROUPS = len(POOL_WINDOWS)
POOL_GROUP_DIM = D_POOL // POOL_GROUPS
POOL_OUT_DIM = D_MODEL // POOL_GROUPS
N_BRANCHES = 3
D_FF = -(-8 * D_MODEL // (3 * 256)) * 256
EPS = 1e-6

IN_SIZES = (D_ATTN, D_ATTN, D_ATTN, ATTN_HEADS, D_CONV, D_CONV, D_CONV, D_POOL, N_BRANCHES * D_MODEL)
D_IN = sum(IN_SIZES)
IN_SPLITS = tuple(int(v) for v in np.cumsum(IN_SIZES)[:-1])


def rmsnorm(x, g):
    xf = x.astype(jnp.float32)
    y = xf * lax.rsqrt(jnp.mean(xf * xf, axis=-1, keepdims=True) + EPS)
    return (y * g.astype(jnp.float32)).astype(x.dtype)

def forgetting_attention(q, k, v, logf):
    S = q.shape[2]
    c = jnp.cumsum(logf, axis=-1)
    scale = HEAD_DIM ** -0.5
    outs = []
    for i in range(S // Q_BLOCK):
        q0, q1 = i * Q_BLOCK, (i + 1) * Q_BLOCK
        qb = q[:, :, q0:q1]
        kb = k[:, :, :q1]
        vb = v[:, :, :q1]
        logits = jnp.einsum('bhqd,bhkd->bhqk', qb, kb, preferred_element_type=jnp.float32) * scale
        logits = logits + (c[:, :, q0:q1, None] - c[:, :, None, :q1])
        causal = (q0 + jnp.arange(Q_BLOCK))[:, None] >= jnp.arange(q1)[None, :]
        logits = jnp.where(causal, logits, -jnp.inf)
        p = jax.nn.softmax(logits, axis=-1)
        outs.append(jnp.einsum('bhqk,bhkd->bhqd', p.astype(vb.dtype), vb))
    return jnp.concatenate(outs, axis=2)

def short_conv_mixer(u, b_gate, c_gate, w):
    S = u.shape[1]
    z = c_gate * u
    zp = jnp.pad(z, ((0, 0), (CONV_K - 1, 0), (0, 0)))
    conv = w[0] * zp[:, 0:S]
    for j in range(1, CONV_K):
        conv = conv + w[j] * zp[:, j:j + S]
    return b_gate * conv

def pooling_mixer(u, w_grp, scale):
    Bsz, S, _ = u.shape
    uf = u.astype(jnp.float32)
    cs = jnp.cumsum(uf, axis=1)
    t = jnp.arange(S, dtype=jnp.float32)
    groups = []
    for g, w in enumerate(POOL_WINDOWS):
        sl = slice(g * POOL_GROUP_DIM, (g + 1) * POOL_GROUP_DIM)
        csg = cs[:, :, sl]
        lagged = jnp.pad(csg[:, :S - w], ((0, 0), (w, 0), (0, 0)))
        counts = jnp.minimum(t + 1.0, float(w))[None, :, None]
        groups.append((csg - lagged) / counts - uf[:, :, sl])
    d = jnp.stack(groups, axis=2).astype(u.dtype)
    out = jnp.einsum('bsgc,gcd->bsgd', d, w_grp).reshape(Bsz, S, D_MODEL)
    return out * scale

def first_inputs(seed: int = 0) -> dict:
    key = jax.random.key(seed)
    ks = jax.random.split(key, 16)
    nrm = lambda k, shape, fan_in: jax.random.normal(k, shape, jnp.float32) * (fan_in ** -0.5)
    return {
        "x": jax.random.normal(ks[0], (BATCH, SEQ, D_MODEL), jnp.float32),
        "norm_mix_g": 1.0 + 0.02 * jax.random.normal(ks[1], (DEPTH, D_MODEL), jnp.float32),
        "w_in": nrm(ks[2], (DEPTH, D_MODEL, D_IN), D_MODEL),
        "forget_b": jax.random.uniform(ks[3], (DEPTH, ATTN_HEADS), jnp.float32, 2.0, 5.0),
        "q_norm_g": 1.0 + 0.02 * jax.random.normal(ks[4], (DEPTH, HEAD_DIM), jnp.float32),
        "k_norm_g": 1.0 + 0.02 * jax.random.normal(ks[5], (DEPTH, HEAD_DIM), jnp.float32),
        "w_attn_out": nrm(ks[6], (DEPTH, D_ATTN, D_MODEL), D_ATTN),
        "conv_w": nrm(ks[7], (DEPTH, CONV_K, D_CONV), CONV_K),
        "w_conv_out": nrm(ks[8], (DEPTH, D_CONV, D_MODEL), D_CONV),
        "pool_w": nrm(ks[9], (DEPTH, POOL_GROUPS, POOL_GROUP_DIM, POOL_OUT_DIM), POOL_GROUP_DIM),
        "pool_scale": 1.0 + 0.1 * jax.random.normal(ks[10], (DEPTH, D_MODEL), jnp.float32),
        "w_o": nrm(ks[11], (DEPTH, D_MODEL, D_MODEL), D_MODEL),
        "norm_ffn_g": 1.0 + 0.02 * jax.random.normal(ks[12], (DEPTH, D_MODEL), jnp.float32),
        "w_ffn_in": nrm(ks[13], (DEPTH, D_MODEL, 2 * D_FF), D_MODEL),
        "w_ffn_out": nrm(ks[14], (DEPTH, D_FF, D_MODEL), D_FF),
    }

def first_block(x, norm_mix_g, w_in, forget_b, q_norm_g, k_norm_g, w_attn_out, conv_w,
              w_conv_out, pool_w, pool_scale, w_o, norm_ffn_g, w_ffn_in, w_ffn_out):
    Bsz, S, _ = x.shape

    def heads(t):
        return t.reshape(Bsz, S, ATTN_HEADS, HEAD_DIM).transpose(0, 2, 1, 3)

    for l in range(DEPTH):
        h = rmsnorm(x, norm_mix_g[l])
        proj = h @ w_in[l]
        q, k, v, f_logit, cx, cb, cc, px, gate_logit = jnp.split(proj, IN_SPLITS, axis=-1)

        qh = rmsnorm(heads(q), q_norm_g[l])
        kh = rmsnorm(heads(k), k_norm_g[l])
        vh = heads(v)
        logf = jax.nn.log_sigmoid((f_logit + forget_b[l]).astype(jnp.float32)).transpose(0, 2, 1)
        a = forgetting_attention(qh, kh, vh, logf).transpose(0, 2, 1, 3).reshape(Bsz, S, D_ATTN)
        y_attn = a @ w_attn_out[l]

        y_conv = short_conv_mixer(cx, cb, cc, conv_w[l]) @ w_conv_out[l]

        y_pool = pooling_mixer(px, pool_w[l], pool_scale[l])

        g = jax.nn.sigmoid(gate_logit).reshape(Bsz, S, N_BRANCHES, D_MODEL)
        merged = g[:, :, 0] * y_attn + g[:, :, 1] * y_conv + g[:, :, 2] * y_pool
        x = x + merged @ w_o[l]

        h = rmsnorm(x, norm_ffn_g[l])
        gt, up = jnp.split(h @ w_ffn_in[l], 2, axis=-1)
        x = x + (jax.nn.silu(gt) * up) @ w_ffn_out[l]
    return x


N_MIXERS = 2
N_MLA_LAYERS = (DEPTH + 1) // 2
N_DIL_LAYERS = DEPTH // 2

MLA_HEADS = 16
MLA_NOPE = 64
MLA_ROPE = 32
MLA_QK = MLA_NOPE + MLA_ROPE
MLA_V = 64
Q_LORA = 3 * D_MODEL // 8
KV_LORA = D_MODEL // 4
MLA_IN = Q_LORA + KV_LORA + MLA_ROPE
ROPE_THETA = 10000.0

DIL_GROUPS = ((128, 1), (512, 4), (2048, 16))
N_DIL_GROUPS = len(DIL_GROUPS)
DIL_HEADS = 16
DIL_HEAD_DIM = 64
DIL_IN = N_DIL_GROUPS * 3 * DIL_HEADS * DIL_HEAD_DIM

N_BUCKETS = 32
MAX_DISTANCE = 1024

D_FF_2 = 4 * D_MODEL
N_MOD = 6


def rms_norm(x, g):
    xf = x.astype(jnp.float32)
    y = xf * lax.rsqrt(jnp.mean(xf * xf, axis=-1, keepdims=True) + EPS)
    return (y * g.astype(jnp.float32)).astype(x.dtype)

def rope(x, pos):
    half = x.shape[-1] // 2
    inv = 1.0 / (ROPE_THETA ** (jnp.arange(half, dtype=jnp.float32) / half))
    ang = pos.astype(jnp.float32)[..., None] * inv
    ang = ang.reshape(ang.shape[:2] + (1,) * (x.ndim - 3) + (half,))
    cos, sin = jnp.cos(ang), jnp.sin(ang)
    x1 = x[..., :half].astype(jnp.float32)
    x2 = x[..., half:].astype(jnp.float32)
    out = jnp.concatenate([x1 * cos - x2 * sin, x2 * cos + x1 * sin], axis=-1)
    return out.astype(x.dtype)

def t5_bucket(rel):
    nb = N_BUCKETS // 2
    max_exact = nb // 2
    ret = jnp.where(rel > 0, nb, 0)
    n = jnp.abs(rel)
    nf = jnp.maximum(n, 1).astype(jnp.float32)
    large = max_exact + (jnp.log(nf / max_exact) / math.log(MAX_DISTANCE / max_exact)
                         * (nb - max_exact)).astype(jnp.int32)
    large = jnp.minimum(large, nb - 1)
    return ret + jnp.where(n < max_exact, n, large)

def dense_attention(q, k, v, scale):
    B, S, H, Dk = q.shape
    nq = S // Q_BLOCK
    qb = jnp.moveaxis(q.reshape(B, nq, Q_BLOCK, H, Dk), 1, 0)

    def block(qi):
        s = jnp.einsum('bqhd,bkhd->bhqk', qi, k, preferred_element_type=jnp.float32) * scale
        p = jax.nn.softmax(s, axis=-1).astype(v.dtype)
        return jnp.einsum('bhqk,bkhd->bqhd', p, v)

    o = lax.map(block, qb)
    return jnp.moveaxis(o, 0, 1).reshape(B, S, H, v.shape[-1])

def mla_mixer(h, pos, w_in, g_qa, w_qb, g_kva, w_kvb, g_q, g_k, w_o):
    B, S, _ = h.shape
    proj = h @ w_in
    q_lat = proj[..., :Q_LORA]
    kv_lat = proj[..., Q_LORA:Q_LORA + KV_LORA]
    k_rope = rope(proj[..., Q_LORA + KV_LORA:], pos)
    q = (rms_norm(q_lat, g_qa) @ w_qb).reshape(B, S, MLA_HEADS, MLA_QK)
    kv = (rms_norm(kv_lat, g_kva) @ w_kvb).reshape(B, S, MLA_HEADS, MLA_NOPE + MLA_V)
    q = jnp.concatenate([q[..., :MLA_NOPE], rope(q[..., MLA_NOPE:], pos)], axis=-1)
    k = jnp.concatenate([kv[..., :MLA_NOPE],
                         jnp.broadcast_to(k_rope[:, :, None, :], (B, S, MLA_HEADS, MLA_ROPE))],
                        axis=-1)
    v = kv[..., MLA_NOPE:]
    q = rms_norm(q, g_q)
    k = rms_norm(k, g_k)
    o = dense_attention(q, k, v, MLA_QK ** -0.5)
    return o.reshape(B, S, MLA_HEADS * MLA_V) @ w_o

def _to_residues(t, dilation):
    B, S = t.shape[:2]
    L = S // dilation
    t = t.reshape((B, L, dilation) + t.shape[2:])
    t = jnp.moveaxis(t, 2, 1)
    return t.reshape((B * dilation, L) + t.shape[3:])

def _from_residues(t, batch, dilation):
    L = t.shape[1]
    t = t.reshape((batch, dilation, L) + t.shape[2:])
    t = jnp.moveaxis(t, 1, 2)
    return t.reshape((batch, L * dilation) + t.shape[3:])

def dilated_group(q, k, v, pos, bias_table, window, dilation):
    B, S, H, Dh = q.shape
    half = window // (2 * dilation)
    blk = half
    L = S // dilation
    nb = -(-L // blk)
    Lp = nb * blk
    padq = Lp - L
    N = B * dilation
    qr, kr, vr, pr = (_to_residues(t, dilation) for t in (q, k, v, pos))
    qb = jnp.pad(qr, ((0, 0), (0, padq), (0, 0), (0, 0))).reshape(N, nb, blk, H, Dh)

    def key_blocks(t):
        pad = [(0, 0), (blk, padq + blk)] + [(0, 0)] * (t.ndim - 2)
        t = jnp.pad(t, pad).reshape((N, nb + 2, blk) + t.shape[2:])
        return jnp.concatenate([t[:, :-2], t[:, 1:-1], t[:, 2:]], axis=2)

    kb, vb, pk = key_blocks(kr), key_blocks(vr), key_blocks(pr)
    pq = jnp.pad(pr, ((0, 0), (0, padq))).reshape(N, nb, blk)
    qi = jnp.arange(nb)[:, None] * blk + jnp.arange(blk)[None, :]
    ki = jnp.arange(nb)[:, None] * blk - blk + jnp.arange(3 * blk)[None, :]
    valid = ((ki[:, None, :] >= 0) & (ki[:, None, :] < L)
             & (jnp.abs(qi[:, :, None] - ki[:, None, :]) <= half))
    bucket = t5_bucket(pk[:, :, None, :] - pq[:, :, :, None])
    bias = jnp.moveaxis(bias_table[bucket], -1, 2).astype(jnp.float32)
    s = jnp.einsum('nbqhd,nbkhd->nbhqk', qb, kb,
                   preferred_element_type=jnp.float32) * (DIL_HEAD_DIM ** -0.5) + bias
    s = jnp.where(valid[None, :, None], s, -jnp.inf)
    lse = jax.nn.logsumexp(s, axis=-1)
    p = jnp.exp(s - lse[..., None]).astype(v.dtype)
    o = jnp.einsum('nbhqk,nbkhd->nbqhd', p, vb).reshape(N, Lp, H, Dh)[:, :L]
    lse = jnp.moveaxis(lse, 2, 3).reshape(N, Lp, H)[:, :L]
    return _from_residues(o, B, dilation), _from_residues(lse, B, dilation)

def dilated_mixer(h, pos, w_in, g_q, g_k, rel_bias, w_o):
    B, S, _ = h.shape
    proj = (h @ w_in).reshape(B, S, N_DIL_GROUPS, 3, DIL_HEADS, DIL_HEAD_DIM)
    outs, lses = [], []
    for gi, (window, dilation) in enumerate(DIL_GROUPS):
        q = rms_norm(proj[:, :, gi, 0], g_q[gi])
        k = rms_norm(proj[:, :, gi, 1], g_k[gi])
        v = proj[:, :, gi, 2]
        table = rel_bias[:, gi * DIL_HEADS:(gi + 1) * DIL_HEADS]
        o, lse = dilated_group(q, k, v, pos, table, window, dilation)
        outs.append(o)
        lses.append(lse)
    o_all = jnp.stack(outs, axis=0)
    wts = jax.nn.softmax(jnp.stack(lses, axis=0), axis=0)
    o = jnp.einsum('gbsh,gbshd->bshd', wts.astype(o_all.dtype), o_all)
    return o.reshape(B, S, DIL_HEADS * DIL_HEAD_DIM) @ w_o

def second_inputs(seed: int = 0) -> dict:
    key = jax.random.key(seed)
    ks = jax.random.split(key, 24)
    f32 = jnp.float32
    nrm = lambda k, shape, s: jax.random.normal(k, shape, f32) * s
    gain = lambda k, shape: 1.0 + 0.05 * jax.random.normal(k, shape, f32)
    D = D_MODEL
    return {
        "x": nrm(ks[0], (BATCH, SEQ, D), 1.0),
        "c": nrm(ks[1], (BATCH, D), 1.0),
        "positions": jnp.broadcast_to(jnp.arange(SEQ, dtype=jnp.int32), (BATCH, SEQ)),
        "ada_w": nrm(ks[2], (DEPTH, D, N_MOD * D), 0.5 * D ** -0.5),
        "ada_b": nrm(ks[3], (DEPTH, N_MOD * D), 0.02),
        "norm_mix": gain(ks[4], (DEPTH, D)),
        "norm_mlp": gain(ks[5], (DEPTH, D)),
        "mlp_w1": nrm(ks[6], (DEPTH, D, D_FF_2), D ** -0.5),
        "mlp_w2": nrm(ks[7], (DEPTH, D_FF_2, D), D_FF_2 ** -0.5),
        "mla_w_in": nrm(ks[8], (N_MLA_LAYERS, D, MLA_IN), D ** -0.5),
        "mla_g_qa": gain(ks[9], (N_MLA_LAYERS, Q_LORA)),
        "mla_w_qb": nrm(ks[10], (N_MLA_LAYERS, Q_LORA, MLA_HEADS * MLA_QK), Q_LORA ** -0.5),
        "mla_g_kva": gain(ks[11], (N_MLA_LAYERS, KV_LORA)),
        "mla_w_kvb": nrm(ks[12], (N_MLA_LAYERS, KV_LORA, MLA_HEADS * (MLA_NOPE + MLA_V)), KV_LORA ** -0.5),
        "mla_g_q": gain(ks[13], (N_MLA_LAYERS, MLA_QK)),
        "mla_g_k": gain(ks[14], (N_MLA_LAYERS, MLA_QK)),
        "mla_w_o": nrm(ks[15], (N_MLA_LAYERS, MLA_HEADS * MLA_V, D), (MLA_HEADS * MLA_V) ** -0.5),
        "dil_w_in": nrm(ks[16], (N_DIL_LAYERS, D, DIL_IN), D ** -0.5),
        "dil_g_q": gain(ks[17], (N_DIL_LAYERS, N_DIL_GROUPS, DIL_HEAD_DIM)),
        "dil_g_k": gain(ks[18], (N_DIL_LAYERS, N_DIL_GROUPS, DIL_HEAD_DIM)),
        "dil_w_o": nrm(ks[19], (N_DIL_LAYERS, DIL_HEADS * DIL_HEAD_DIM, D), (DIL_HEADS * DIL_HEAD_DIM) ** -0.5),
        "rel_bias": nrm(ks[20], (N_BUCKETS, N_DIL_GROUPS * DIL_HEADS), 0.3),
    }

def second_block(x, c, positions, ada_w, ada_b, norm_mix, norm_mlp, mlp_w1, mlp_w2,
              mla_w_in, mla_g_qa, mla_w_qb, mla_g_kva, mla_w_kvb, mla_g_q, mla_g_k, mla_w_o,
              dil_w_in, dil_g_q, dil_g_k, dil_w_o, rel_bias):
    B, S, D = x.shape
    cond = jax.nn.silu(c)
    for i in range(DEPTH):
        mod = (cond @ ada_w[i] + ada_b[i]).reshape(B, N_MOD, D)
        shift1, scale1, gate1 = mod[:, 0, None, :], mod[:, 1, None, :], mod[:, 2, None, :]
        shift2, scale2, gate2 = mod[:, 3, None, :], mod[:, 4, None, :], mod[:, 5, None, :]
        h = rms_norm(x, norm_mix[i]) * (1 + scale1) + shift1
        j = i // N_MIXERS
        if i % N_MIXERS == 0:
            y = mla_mixer(h, positions, mla_w_in[j], mla_g_qa[j], mla_w_qb[j], mla_g_kva[j],
                          mla_w_kvb[j], mla_g_q[j], mla_g_k[j], mla_w_o[j])
        else:
            y = dilated_mixer(h, positions, dil_w_in[j], dil_g_q[j], dil_g_k[j], rel_bias, dil_w_o[j])
        x = x + gate1 * y
        h = rms_norm(x, norm_mlp[i]) * (1 + scale2) + shift2
        x = x + gate2 * (jnp.square(jax.nn.relu(h @ mlp_w1[i])) @ mlp_w2[i])
    return x


def setup_inputs(seed=0):
    out = dict(first_inputs(seed))
    for name, value in second_inputs(seed + 1).items():
        if name != "x":
            out[name + "_2"] = value
    return out


def reference(
    x, norm_mix_g, w_in, forget_b, q_norm_g, k_norm_g, w_attn_out, conv_w, w_conv_out, pool_w,
    pool_scale, w_o, norm_ffn_g, w_ffn_in, w_ffn_out, c_2, positions_2, ada_w_2, ada_b_2,
    norm_mix_2, norm_mlp_2, mlp_w1_2, mlp_w2_2, mla_w_in_2, mla_g_qa_2, mla_w_qb_2, mla_g_kva_2,
    mla_w_kvb_2, mla_g_q_2, mla_g_k_2, mla_w_o_2, dil_w_in_2, dil_g_q_2, dil_g_k_2, dil_w_o_2,
    rel_bias_2,
):
    x = first_block(
        x, norm_mix_g, w_in, forget_b, q_norm_g, k_norm_g, w_attn_out, conv_w, w_conv_out,
        pool_w, pool_scale, w_o, norm_ffn_g, w_ffn_in, w_ffn_out,
    )
    return second_block(
        x, c_2, positions_2, ada_w_2, ada_b_2, norm_mix_2, norm_mlp_2, mlp_w1_2, mlp_w2_2,
        mla_w_in_2, mla_g_qa_2, mla_w_qb_2, mla_g_kva_2, mla_w_kvb_2, mla_g_q_2, mla_g_k_2,
        mla_w_o_2, dil_w_in_2, dil_g_q_2, dil_g_k_2, dil_w_o_2, rel_bias_2,
    )


_drawn_inputs = setup_inputs


def setup_inputs(seed=0):
    import zlib

    import numpy as np

    out = dict(_drawn_inputs(seed))
    spreads = {}
    factors = {'q_norm_g': 8.0,
     'k_norm_g': 8.0,
     'norm_ffn_g': 3.127,
     'norm_mix_2': 8.0,
     'norm_mlp_2': 2.954,
     'mla_g_qa_2': 8.0,
     'mla_w_qb_2': 3.361,
     'mla_g_kva_2': 8.0,
     'mla_g_q_2': 8.0,
     'mla_g_k_2': 8.0,
     'dil_g_q_2': 8.0,
     'dil_g_k_2': 8.0,
     'rel_bias_2': 8.0}
    for name, (base, spread) in spreads.items():
        noise = np.random.default_rng([zlib.crc32(name.encode()), seed]).standard_normal(out[name].shape)
        drawn = base * np.exp(spread * noise) if base else spread * noise
        out[name] = jnp.asarray(drawn.astype(out[name].dtype))
    for name, factor in factors.items():
        out[name] = (out[name] * factor).astype(out[name].dtype)
    return out
```

```python
from contextlib import ExitStack

import concourse.bass as bass
from concourse import mybir

F32 = mybir.dt.float32
F32R = mybir.dt.float32r
BF16 = mybir.dt.bfloat16
I32 = mybir.dt.int32
ALU = mybir.AluOpType
ACT = mybir.ActivationFunctionType
AX = mybir.AxisListType.X

P = 128
S = 256
TT = S // P
D = 1024
DK = D // P
DEPTH = 2
EPS = 1e-6
H1, HD = 8, 64
DA = H1 * HD
DC = D // 4
FF1 = 2816
NF1 = FF1 // 256
FF2 = 4 * D
NF2 = FF2 // 256
MH, MQK, MNOPE, MROPE = 16, 96, 64, 32
QL, KVL = 384, 256
DH = 16
NG = 3
HB = 4
F_AT = 3 * DA
CX_AT = F_AT + H1
CB_AT, CC_AT, PX_AT, G_AT = CX_AT + DC, CX_AT + 2 * DC, CX_AT + 3 * DC, CX_AT + 4 * DC
POOL_WINDOWS = (2, 4, 8, 16)
PAD = 16
DIL = ((128, 1), (512, 4), (2048, 16))
NEG = -1e30

RAW = 3
SPL = 3
WB, AB = 3, 5
AR = 3
NP_ADA = 48
NU = S // 8

_FAR = [15, 27, 50, 91, 166, 305, 559]


def bucket_steps():
    edges = list(range(1, 9)) + _FAR
    steps = [(-1e9, 15)]
    for b in range(14, -1, -1):
        steps.append((float(-(edges[b] - 1)), b))
    for b in range(1, 16):
        steps.append((float(edges[b - 1]), 16 + b))
    return steps


def host_constants():
    import numpy as np
    c = {}
    c["ident"] = np.eye(P, dtype=np.float32)
    q, k = np.arange(P)[:, None], np.arange(S)[None, :]
    tri = np.where(q >= k[:, :P], 0.0, NEG).astype(np.float32)
    c["causal"] = np.concatenate([tri, np.zeros((P, P), np.float32), tri], axis=1)
    i, j = np.arange(S)[:, None], np.arange(S)[None, :]
    dil = np.stack([np.where(((i - j) % r == 0) & (np.abs(i - j) // r <= w // (2 * r)), 0.0, NEG)
                    for w, r in DIL], axis=1).astype(np.float32)
    c["dilmask"] = dil.reshape(TT, P, NG * S)
    inv = np.zeros((P, 2, S), np.float32)
    for g, w in enumerate(POOL_WINDOWS):
        inv[(g % 2) * 64:(g % 2) * 64 + 64, g // 2] = 1.0 / np.minimum(np.arange(S) + 1.0, w)
    c["invcount"] = inv.reshape(P, 2 * S)
    half = MROPE // 2
    c["freq"] = np.tile((1.0 / (10000.0 ** (np.arange(half, dtype=np.float32) / half))).astype(np.float32), (P, 1))
    steps = bucket_steps()
    m = np.zeros((32, 96), np.float32)
    thr = np.full((96, 1), 1e9, np.float32)
    for n, (lo, b) in enumerate(steps):
        for part in range(3):
            m[b, 32 * part + n] += 1.0
            if n:
                m[steps[n - 1][1], 32 * part + n] -= 1.0
            thr[32 * part + n] = lo
    c["stepmat"], c["thr"] = m, thr
    return c


def block_pair(nc, ins, out):
    A = ins
    with ExitStack() as ctx:
        def sem(name):
            return ctx.enter_context(nc.semaphore(name))

        def sb(name, shape, dt=F32, at=None):
            return (at or ctx).enter_context(nc.sbuf_tensor(name, shape, dt))

        bias_dram = nc.dram_tensor("bias_scratch", (TT, DH, P, NG * S), F32, kind="Internal").ap()

        raw = [sb(f"raw{i}", [P, 2048]) for i in range(RAW)]
        whi = [sb(f"whi{i}", [P, 2048], F32R) for i in range(SPL)]
        wlo = [sb(f"wlo{i}", [P, 2048], F32R) for i in range(SPL)]
        x = sb("x", [P, TT, D])
        hT_hi, hT_lo = sb("hT_hi", [P, DK, S], F32R), sb("hT_lo", [P, DK, S], F32R)
        aT_hi, aT_lo = sb("aT_hi", [P, DK, S], F32R), sb("aT_lo", [P, DK, S], F32R)
        h32 = [sb(f"h32_{i}", [P, 2, S]) for i in range(2)]
        ident = sb("ident", [P, P])
        causal = sb("causal", [P, 3 * P])
        invcount = sb("invcount", [P, 2, S])
        ones = sb("ones", [P, 1])
        mhalf = sb("mhalf", [P, 32])
        ss, ms, rstd = (sb(n, [P, 2, 32]) for n in ("ss", "ms", "rstd"))
        NA_ROWS, NB_ROWS = 105, 108
        colA, colB = sb("colA", [P, NA_ROWS]), sb("colB", [P, NB_ROWS])
        fb = sb("fb", [H1, DEPTH])
        csil = sb("csil", [P, DK])
        mods = sb("mods", [P, DEPTH, 48])
        gain2 = sb("gain2", [P, DEPTH, 2, DK])
        cosn, sinn = sb("cosn", [P, TT, 16]), sb("sinn", [P, TT, 16])
        poolw = sb("poolw", [P, 2, S])
        gq8 = sb("gq8", [P, 8])
        nmax, zsum, rz = (sb(n, [P, 2, TT]) for n in ("nmax", "zsum", "rz"))
        mx = sb("mx", [P, 2, TT])

        def c_mix(l): return 8 * l
        def c_ffn(l): return 16 + 8 * l
        def c_psc(l): return 32 + 8 * l
        def c_mix2(l): return 48 + 8 * l
        def c_mlp2(l): return 64 + 8 * l
        def c_conv(l, j): return 80 + 6 * l + 2 * j
        C_COND, C_QA, C_KVA = 92, 100, 103
        def b_ada(l): return 48 * l
        B_Q1, B_K1, B_DQ, B_DK, B_MQ, B_MK = 96, 98, 100, 103, 106, 107

        with ExitStack() as ph:
            rowA, rowB = sb("rowA", [NA_ROWS, P], at=ph), sb("rowB", [NB_ROWS, P], at=ph)
            pos_t = sb("pos_t", [P, TT], I32, ph)
            posf = sb("posf", [P, TT], at=ph)
            freq = sb("freq", [P, 16], at=ph)
            ang = sb("ang", [P, 6, TT * 16], at=ph)
            angi = sb("angi", [P, TT * 16], I32, ph)
        with ExitStack() as ph:
            sq1 = sb("sq1", [P, D], at=ph)
            xn1 = sb("xn1", [P, TT, D], at=ph)
        with ExitStack() as ph:
            gates = sb("gates", [P, 24, S], at=ph)
            qT1, kT1 = sb("qT1", [P, 4, S], at=ph), sb("kT1", [P, 4, S], at=ph)
            V1 = sb("V1", [P, TT, DA], at=ph)
            zf, tf = sb("zf", [H1, S], at=ph), sb("tf", [H1, S], at=ph)
            mf, ncum = sb("mf", [H1, S], at=ph), sb("ncum", [H1, S], at=ph)
            zero8 = sb("zero8", [H1, S], at=ph)
            sqh = [sb(f"sqh{i}", [P, 512], at=ph) for i in range(2)]
            qn = [sb(f"qn{i}", [P, TT, 256], at=ph) for i in range(2)]
            cxs, cbs = sb("cxs", [P, 2, S], at=ph), sb("cbs", [P, 2, S], at=ph)
            zc = sb("zc", [P, 2, S + 2], at=ph)
            cva, cvb = sb("cva", [P, 2, S], at=ph), sb("cvb", [P, 2, S], at=ph)
            pu, s2, s4 = (sb(n, [P, 2, S + PAD], at=ph) for n in ("pu", "s2", "s4"))
            s8, s16 = (sb(n, [P, S + PAD], at=ph) for n in ("s8", "s16"))
            pd = sb("pd", [P, 2, S], at=ph)
            L1, P1 = ([sb(f"{n}{i}", [P, 3 * P], at=ph) for i in range(2)] for n in ("L1_", "P1_"))
            PT1 = [sb(f"PT1_{i}", [P, 3 * P], at=ph) for i in range(2)]
            mg = gates[:, 2 * DK:3 * DK, :]
            mt = [sb(f"mt{i}", [P, 2, S], at=ph) for i in range(2)]
        with ExitStack() as ph:
            sqf = sb("sqf", [P, D], at=ph)
            xnf = sb("xnf", [P, TT, D], at=ph)
            ada_raw = [sb(f"ada_raw{i}", [P, D], at=ph) for i in range(AR)]
            ada_tmp = [sb(f"ada_tmp{i}", [P, D], at=ph) for i in range(2)]
            ada_acc = sb("ada_acc", [P, 6 * D], at=ph)
            sg = [sb(f"sg{i}", [P, 2, S], at=ph) for i in range(2)]
            dmask = sb("dmask", [P, NG, S], at=ph)
            posb = sb("posb", [96, S], I32, ph)
            hi16, lo16 = sb("hi16", [96, S], at=ph), sb("lo16", [96, S], at=ph)
            ihi, ilo = sb("ihi", [96, S], I32, ph), sb("ilo", [96, S], I32, ph)
            relk, relq = sb("relk", [96, S], at=ph), sb("relq", [96, S], at=ph)
            thr = sb("thr", [96, 1], at=ph)
            stepmat = sb("stepmat", [32, 96], at=ph)
            relb = sb("relb", [32, NG * DH], at=ph)
            dres = sb("dres", [96, 3, NG * DH], at=ph)
            dpart = sb("dpart", [96, 3, NG * DH], BF16, ph)
            dsel = sb("dsel", [96, NG * DH], BF16, ph)
            Gst = [sb(f"Gst{i}", [96, 8, P], BF16, ph) for i in range(2)]
            stage = sb("stage", [P, NG * DH, 32], at=ph)
        with ExitStack() as ph:
            sqm = sb("sqm", [P, D], at=ph)
            xnm = sb("xnm", [P, TT, D], at=ph)
        with ExitStack() as ph:
            lat = sb("lat", [P, TT, 672], at=ph)
            latn = sb("latn", [P, TT, 640], at=ph)
            q96 = sb("q96", [P, TT, MH * MQK], at=ph)
            rt = sb("rt", [P, 4, TT * MH * 16], at=ph)
            qTm, kTm = sb("qTm", [MQK, MH, S], at=ph), sb("kTm", [MQK, MH, S], at=ph)
            Vm = sb("Vm", [P, TT, MH * 64], at=ph)
            krope = sb("krope", [P, TT, MROPE], at=ph)
            sq96 = sb("sq96", [P, MH * MQK], at=ph)
        with ExitStack() as ph:
            Pm = [sb(f"Pm{i}", [P, TT, S], at=ph) for i in range(2)]
            PTm = [sb(f"PTm{i}", [P, TT, S], at=ph) for i in range(2)]
            gbc0 = sb("gbc0", [P, D], at=ph)
            gy0 = [sb(f"gy0_{i}", [P, TT, 256], at=ph) for i in range(2)]
        with ExitStack() as ph:
            sqd = sb("sqd", [P, D], at=ph)
            xnd = sb("xnd", [P, TT, D], at=ph)
        with ExitStack() as ph:
            qTd, kTd = sb("qTd", [P, NG, 2, S], at=ph), sb("kTd", [P, NG, 2, S], at=ph)
            Vd = sb("Vd", [P, NG, TT, 256], at=ph)
            sqh2 = [sb(f"sqh2_{i}", [P, 512], at=ph) for i in range(2)]
            qn2 = [sb(f"qn2_{i}", [P, TT, 256], at=ph) for i in range(2)]
            biasb = [sb(f"biasb{i}", [P, TT, NG * S], at=ph) for i in range(2)]
            Ld = [sb(f"Ld{i}", [P, TT, NG * S], at=ph) for i in range(2)]
            PTd = sb("PTd", [P, NG, TT, S], at=ph)
            gbc = sb("gbc", [P, D], at=ph)
            gy1 = [sb(f"gy1_{i}", [P, TT, 256], at=ph) for i in range(2)]
        with ExitStack() as ph:
            sqp = sb("sqp", [P, D], at=ph)
            xnp = sb("xnp", [P, TT, D], at=ph)
            rl = [sb(f"rl{i}", [P, 2, S], at=ph) for i in range(2)]
            gbc2 = sb("gbc2", [P, D], at=ph)
            gy2 = sb("gy2", [P, 512], at=ph)

        bank = [ctx.enter_context(nc.psum_tensor(f"bank{i}", [P, 512], F32)) for i in range(WB + AB)]

        s_raw = [sem(f"raw_arrived{i}") for i in range(RAW)]
        s_hi, s_lo = sem("high_part_ready"), sem("low_part_ready")
        s_w, s_a, s_acc = sem("projection_summed"), sem("attention_summed"), sem("down_chunk_added")
        drained = [sem(f"bank_drained{i}") for i in range(WB + AB)]
        s_rows, s_const, s_set = sem("rows_loaded"), sem("constants_loaded"), sem("memsets_done")
        s_cols, s_ropein, s_rope = sem("columns_ready"), sem("angles_ready"), sem("rope_ready")
        s_x = sem("x_loaded")
        s_ss, s_ms, s_rstd, s_xn = sem("squares_summed"), sem("mean_square_ready"), sem("rstd_ready"), sem("x_normed")
        s_hhi, s_hlo = sem("h_high_ready"), sem("h_low_ready")
        s_sq = sem("head_squares_ready")
        s_z, s_zt, s_cum = sem("forget_logit_ready"), sem("forget_softplus_ready"), sem("forget_sum_ready")
        s_cv, s_cvhi, s_cvlo = sem("conv_ready"), sem("conv_high_ready"), sem("conv_low_ready")
        s_pd = sem("pool_ready")
        s_logit, s_nmax, s_exp, s_prob = (sem(n) for n in ("logits_ready", "row_max_ready", "exp_ready", "probs_ready"))
        s_athi, s_atlo = sem("attn_high_ready"), sem("attn_low_ready")
        s_hidhi, s_hidlo = sem("hidden_high_ready"), sem("hidden_low_ready")
        s_ada = [sem(f"ada_arrived{i}") for i in range(AR)]
        s_adaused, s_adasum, s_csil = sem("ada_piece_used"), sem("ada_summed"), sem("cond_ready")
        s_bin, s_bprep, s_step, s_g = sem("bias_inputs_loaded"), sem("bias_prep"), sem("bucket_steps_ready"), sem("steps_built")
        s_bout, s_bld = sem("bias_stored"), [sem(f"bias_loaded{i}") for i in range(2)]
        s_mods, s_latn, s_q96, s_sq96 = sem("mods_ready"), sem("latent_normed"), sem("heads_normed"), sem("head96_squares")
        s_poolw, s_set0, s_freq = sem("pool_weights_loaded"), sem("rows_cleared"), sem("frequencies_loaded")
        s_final, s_latss, s_hn = sem("result_ready"), sem("latent_squares_summed"), sem("head_squares_summed")
        s_roped, s_sum96, s_hid32 = sem("heads_rotated"), sem("head96_squares_summed"), sem("hidden_ready")
        s_x2, s_mg = sem("x_updated"), sem("branches_merged")
        s_dc, s_ac, s_pc = sem("vector_step"), sem("scalar_step"), sem("pool_step")
        s_out = sem("out_stored")

        chunks, chunk_at, names = [], {}, []

        def chunk(name, src):
            chunk_at[name] = len(chunks)
            names.append(name)
            chunks.append(src)

        def kmajor(w, c0, n):
            return w[:, c0:c0 + n].rearrange("(k p) n -> p k n", p=P)

        for l in range(DEPTH):
            w_in = A["w_in"][l]
            chunk(("F", l), kmajor(w_in, F_AT, P))
            for n, c0 in (("Q", 0), ("K", DA), ("V", 2 * DA)):
                for c in range(2):
                    chunk((n, l, c), kmajor(w_in, c0 + 256 * c, 256))
            for n, c0 in (("PX", PX_AT), ("CX", CX_AT), ("CC", CC_AT), ("CB", CB_AT)):
                chunk((n, l), kmajor(w_in, c0, 256))
            for c in range(12):
                chunk(("G", l, c), kmajor(w_in, G_AT + 256 * c, 256))
            chunk(("CO", l), kmajor(A["w_conv_out"][l], 0, D))
            for c in range(2):
                chunk(("AO", l, c), kmajor(A["w_attn_out"][l], 512 * c, 512))
            for c in range(4):
                chunk(("WO", l, c), kmajor(A["w_o"][l], 256 * c, 256))
            for c in range(NF1 + 1):
                if c < NF1:
                    chunk(("GT", l, c), kmajor(A["w_ffn_in"][l], 256 * c, 256))
                    chunk(("UP", l, c), kmajor(A["w_ffn_in"][l], FF1 + 256 * c, 256))
                if c:
                    chunk(("DN", l, c - 1), kmajor(A["w_ffn_out"][l][256 * (c - 1):256 * c, :], 0, D))
        for i in range(DEPTH):
            if i == 0:
                for c in range(3):
                    chunk(("LI", c), kmajor(A["mla_w_in_2"][0], 256 * c, min(256, 672 - 256 * c)))
                for c in range(4):
                    chunk(("QB", c), kmajor(A["mla_w_qb_2"][0], 384 * c, 384))
                for c in range(2):
                    chunk(("KV", c), kmajor(A["mla_w_kvb_2"][0], D * c, D))
                for c in range(4):
                    chunk(("MO", 0, c), kmajor(A["mla_w_o_2"][0], 256 * c, 256))
            else:
                for j in range(4):
                    for g in range(NG):
                        for n in range(3):
                            chunk(("D", j, g, n), kmajor(A["dil_w_in_2"][0], (3 * g + n) * D + 256 * j, 256))
                for c in range(4):
                    chunk(("MO", 1, c), kmajor(A["dil_w_o_2"][0], 256 * c, 256))
            for c in range(NF2 + 1):
                if c < NF2:
                    chunk(("M1", i, c), kmajor(A["mlp_w1_2"][i], 256 * c, 256))
                if c:
                    chunk(("M2", i, c - 1), kmajor(A["mlp_w2_2"][i][256 * (c - 1):256 * c, :], 0, D))

        def view(buf, c):
            kk, n = chunks[c].shape[1:]
            return buf[:, 0:kk * n].rearrange("p (k n) -> p k n", k=kk)

        h_done, n_pairs = {}, 0
        for name, k in ((("nrm", 0), 4), (("mg", 0), 4), (("nrm", 1), 4), (("nrm", 2), 4), (("mg", 1), 4),
                        (("nrm", 3), 4), (("nrm", 4), 4), (("lat",), 3), (("nrm", 5), 4), (("nrm", 6), 4),
                        (("nrm", 7), 4)):
            n_pairs += k
            h_done[name] = n_pairs

        CONSTS, BIN, N_ROWS_DMA = 16 * 5, 16 * 5, 27
        jobs, chunk_done = {}, []
        def unit1(l, h): return 8 * l + h
        def unitm(h): return 16 + h
        def unitd(h): return 32 + h

        def full(eng, name):
            s, n, b, _ = jobs[name]
            eng.wait_ge(s, n)
            return bank[b]

        def drain_sem(name):
            return drained[jobs[name][2]]

        def emptied(eng, name):
            _, _, b, k = jobs[name]
            eng.wait_ge(drained[b], k)

        block = ctx.enter_context(nc.Block())

        @block.tensor
        def _(pe):
            n = {"w": 0, "a": 0, "acc": 0, "c": 0}
            ended = {"w": 0, "a": 0}

            def begin(kind, name):
                j, nb = n[kind], (WB if kind == "w" else AB)
                n[kind] += 1
                b = j % nb + (WB if kind == "a" else 0)
                if j >= nb:
                    pe.wait_ge(drained[b], j // nb)
                jobs[name] = (kind, None, b, j // nb + 1)
                return bank[b]

            def end(ins, name):
                kind, _, b, k = jobs[name]
                s = s_w if kind == "w" else s_a
                ins.then_inc(s, 1)
                ended[kind] += 1
                jobs[name] = (s, ended[kind], b, k)

            def weights(name):
                c = chunk_at[name]
                assert c == n["c"], (name, c, n["c"])
                n["c"] += 1
                pe.wait_ge(s_lo, c + 1)
                return view(whi[c % SPL], c), view(wlo[c % SPL], c)

            def used(name):
                chunk_done.append(jobs[name][:2])

            def mm3(dst, lh, ll, rh, rl, start, stop):
                pe.matmul(dst, lh, rh, start=start, stop=False)
                pe.matmul(dst, lh, rl, start=False, stop=False)
                return pe.matmul(dst, ll, rh, start=False, stop=stop)

            def feature_major(name, w, cols, a_hi, a_lo, k0, kk):
                bk = begin("w", name)
                for t, c0 in enumerate(cols):
                    for k in range(kk):
                        m = mm3(bk[:, S * t:S * t + S], w[0][:, k, c0:c0 + P], w[1][:, k, c0:c0 + P],
                                a_hi[:, k0 + k, :], a_lo[:, k0 + k, :], k == 0, k == kk - 1)
                end(m, name)

            def token_major(name, w, c0, nc_, a_hi, a_lo, k0, kk, toks=(0, 1)):
                bk = begin("w", name)
                for i, t in enumerate(toks):
                    for k in range(kk):
                        m = mm3(bk[:, 256 * i:256 * i + nc_], a_hi[:, k0 + k, P * t:P * t + P],
                                a_lo[:, k0 + k, P * t:P * t + P], w[0][:, k, c0:c0 + nc_], w[1][:, k, c0:c0 + nc_],
                                k == 0, k == kk - 1)
                end(m, name)

            def turn(name, src, nblk, w=P):
                bk = begin("w", name)
                for i in range(nblk):
                    for t in range(TT):
                        m = pe.transpose(bk[0:w, S * i + P * t:S * i + P * t + P], src(i, t), ident[:, :])
                end(m, name)

            def norm(e, xn):
                pe.wait_ge(s_xn, 2 * e + 2)
                for kp in range(DK // 2):
                    turn(("nrm", e, kp), lambda i, t: xn[:, t, P * (2 * kp + i):P * (2 * kp + i) + P], 2)

            def qk_turn(r, job, buf):
                emptied(pe, job)
                turn(("qkT", r), lambda i, t: buf[:, t, P * i:P * i + P], 2)

            pe.wait_ge(s_const, CONSTS)
            pe.wait_ge(s_rows, 16 * N_ROWS_DMA)
            pe.wait_ge(s_set, 1)
            bk = begin("w", "colA")
            end(pe.transpose(bk[:, 0:NA_ROWS], rowA[:, :], ident[0:NA_ROWS, 0:NA_ROWS]), "colA")
            bk = begin("w", "colB")
            end(pe.transpose(bk[:, 0:NB_ROWS], rowB[:, :], ident[0:NB_ROWS, 0:NB_ROWS]), "colB")

            def head_out(u, name, vt, kts, kind="a"):
                if u % 2 == 0:
                    begin(kind, name)
                bk = bank[jobs[name][2]]
                r0 = 64 * (u % 2)
                for i, (kt, rhs, q0) in enumerate(kts):
                    m = pe.matmul(bk[r0:r0 + 64, q0:S], vt(kt), rhs, start=i == 0, stop=i == len(kts) - 1)
                if u % 2:
                    end(m, name)

            def ffn_down(key, c, accs, nf, hid0):
                w = weights((key[0], key[1], c))
                pe.wait_ge(s_hidlo, hid0 + c + 1)
                sl = 2 * (c % 3)
                for t in range(TT):
                    for half in range(2):
                        for k in range(2):
                            m = mm3(accs[2 * t + half][:, :], aT_hi[:, sl + k, P * t:P * t + P],
                                    aT_lo[:, sl + k, P * t:P * t + P], w[0][:, k, 512 * half:512 * half + 512],
                                    w[1][:, k, 512 * half:512 * half + 512], c == 0 and k == 0, c == nf - 1 and k == 1)
                n["acc"] += 1
                m.then_inc(s_acc, 1)
                chunk_done.append((s_acc, n["acc"]))
                if c == nf - 1:
                    for q in range(4):
                        nm = (key[0], key[1], "sum", q)
                        jobs[nm] = (s_acc, n["acc"]) + jobs[nm][2:]

            for l in range(DEPTH):
                norm(2 * l, xn1)
                pe.wait_ge(s_hlo, h_done[("nrm", 2 * l)])
                w = weights(("F", l))
                bk = begin("w", ("F", l))
                for k in range(DK):
                    m = mm3(bk[:, 0:S], w[0][:, k, :], w[1][:, k, :], hT_hi[:, k, :], hT_lo[:, k, :], k == 0, k == DK - 1)
                end(m, ("F", l))
                used(("F", l))
                order = [("Q", 0), ("Q", 1), ("K", 0), ("K", 1), ("V", 0), ("V", 1)]
                for i, (nm, c) in enumerate(order):
                    w = weights((nm, l, c))
                    token_major((nm, l, c), w, 0, 256, hT_hi, hT_lo, 0, DK)
                    used((nm, l, c))
                    if 1 <= i <= 4:
                        r = 4 * l + i - 1
                        qk_turn(r, (order[i - 1][0], l, order[i - 1][1]), qn[r % 2])
                for nm in ("PX", "CX", "CC", "CB"):
                    w = weights((nm, l))
                    feature_major((nm, l), w, (0, P), hT_hi, hT_lo, 0, DK)
                    used((nm, l))

                def gate(c):
                    w = weights(("G", l, c))
                    feature_major(("G", l, c), w, (0, P), hT_hi, hT_lo, 0, DK)
                    used(("G", l, c))

                emptied(pe, ("qkT", 4 * l + 3))
                emptied(pe, ("V", l, 1))
                emptied(pe, ("qkT", 4 * l + 2))
                emptied(pe, ("qkT", 4 * l + 1))
                pe.wait_ge(s_cum, l + 1)
                g = 0
                for i in range(H1 + 2):
                    if i < H1:
                        u = unit1(l, i)
                        bk = begin("a", ("S", u))
                        r0, t = 64 * (i % 2), i // 2
                        for q0, q1, c0 in ((0, P, 0), (P, S, P)):
                            pe.matmul(bk[:, c0:c0 + q1], qT1[r0:r0 + 64, t, q0:q1], kT1[r0:r0 + 64, t, 0:q1],
                                      start=True, stop=False)
                            m = pe.matmul(bk[:, c0:c0 + q1], ident[0:H1, i:i + 1].broadcast_to([H1, P]),
                                          ncum[:, 0:q1], start=False, stop=True)
                        end(m, ("S", u))
                    if g < 12:
                        gate(g)
                        g += 1
                    if 1 <= i <= H1:
                        u = unit1(l, i - 1)
                        pe.wait_ge(s_prob, u + 1)
                        bk = begin("a", ("T", u))
                        pr = P1[u % 2]
                        pe.transpose(bk[:, 0:P], pr[:, 0:P], ident[:, :])
                        pe.transpose(bk[:, P:2 * P], pr[:, P:2 * P], ident[:, :])
                        end(pe.transpose(bk[:, 2 * P:3 * P], pr[:, 2 * P:3 * P], ident[:, :]), ("T", u))
                    if g < 12 and i % 4 == 0:
                        gate(g)
                        g += 1
                    if i >= 2:
                        u = unit1(l, i - 2)
                        emptied(pe, ("T", u))
                        pt = PT1[u % 2]
                        head_out(u, ("O", u // 2), lambda kt, h=i - 2: V1[:, kt, 64 * h:64 * h + 64],
                                 [(0, pt[:, 0:S], 0), (1, pt[:, S:3 * P], P)])
                while g < 12:
                    gate(g)
                    g += 1
                pe.wait_ge(s_poolw, 16 * (l + 1))
                pe.wait_ge(s_pd, l + 1)
                for gi in range(4):
                    bk = begin("w", ("YP", l, gi))
                    r0 = 64 * (gi % 2)
                    for half in range(2):
                        m = pe.matmul(bk[:, S * half:S * half + S], poolw[r0:r0 + 64, gi // 2, P * half:P * half + P],
                                      pd[r0:r0 + 64, gi // 2, :], start=True, stop=True)
                    end(m, ("YP", l, gi))
                w = weights(("CO", l))
                pe.wait_ge(s_cvlo, l + 1)
                for jp in range(4):
                    feature_major(("YC", l, jp), w, (256 * jp, 256 * jp + P), aT_hi, aT_lo, 4, 2)
                used(("YC", l, 3))
                pe.wait_ge(s_atlo, 4 * (l + 1))
                for c in range(2):
                    w = weights(("AO", l, c))
                    for jp in range(2):
                        feature_major(("YA", l, 2 * c + jp), w, (256 * jp, 256 * jp + P), aT_hi, aT_lo, 0, 4)
                    used(("YA", l, 2 * c + 1))
                pe.wait_ge(s_hlo, h_done[("mg", l)])
                for c in range(4):
                    w = weights(("WO", l, c))
                    token_major(("WO", l, c), w, 0, 256, hT_hi, hT_lo, 0, DK)
                    used(("WO", l, c))
                norm(2 * l + 1, xnf)
                pe.wait_ge(s_hlo, h_done[("nrm", 2 * l + 1)])
                pe.wait_ge(s_bin, BIN * (l + 1))
                bk = begin("w", ("steps", l))
                end(pe.matmul(bk[0:96, 0:NG * DH], stepmat[:, :], relb[:, :], start=True, stop=True), ("steps", l))
                accs = None
                for c in range(NF1 + 1):
                    if c < NF1:
                        for nm in ("GT", "UP"):
                            w = weights((nm, l, c))
                            feature_major((nm, l, c), w, (0, P), hT_hi, hT_lo, 0, DK)
                            used((nm, l, c))
                        for u in range(3 * c, min(3 * c + 3, NU)):
                            pe.wait_ge(s_g, NU * l + u + 1)
                            bk = begin("w", ("B", l, u))
                            gb = Gst[(NU * l + u) % 2]
                            for k in range(8):
                                m = pe.matmul(bk[:, 48 * k:48 * k + 48], gb[:, k, :], dsel[:, :], start=True, stop=True)
                            end(m, ("B", l, u))
                    if c:
                        if c == 1:
                            accs = [begin("a", ("DN", l, "sum", q)) for q in range(4)]
                        ffn_down(("DN", l), c - 1, accs, NF1, NF1 * l)
                pe.wait_ge(s_adasum, l + 1)
                bk = begin("w", ("mod", l))
                for k in range(48):
                    m = pe.matmul(bk[:, k:k + 1], ada_acc[:, P * k:P * k + P], ones[:, :], start=True, stop=True)
                end(m, ("mod", l))

            def gate_rows(e, col0, i):
                pe.wait_ge(s_mods, i + 1)
                for half in range(2):
                    bk = begin("w", ("gb", e, half))
                    for k in range(4):
                        kk = col0 + 4 * half + k
                        m = pe.matmul(bk[:, P * k:P * k + P], mods[:, i, kk:kk + 1].broadcast_to([P, P]), ident[:, :],
                                      start=True, stop=True)
                    end(m, ("gb", e, half))

            def wo(i):
                gate_rows(2 * i, 16, i)
                pe.wait_ge(s_atlo, 8 * (i + 2))
                for c in range(4):
                    w = weights(("MO", i, c))
                    token_major(("MO", i, c), w, 0, 256, aT_hi, aT_lo, 0, DK)
                    used(("MO", i, c))

            def mlp(i):
                norm(5 + 2 * i, xnp)
                gate_rows(2 * i + 1, 40, i)
                pe.wait_ge(s_hlo, h_done[("nrm", 5 + 2 * i)])
                accs = None
                for c in range(NF2 + 1):
                    if c < NF2:
                        w = weights(("M1", i, c))
                        feature_major(("M1", i, c), w, (0, P), hT_hi, hT_lo, 0, DK)
                        used(("M1", i, c))
                    if c:
                        if c == 1:
                            accs = [begin("a", ("M2", i, "sum", q)) for q in range(4)]
                        ffn_down(("M2", i), c - 1, accs, NF2, 2 * NF1 + NF2 * i)

            norm(4, xnm)
            pe.wait_ge(s_hlo, h_done[("nrm", 4)])
            for c in range(3):
                w = weights(("LI", c))
                token_major(("LI", c), w, 0, min(256, 672 - 256 * c), hT_hi, hT_lo, 0, DK)
                used(("LI", c))
            pe.wait_ge(s_latn, 1)
            for kp in range(3):
                turn(("latT", kp), lambda i, t: latn[:, t, P * (2 * kp + i):P * (2 * kp + i) + P], 2 if kp < 2 else 1)
            pe.wait_ge(s_hlo, h_done[("lat",)])
            for c in range(4):
                w = weights(("QB", c))
                for t in range(TT):
                    token_major(("QB", c, t), w, 0, 384, hT_hi, hT_lo, 0, 3, (t,))
                used(("QB", c, 1))
            pe.wait_ge(s_q96, 1)
            for hp in range(MH // 2):
                turn(("qT", hp), lambda i, t: q96[:, t, MQK * (2 * hp + i):MQK * (2 * hp + i) + MQK], 2, MQK)
            for c in range(2):
                w = weights(("KV", c))
                for t in range(TT):
                    for half in range(2):
                        token_major(("KV", c, t, half), w, 512 * half, 512, hT_hi, hT_lo, 3, 2, (t,))
                used(("KV", c, 1, 1))
            pe.wait_ge(s_q96, 2)
            for hp in range(MH // 2):
                turn(("kT", hp), lambda i, t: q96[:, t, MQK * (2 * hp + i):MQK * (2 * hp + i) + MQK], 2, MQK)
            for hp in range(MH // 2 - 3, MH // 2):
                emptied(pe, ("kT", hp))
            for i in range(MH + 2):
                if i < MH:
                    u = unitm(i)
                    bk = begin("a", ("S", u))
                    for t in range(TT):
                        m = pe.matmul(bk[:, S * t:S * t + S], qTm[:, i, P * t:P * t + P], kTm[:, i, :],
                                      start=True, stop=True)
                    end(m, ("S", u))
                if 1 <= i <= MH:
                    u = unitm(i - 1)
                    pe.wait_ge(s_prob, u + 1)
                    bk = begin("a", ("T", u))
                    for kt in range(TT):
                        for t in range(TT):
                            m = pe.transpose(bk[:, S * kt + P * t:S * kt + P * t + P],
                                             Pm[u % 2][:, t, P * kt:P * kt + P], ident[:, :])
                    end(m, ("T", u))
                if i >= 2:
                    u = unitm(i - 2)
                    emptied(pe, ("T", u))
                    pt = PTm[u % 2]
                    head_out(u, ("O", u // 2), lambda kt, h=i - 2: Vm[:, kt, 64 * h:64 * h + 64],
                             [(0, pt[:, 0, :], 0), (1, pt[:, 1, :], 0)])
            wo(0)
            mlp(0)

            norm(6, xnd)
            pe.wait_ge(s_hlo, h_done[("nrm", 6)])
            for j in range(4):
                todo = []
                for g in range(NG):
                    for m3 in range(3):
                        w = weights(("D", j, g, m3))
                        token_major(("D", j, g, m3), w, 0, 256, hT_hi, hT_lo, 0, DK)
                        used(("D", j, g, m3))
                        if todo:
                            r, job = todo.pop(0)
                            qk_turn(r, job, qn2[r % 2])
                        if m3 < 2:
                            todo.append((8 + 6 * j + 2 * g + m3, ("D", j, g, m3)))
                for g in range(NG):
                    emptied(pe, ("qkT", 8 + 6 * j + 2 * g))
                    emptied(pe, ("qkT", 8 + 6 * j + 2 * g + 1))
                    emptied(pe, ("D", j, g, 2))
                for i in range(HB + 1):
                    if i < HB:
                        u = unitd(HB * j + i)
                        r0, pr = 64 * (i % 2), i // 2
                        for g in range(NG):
                            bk = begin("a", ("S", u, g))
                            for t in range(TT):
                                m = pe.matmul(bk[:, S * t:S * t + S], qTd[r0:r0 + 64, g, pr, P * t:P * t + P],
                                              kTd[r0:r0 + 64, g, pr, :], start=True, stop=True)
                            end(m, ("S", u, g))
                    if 1 <= i <= HB:
                        u = unitd(HB * j + i - 1)
                        pe.wait_ge(s_prob, u + 1)
                        for g in range(NG):
                            bk = begin("a", ("T", u, g))
                            for kt in range(TT):
                                for t in range(TT):
                                    c0 = S * g + P * kt
                                    m = pe.transpose(bk[:, S * kt + P * t:S * kt + P * t + P],
                                                     Ld[u % 2][:, t, c0:c0 + P], ident[:, :])
                            end(m, ("T", u, g))
                        for g in range(NG):
                            emptied(pe, ("T", u, g))
                        h = i - 1
                        head_out(u, ("O", u // 2), lambda kt, h=h: Vd[:, kt // 2, kt % 2, 64 * h:64 * h + 64],
                                 [(kt, PTd[:, kt // 2, kt % 2, :], 0) for kt in range(2 * NG)], "w")
            wo(1)
            mlp(1)
            assert n["c"] == len(chunks)

        def rows_of(v):
            return v.rearrange("(r c) -> r c", c=P)

        row_loads = []
        for l in range(DEPTH):
            row_loads += [(rowA[c_mix(l):c_mix(l) + 8, :], rows_of(A["norm_mix_g"][l])),
                          (rowA[c_ffn(l):c_ffn(l) + 8, :], rows_of(A["norm_ffn_g"][l])),
                          (rowA[c_psc(l):c_psc(l) + 8, :], rows_of(A["pool_scale"][l])),
                          (rowA[c_mix2(l):c_mix2(l) + 8, :], rows_of(A["norm_mix_2"][l])),
                          (rowA[c_mlp2(l):c_mlp2(l) + 8, :], rows_of(A["norm_mlp_2"][l])),
                          (rowA[c_conv(l, 0):c_conv(l, 0) + 6, :], A["conv_w"][l].rearrange("j (r c) -> (j r) c", c=P)),
                          (rowB[b_ada(l):b_ada(l) + 48, :], rows_of(A["ada_b_2"][l]))]
        row_loads += [(rowA[C_COND:C_COND + 8, :], rows_of(A["c_2"][0])),
                      (rowA[C_QA:C_QA + 3, :], rows_of(A["mla_g_qa_2"][0])),
                      (rowA[C_KVA:C_KVA + 2, :], rows_of(A["mla_g_kva_2"][0])),
                      (rowB[B_MQ:B_MQ + 1, 0:MQK], A["mla_g_q_2"][0:1, :]),
                      (rowB[B_MK:B_MK + 1, 0:MQK], A["mla_g_k_2"][0:1, :])]
        for half in (0, 64):
            row_loads += [(rowB[B_Q1:B_Q1 + 2, half:half + 64], A["q_norm_g"]),
                          (rowB[B_K1:B_K1 + 2, half:half + 64], A["k_norm_g"]),
                          (rowB[B_DQ:B_DQ + 3, half:half + 64], A["dil_g_q_2"][0]),
                          (rowB[B_DK:B_DK + 3, half:half + 64], A["dil_g_k_2"][0])]
        assert len(row_loads) == N_ROWS_DMA

        @block.sync
        def _(sp):
            sp.dma_start(x[:, :, :], A["x"][0].rearrange("(t p) d -> p t d", p=P)).then_inc(s_x, 16)

            def ada_piece(q):
                if q >= AR:
                    sp.wait_ge(s_adaused, q - AR + 1)
                k, cb = divmod(q % NP_ADA, 6)
                sp.dma_start(ada_raw[q % AR][:, :], A["ada_w_2"][q // NP_ADA, P * k:P * k + P, D * cb:D * cb + D])\
                  .then_inc(s_ada[q % AR], 16)

            ada_next = 0
            for c, src in enumerate(chunks):
                name = names[c]
                if c >= RAW:
                    sp.wait_ge(s_lo, c - RAW + 1)
                sp.dma_start(view(raw[c % RAW], c), src).then_inc(s_raw[c % RAW], 16)
                if name[0] == "PX":
                    l = name[1]
                    if l:
                        sp.wait_ge(jobs[("YP", l - 1, 3)][0], jobs[("YP", l - 1, 3)][1])
                    sp.dma_start(poolw[:, :, :], A["pool_w"][l].rearrange("(a b) c d -> (b c) a d", b=2))\
                      .then_inc(s_poolw, 16)
                if name[0] == "DN":
                    l, r = name[1:]
                    if r == 0:
                        sp.wait_ge(s_xn, 2 * (2 * l + 1) + 2)
                    while ada_next < NP_ADA * l + (NP_ADA * (r + 1)) // NF1:
                        ada_piece(ada_next)
                        ada_next += 1
            sp.wait_ge(s_final, 4)
            sp.dma_start(out[0].rearrange("(t p) d -> p t d", p=P), x[:, :, :]).then_inc(s_out, 16)
            sp.wait_ge(s_out, 16)

        @block.gpsimd
        def _(pool):
            steps = [0]

            def link(ins):
                steps[0] += 1
                ins.then_inc(s_pc, 1)
                pool.wait_ge(s_pc, steps[0])

            pool.memset(rowB[:, :], 0.0).then_inc(s_set0, 1)
            pool.memset(ones[:, :], 1.0).then_inc(s_set, 1)
            pool.memset(mhalf[:, :], -0.5).then_inc(s_set, 1)
            pool.wait_ge(s_set, 2)
            e = [0]

            def rsqrt(w):
                i = e[0]
                e[0] += 1
                pool.wait_ge(s_ms, i + 1)
                pool.tensor_tensor(rstd[:, i % 2, 0:w], ms[:, i % 2, 0:w], mhalf[:, 0:w], ALU.pow).then_inc(s_rstd, 1)

            for l in range(DEPTH):
                rsqrt(TT)
                for _ in range(4):
                    rsqrt(TT * 4)
                emptied(pool, ("PX", l))
                for b in (pu, s2, s4):
                    link(pool.memset(b[:, :, 0:PAD], 0.0))
                for b in (s8, s16):
                    link(pool.memset(b[:, 0:PAD], 0.0))
                n = S + PAD
                link(pool.tensor_tensor(s2[:, :, 1:n], pu[:, :, 1:n], pu[:, :, 0:n - 1], ALU.add))
                link(pool.tensor_tensor(s4[:, :, 2:n], s2[:, :, 2:n], s2[:, :, 0:n - 2], ALU.add))
                link(pool.tensor_tensor(s8[:, 4:n], s4[:, 1, 4:n], s4[:, 1, 0:n - 4], ALU.add))
                link(pool.tensor_tensor(s16[:, 8:n], s8[:, 8:n], s8[:, 0:n - 8], ALU.add))
                for dst, src, i, p0 in ((pd, s2[:, 0, :], 0, 0), (pd, s4[:, 0, :], 0, 64),
                                        (pd, s8[:, :], 1, 0), (pd, s16[:, :], 1, 64)):
                    link(pool.tensor_tensor(dst[p0:p0 + 64, i, :], src[p0:p0 + 64, PAD:], invcount[p0:p0 + 64, i, :], ALU.mult))
                pool.tensor_tensor(pd[:, :, :], pd[:, :, :], pu[:, :, PAD:], ALU.subtract).then_inc(s_pd, 1)
                rsqrt(TT)
                pool.wait_ge(s_csil, 1)
                if l:
                    full(pool, ("mod", l - 1))
                for q in range(NP_ADA):
                    qa = NP_ADA * l + q
                    k, cb = divmod(q, 6)
                    pool.wait_ge(s_ada[qa % AR], 16 * (qa // AR + 1))
                    acc = ada_acc[:, D * cb:D * cb + D]
                    w = ada_raw[qa % AR]
                    if k == 0:
                        pool.tensor_scalar(acc, w[:, :], csil[:, k:k + 1], None, ALU.mult).then_inc(s_adaused, 1)
                        continue
                    t = ada_tmp[q % 2]
                    pool.tensor_scalar(t[:, :], w[:, :], csil[:, k:k + 1], None, ALU.mult).then_inc(s_adaused, 1)
                    pool.wait_ge(s_adaused, qa + 1)
                    ins = pool.tensor_tensor(acc, acc, t[:, :], ALU.add)
                    if q < NP_ADA - 1:
                        link(ins)
                    else:
                        ins.then_inc(s_adasum, 1)
            rsqrt(TT)
            rsqrt(4)
            rsqrt(32)
            rsqrt(32)
            rsqrt(TT)
            rsqrt(TT)
            for _ in range(24):
                rsqrt(TT * 4)
            rsqrt(TT)

        @block.scalar
        def _(act):
            steps, split_next = [0], [0]

            def link(ins):
                steps[0] += 1
                ins.then_inc(s_ac, 1)
                act.wait_ge(s_ac, steps[0])

            def split_ahead(name, ahead=2):
                while split_next[0] <= min(chunk_at[name] + ahead, len(chunks) - 1):
                    c = split_next[0]
                    split_next[0] += 1
                    act.wait_ge(s_raw[c % RAW], 16 * (c // RAW + 1))
                    if c >= SPL:
                        act.wait_ge(*chunk_done[c - SPL])
                    act.activation(view(whi[c % SPL], c), view(raw[c % RAW], c), ACT.Copy).then_inc(s_hi, 1)

            act.dma_start(ident[:, :], A["ident"]).then_inc(s_const, 16)
            act.dma_start(causal[:, :], A["causal"]).then_inc(s_const, 16)
            act.dma_start(invcount[:, :, :], A["invcount"].rearrange("p (a s) -> p a s", a=2)).then_inc(s_const, 16)
            act.dma_start(fb[:, :], A["forget_b"].rearrange("l h -> h l"), allow_slow_non_contiguous=True).then_inc(s_const, 16)
            act.dma_start(pos_t[:, :], A["positions_2"][0].rearrange("(t p) -> p t", p=P), allow_slow_non_contiguous=True).then_inc(s_const, 16)
            act.dma_start(freq[:, :], A["freq"]).then_inc(s_freq, 16)
            act.wait_ge(s_set0, 1)
            for dst, src in row_loads:
                act.dma_start(dst, src).then_inc(s_rows, 16)
            full(act, "colA")
            act.activation(colA[:, :], bank[jobs["colA"][2]][:, 0:NA_ROWS], ACT.Copy).then_inc(drain_sem("colA"), 1)
            full(act, "colB")
            act.activation(colB[:, :], bank[jobs["colB"][2]][:, 0:NB_ROWS], ACT.Copy).then_inc(drain_sem("colB"), 1)
            emptied(act, "colB")
            act.activation(csil[:, :], colA[:, C_COND:C_COND + 8], ACT.Silu).then_inc(s_csil, 1)
            act.wait_ge(s_ropein, 1)
            act.activation(cosn[:, :, :], ang[:, 4, :].rearrange("p (t f) -> p t f", t=TT), ACT.Sin).then_inc(s_rope, 1)
            act.activation(sinn[:, :, :], ang[:, 3, :].rearrange("p (t f) -> p t f", t=TT), ACT.Sin).then_inc(s_rope, 1)
            act.wait_ge(s_rope, 2)

            def norm_sums(e, sq):
                if e == 0:
                    act.wait_ge(s_x, 16)
                elif e <= 4:
                    emptied(act, ("WO", e // 2, 3) if e % 2 else ("DN", e // 2 - 1, "sum", 3))
                else:
                    act.wait_ge(s_x2, e - 4)
                for t in range(TT):
                    if e or t:
                        act.wait_ge(s_ss, 2 * e + t)
                    act.activation(sq[:, :], x[:, t, :], ACT.Square, accum_out=ss[:, 0, t:t + 1]).then_inc(s_ss, 1)

            cnt = {"h": 0, "at": 0, "hid": 0, "hs": 0}

            def h_high(n, src, dst, width=2, scale=1.0):
                act.activation(dst, src, ACT.Copy, scale=scale).then_inc(s_hhi, 1)
                cnt["h"] += 1

            def norm_high(e, what="nrm", pairs=DK // 2):
                for kp in range(pairs):
                    nm = (what, e, kp) if what == "nrm" else (what, kp)
                    emptied(act, nm)
                    w = 2 if not (what == "latT" and kp == 2) else 1
                    h_high(0, h32[kp % 2][:, 0:w, :], hT_hi[:, 2 * kp:2 * kp + w, :])

            def head_squares(job, r, buf, bufs):
                bk = full(act, job)
                if r >= 2:
                    act.wait_ge(s_hn, r - 1)
                act.activation(buf[:, :], bk[:, :], ACT.Square).then_inc(s_sq, 1)

            def exps(u, src, dst, segs, scale, wait_logits, drain=None):
                act.wait_ge(s_nmax, u + 1)
                if u >= 2:
                    act.wait_ge(s_prob, u - 1)
                    full(act, ("T", u - 2))
                for t, (a, b) in enumerate(segs):
                    ins = act.activation(dst(a, b), src(a, b), ACT.Exp, bias=nmax[:, u % 2, t:t + 1], scale=scale,
                                         accum_out=zsum[:, u % 2, t:t + 1])
                    ins.then_inc(s_exp, 1)

            def at_high(pair, dst):
                emptied(act, ("O", pair))
                act.activation(dst, h32[pair % 2][:, 0, :], ACT.Copy).then_inc(s_athi, 1)

            for l in range(DEPTH):
                split_ahead(("F", l), 1 if l == 0 else 2)
                norm_sums(2 * l, sq1)
                norm_high(2 * l)
                split_ahead(("F", l))
                act.wait_ge(s_z, l + 1)
                link(act.activation(tf[:, :], zf[:, :], ACT.Abs))
                link(act.activation(tf[:, :], tf[:, :], ACT.Exp, scale=-1.0))
                act.activation(tf[:, :], tf[:, :], ACT.Ln, bias=1.0).then_inc(s_zt, 1)
                order = [("Q", 0), ("Q", 1), ("K", 0), ("K", 1)]

                def qk_out(i):
                    nm, c = order[i]
                    r = 4 * l + i
                    dst, col = (qT1, gq8[:, l:l + 1]) if nm == "Q" else (kT1, colB[:, B_K1 + l:B_K1 + l + 1])
                    bk = full(act, ("qkT", r))
                    act.activation(dst[:, 2 * c:2 * c + 2, :], bk[:, :].rearrange("p (a s) -> p a s", a=2), ACT.Copy,
                                   scale=col).then_inc(drain_sem(("qkT", r)), 1)

                for i, (nm, c) in enumerate(order):
                    split_ahead((nm, l, c))
                    head_squares((nm, l, c), 4 * l + i, sqh[i % 2], sqh)
                    if i:
                        qk_out(i - 1)
                for c in range(2):
                    split_ahead(("V", l, c))
                    bk = full(act, ("V", l, c))
                    act.activation(V1[:, :, 256 * c:256 * c + 256], bk[:, :].rearrange("p (t n) -> p t n", t=TT), ACT.Copy)\
                       .then_inc(drain_sem(("V", l, c)), 1)
                    if c == 0:
                        qk_out(3)
                for nm in ("PX", "CX", "CC", "CB"):
                    split_ahead((nm, l))
                    if nm == "CC":
                        continue
                    dst = {"PX": pu[:, :, PAD:], "CX": cxs[:, :, :], "CB": cbs[:, :, :]}[nm]
                    bk = full(act, (nm, l))
                    act.activation(dst, bk[:, :].rearrange("p (a s) -> p a s", a=2), ACT.Copy)\
                       .then_inc(drain_sem((nm, l)), 1)
                g = 0

                def gate(c):
                    split_ahead(("G", l, c))
                    bk = full(act, ("G", l, c))
                    act.activation(gates[:, 2 * c:2 * c + 2, :], bk[:, :].rearrange("p (a s) -> p a s", a=2), ACT.Tanh,
                                   scale=0.5).then_inc(drain_sem(("G", l, c)), 1)

                for i in range(H1 + 2):
                    if i < H1:
                        u = unit1(l, i)
                        exps(u, lambda a, b: L1[u % 2][:, a:b], lambda a, b: P1[u % 2][:, a:b], ((0, P), (P, 3 * P)), 1.0, None)
                    if g < 12:
                        gate(g)
                        g += 1
                    if 1 <= i <= H1:
                        u = unit1(l, i - 1)
                        bk = full(act, ("T", u))
                        act.activation(PT1[u % 2][:, :], bk[:, 0:3 * P], ACT.Copy).then_inc(drain_sem(("T", u)), 1)
                    if g < 12 and i % 4 == 0:
                        gate(g)
                        g += 1
                    if i >= 2 and i % 2:
                        pair = unit1(l, i - 2) // 2
                        at_high(pair, aT_hi[:, pair % 4, :])
                while g < 12:
                    gate(g)
                    g += 1
                act.wait_ge(s_cv, l + 1)
                act.activation(aT_hi[:, 4:6, :], cvb[:, :, :], ACT.Copy).then_inc(s_cvhi, 1)
                split_ahead(("CO", l))
                split_ahead(("AO", l, 0))
                split_ahead(("AO", l, 1))
                for kp in range(4):
                    act.wait_ge(s_mg, 4 * l + kp + 1)
                    h_high(0, mg[:, 2 * kp:2 * kp + 2, :], hT_hi[:, 2 * kp:2 * kp + 2, :], 2, 0.5)
                for c in range(4):
                    split_ahead(("WO", l, c))
                norm_sums(2 * l + 1, sqf)
                norm_high(2 * l + 1)
                act.wait_ge(s_xn, 2 * (2 * l + 1) + 2)
                for dst, src in ((posb[:, :], A["positions_2"][0:1, :].broadcast_to([96, S])), (thr[:, :], A["thr"]),
                                 (stepmat[:, :], A["stepmat"]), (relb[:, :], A["rel_bias_2"]),
                                 (dmask[:, :, :], A["dilmask"][l].rearrange("p (g s) -> p g s", g=NG))):
                    act.dma_start(dst, src).then_inc(s_bin, 16)

                def store_biases(units):
                    for u in units:
                        if u >= 0 and u % 4 == 3:
                            emptied(act, ("B", l, u))
                            k0 = 32 * (u // 4)
                            for g in range(NG):
                                act.dma_start(bias_dram[l, :, :, S * g + k0:S * g + k0 + 32].rearrange("h p k -> p h k"),
                                              stage[:, DH * g:DH * g + DH, :]).then_inc(s_bout, 16)

                for c in range(NF1 + 1):
                    if c < NF1:
                        split_ahead(("GT", l, c))
                        bk = full(act, ("GT", l, c))
                        if c >= 2:
                            emptied(act, ("UP", l, c - 2))
                        act.activation(sg[c % 2][:, :, :], bk[:, :].rearrange("p (a s) -> p a s", a=2), ACT.Silu)\
                           .then_inc(drain_sem(("GT", l, c)), 1)
                        split_ahead(("UP", l, c))
                        store_biases(range(3 * c - 1, min(3 * c + 2, NU - 1)))
                        emptied(act, ("UP", l, c))
                        if c >= 3:
                            act.wait_ge(*chunk_done[chunk_at[("DN", l, c - 3)]])
                        act.activation(aT_hi[:, 2 * (c % 3):2 * (c % 3) + 2, :], h32[c % 2][:, :, :], ACT.Copy)\
                           .then_inc(s_hidhi, 1)
                    if c:
                        split_ahead(("DN", l, c - 1))
                store_biases([NU - 1])
                act.wait_ge(s_bout, 16 * NG * NU // 4 * (l + 1))

            def gate_rows(e, dst):
                for half in range(2):
                    bk = full(act, ("gb", e, half))
                    act.activation(dst[:, 512 * half:512 * half + 512], bk[:, :], ACT.Copy)\
                       .then_inc(drain_sem(("gb", e, half)), 1)

            def wo(i):
                for c in range(4):
                    split_ahead(("MO", i, c))

            def mlp(i):
                norm_sums(5 + 2 * i, sqp)
                norm_high(5 + 2 * i)
                gate_rows(2 * i + 1, gbc2)
                for c in range(NF2 + 1):
                    if c < NF2:
                        split_ahead(("M1", i, c))
                        bk = full(act, ("M1", i, c))
                        if c >= 2:
                            act.wait_ge(s_hid32, NF2 * i + c - 1)
                        act.activation(rl[c % 2][:, :, :], bk[:, :].rearrange("p (a s) -> p a s", a=2), ACT.Relu)\
                           .then_inc(drain_sem(("M1", i, c)), 1)
                        act.wait_ge(s_hid32, NF2 * i + c + 1)
                        if c >= 3:
                            act.wait_ge(*chunk_done[chunk_at[("M2", i, c - 3)]])
                        act.activation(aT_hi[:, 2 * (c % 3):2 * (c % 3) + 2, :], h32[c % 2][:, :, :], ACT.Copy)\
                           .then_inc(s_hidhi, 1)
                    if c:
                        split_ahead(("M2", i, c - 1))

            norm_sums(4, sqm)
            norm_high(4)
            for c in range(3):
                split_ahead(("LI", c))
                w = min(256, 672 - 256 * c)
                bk = full(act, ("LI", c))
                act.activation(lat[:, :, 256 * c:256 * c + w], bk[:, :].rearrange("p (t n) -> p t n", t=TT)[:, :, 0:w],
                               ACT.Copy).then_inc(drain_sem(("LI", c)), 1)
            emptied(act, ("LI", 0))
            emptied(act, ("LI", 1))
            for t in range(TT):
                for n, (a, b) in enumerate(((0, QL), (QL, QL + KVL))):
                    ins = act.activation(sq96[:, a:b], lat[:, t, a:b], ACT.Square,
                                         accum_out=ss[:, 0, 2 * t + n:2 * t + n + 1])
                    if (t, n) == (1, 1):
                        ins.then_inc(s_latss, 1)
                    else:
                        link(ins)
            norm_high(0, "latT", 3)
            for c in range(4):
                split_ahead(("QB", c))
                for t in range(TT):
                    bk = full(act, ("QB", c, t))
                    act.activation(q96[:, t, 384 * c:384 * c + 384], bk[:, 0:384], ACT.Copy)\
                       .then_inc(drain_sem(("QB", c, t)), 1)

            def squares96(n):
                act.wait_ge(s_roped, n + 1)
                for t in range(TT):
                    if n or t:
                        act.wait_ge(s_sum96, 2 * n + t)
                    act.activation(sq96[:, :], q96[:, t, :], ACT.Square).then_inc(s_sq96, 1)

            def turned96(what, dst, col):
                for hp in range(MH // 2):
                    bk = full(act, (what, hp))
                    act.activation(dst[:, 2 * hp:2 * hp + 2, :], bk[0:MQK, :].rearrange("p (a s) -> p a s", a=2),
                                   ACT.Copy, scale=col).then_inc(drain_sem((what, hp)), 1)

            squares96(0)
            turned96("qT", qTm, gq8[0:MQK, 5:6])
            for c in range(2):
                split_ahead(("KV", c), 2)
                for t in range(TT):
                    for half in range(2):
                        nm = ("KV", c, t, half)
                        bk = full(act, nm)
                        full(act, ("qT", MH // 2 - 1))
                        v = bk[:, :].rearrange("p (h n) -> p h n", h=4)
                        h0 = 8 * c + 4 * half
                        act.activation(q96[:, t, :].rearrange("p (h n) -> p h n", h=MH)[:, h0:h0 + 4, 0:MNOPE],
                                       v[:, :, 0:MNOPE], ACT.Copy)
                        act.activation(Vm[:, t, 64 * h0:64 * h0 + 256].rearrange("p (h n) -> p h n", h=4),
                                       v[:, :, MNOPE:P], ACT.Copy).then_inc(drain_sem(nm), 1)
            squares96(1)
            turned96("kT", kTm, colB[0:MQK, B_MK:B_MK + 1])
            for i in range(MH + 2):
                if i < MH:
                    u = unitm(i)
                    bk = full(act, ("S", u))
                    act.wait_ge(s_nmax, u + 1)
                    act.wait_ge(s_prob, u - 1)
                    if i >= 2:
                        full(act, ("T", u - 2))
                    for t in range(TT):
                        act.activation(Pm[u % 2][:, t, :], bk[:, S * t:S * t + S], ACT.Exp, bias=nmax[:, u % 2, t:t + 1],
                                       accum_out=zsum[:, u % 2, t:t + 1]).then_inc(s_exp, 1)
                if 1 <= i <= MH:
                    u = unitm(i - 1)
                    bk = full(act, ("T", u))
                    act.activation(PTm[u % 2][:, :, :], bk[:, :].rearrange("p (a s) -> p a s", a=2), ACT.Copy)\
                       .then_inc(drain_sem(("T", u)), 1)
                if i >= 2 and i % 2:
                    pair = unitm(i - 2) // 2
                    at_high(pair, aT_hi[:, pair % 8, :])
            gate_rows(0, gbc0)
            wo(0)
            mlp(0)

            norm_sums(6, sqd)
            norm_high(6)

            def bias_load(n):
                if n >= 2:
                    act.wait_ge(s_nmax, unitd(n - 2) + 1)
                act.dma_start(biasb[n % 2][:, :, :], bias_dram[:, n, :, :].rearrange("t p k -> p t k"))\
                   .then_inc(s_bld[n % 2], 16)

            for j in range(4):
                todo = []

                def qk_out(r, g, m3):
                    bk = full(act, ("qkT", r))
                    dst, col = (qTd, gq8[:, 2 + g:3 + g]) if m3 == 0 else (kTd, colB[:, B_DK + g:B_DK + g + 1])
                    act.activation(dst[:, g, :, :], bk[:, :].rearrange("p (a s) -> p a s", a=2), ACT.Copy,
                                   scale=col).then_inc(drain_sem(("qkT", r)), 1)

                for b in range(2):
                    bias_load(HB * j + b)
                for g in range(NG):
                    for m3 in range(3):
                        nm = ("D", j, g, m3)
                        split_ahead(nm)
                        if m3 < 2:
                            r = 8 + 6 * j + 2 * g + m3
                            head_squares(nm, r, sqh2[r % 2], sqh2)
                        else:
                            bk = full(act, nm)
                            act.activation(Vd[:, g, :, :], bk[:, :].rearrange("p (t n) -> p t n", t=TT), ACT.Copy)\
                               .then_inc(drain_sem(nm), 1)
                        if todo:
                            qk_out(*todo.pop(0))
                        if m3 < 2:
                            todo.append((r, g, m3))
                for i in range(HB + 1):
                    if i < HB:
                        u = unitd(HB * j + i)
                        act.wait_ge(s_nmax, u + 1)
                        act.wait_ge(s_prob, u - 1)
                        for t in range(TT):
                            act.activation(Ld[u % 2][:, t, :], Ld[u % 2][:, t, :], ACT.Exp, bias=nmax[:, u % 2, t:t + 1],
                                           accum_out=zsum[:, u % 2, t:t + 1]).then_inc(s_exp, 1)
                    if 1 <= i <= HB:
                        u = unitd(HB * j + i - 1)
                        for g in range(NG):
                            bk = full(act, ("T", u, g))
                            act.activation(PTd[:, g, :, :], bk[:, :].rearrange("p (a s) -> p a s", a=2), ACT.Copy)\
                               .then_inc(drain_sem(("T", u, g)), 1)
                    if i >= 1 and i % 2 == 0:
                        pair = unitd(HB * j + i - 1) // 2
                        at_high(pair, aT_hi[:, pair % 8, :])
                    if i + 2 < HB:
                        bias_load(HB * j + i + 2)
            gate_rows(2, gbc)
            wo(1)
            mlp(1)

        @block.vector
        def _(dve):
            steps, split_next, e = [0], [0], [0]

            def link(ins):
                steps[0] += 1
                ins.then_inc(s_dc, 1)
                dve.wait_ge(s_dc, steps[0])

            def split_ahead(name, ahead=2):
                while split_next[0] <= min(chunk_at[name] + ahead, len(chunks) - 1):
                    c = split_next[0]
                    split_next[0] += 1
                    dve.wait_ge(s_hi, c + 1)
                    dve.tensor_tensor(view(wlo[c % SPL], c), view(raw[c % RAW], c), view(whi[c % SPL], c).bitcast(F32),
                                      ALU.subtract).then_inc(s_lo, 1)

            def rms(src, width, n):
                i = e[0]
                e[0] += 1
                dve.tensor_scalar(ms[:, i % 2, 0:width], src, 1.0 / n, EPS, ALU.mult, ALU.add).then_inc(s_ms, 1)
                dve.wait_ge(s_rstd, i + 1)
                return rstd[:, i % 2, :]

            def norm(ev, xn):
                dve.wait_ge(s_ss, 2 * ev + 2)
                r = rms(ss[:, 0, 0:TT], TT, D)
                for t in range(TT):
                    dve.tensor_scalar(xn[:, t, :], x[:, t, :], r[:, t:t + 1], None, ALU.mult).then_inc(s_xn, 1)

            def bias_out(l, u):
                nm = ("B", l, u)
                bk = full(dve, nm)
                if u % 4 == 0 and (l or u):
                    dve.wait_ge(s_bout, 16 * NG * (NU * l + u) // 4)
                k0 = 8 * (u % 4)
                dve.tensor_tensor(stage[:, :, k0:k0 + 8].rearrange("p (g h) k -> p g h k", g=NG),
                                  bk[:, 0:8 * NG * DH].rearrange("p (k g h) -> p g h k", k=8, g=NG),
                                  dmask[:, :, 8 * u:8 * u + 8].unsqueeze(2).broadcast_to([P, NG, DH, 8]), ALU.add)\
                   .then_inc(drain_sem(nm), 1)

            hc = [0]

            def h_low(src, dst_lo, dst_hi, scale=None):
                hc[0] += 1
                dve.wait_ge(s_hhi, hc[0])
                if scale is None:
                    dve.tensor_tensor(dst_lo, src, dst_hi.bitcast(F32), ALU.subtract).then_inc(s_hlo, 1)
                else:
                    dve.scalar_tensor_tensor(out=dst_lo, in0=src, scalar=scale, in1=dst_hi.bitcast(F32), op0=ALU.mult,
                                             op1=ALU.subtract).then_inc(s_hlo, 1)

            def norm_out(names, gain, shift, tiles):
                for kp, nm in enumerate(names):
                    bk = full(dve, nm)
                    w = min(2, tiles - 2 * kp)
                    for i in range(w):
                        k = 2 * kp + i
                        b = bk[:, S * i:S * i + S]
                        if shift is None:
                            ins = dve.tensor_scalar(h32[kp % 2][:, i, :], b, gain(k), None, ALU.mult)
                        else:
                            ins = dve.tensor_scalar(h32[kp % 2][:, i, :], b, gain(k), shift(k), ALU.mult, ALU.add)
                        if i < w - 1:
                            link(ins)
                    ins.then_inc(drain_sem(nm), 1)
                    h_low(h32[kp % 2][:, 0:w, :], hT_lo[:, 2 * kp:2 * kp + w, :], hT_hi[:, 2 * kp:2 * kp + w, :])

            def head_norm(job, r, sqbuf, buf):
                dve.wait_ge(s_sq, r + 1)
                dve.tensor_reduce(ss[:, 1, 0:8], sqbuf[:, :].rearrange("p (a n) -> p a n", n=HD), AX, ALU.add)\
                   .then_inc(s_hn, 1)
                dve.wait_ge(s_hn, r + 1)
                rr = rms(ss[:, 1, 0:8], 8, HD)
                bk = full(dve, job)
                if r >= 2:
                    full(dve, ("qkT", r - 2))
                dve.tensor_tensor(buf[:, :, :].rearrange("p t (h n) -> p (t h) n", n=HD),
                                  bk[:, :].rearrange("p (a n) -> p a n", n=HD),
                                  rr[:, 0:8].unsqueeze(2).broadcast_to([P, 8, HD]), ALU.mult)\
                   .then_inc(drain_sem(job), 1)

            def probs(u, p, segs):
                dve.wait_ge(s_exp, 2 * u + 2)
                link(dve.reciprocal(rz[:, u % 2, :], zsum[:, u % 2, :]))
                for t, (a, b) in enumerate(segs):
                    ins = dve.tensor_scalar(p(t, a, b), p(t, a, b), rz[:, u % 2, t:t + 1], None, ALU.mult)
                    if t == 0:
                        link(ins)
                ins.then_inc(s_prob, 1)

            def at_low(pair, k):
                bk = full(dve, ("O", pair))
                dve.tensor_copy(h32[pair % 2][:, 0, :], bk[:, 0:S]).then_inc(drain_sem(("O", pair)), 1)
                emptied(dve, ("O", pair))
                dve.wait_ge(s_athi, pair + 1)
                dve.tensor_tensor(aT_lo[:, k, :], h32[pair % 2][:, 0, :], aT_hi[:, k, :].bitcast(F32), ALU.subtract)\
                   .then_inc(s_atlo, 1)

            emptied(dve, "colA")
            emptied(dve, "colB")
            dve.wait_ge(s_freq, 16)
            link(dve.tensor_scalar(gq8[:, 0:2], colB[:, B_Q1:B_Q1 + 2], HD ** -0.5, None, ALU.mult))
            link(dve.tensor_scalar(gq8[:, 2:5], colB[:, B_DQ:B_DQ + 3], HD ** -0.5, None, ALU.mult))
            link(dve.tensor_scalar(gq8[:, 5:6], colB[:, B_MQ:B_MQ + 1], MQK ** -0.5, None, ALU.mult))
            link(dve.tensor_copy(posf[:, :], pos_t[:, :]))
            link(dve.tensor_tensor(ang[:, 0, :].rearrange("p (t f) -> p t f", t=TT),
                                   posf[:, :].unsqueeze(2).broadcast_to([P, TT, 16]),
                                   freq[:, :].unsqueeze(1).broadcast_to([P, TT, 16]), ALU.mult))
            two_pi = 6.283185307179586
            c1 = 6.28125
            c2 = 0.0019350051879882812
            c3 = two_pi - c1 - c2
            link(dve.tensor_scalar(ang[:, 1, :], ang[:, 0, :], 1.0 / two_pi, None, ALU.mult))
            link(dve.tensor_copy(angi[:, :], ang[:, 1, :]))
            link(dve.tensor_copy(ang[:, 1, :], angi[:, :]))
            link(dve.scalar_tensor_tensor(out=ang[:, 2, :], in0=ang[:, 1, :], scalar=-c1, in1=ang[:, 0, :], op0=ALU.mult, op1=ALU.add))
            link(dve.scalar_tensor_tensor(out=ang[:, 0, :], in0=ang[:, 1, :], scalar=-c2, in1=ang[:, 2, :], op0=ALU.mult, op1=ALU.add))
            link(dve.scalar_tensor_tensor(out=ang[:, 2, :], in0=ang[:, 1, :], scalar=-c3, in1=ang[:, 0, :], op0=ALU.mult, op1=ALU.add))

            def wrap(dst, src):
                link(dve.tensor_scalar(ang[:, 5, :], src, two_pi / 2, -two_pi, ALU.is_gt, ALU.mult))
                link(dve.tensor_tensor(ang[:, 5, :], ang[:, 5, :], src, ALU.add))
                link(dve.tensor_scalar(dst, ang[:, 5, :], -two_pi / 2, two_pi, ALU.is_lt, ALU.mult))
                link(dve.tensor_tensor(dst, dst, ang[:, 5, :], ALU.add))
                link(dve.tensor_scalar(dst, dst, 3.1415925, -3.1415925, ALU.min, ALU.max))

            wrap(ang[:, 3, :], ang[:, 2, :])
            link(dve.tensor_scalar(ang[:, 0, :], ang[:, 2, :], two_pi / 4, None, ALU.add))
            wrap(ang[:, 4, :], ang[:, 0, :])
            dve.tensor_copy(ang[:, 5, 0:1], ang[:, 4, 0:1]).then_inc(s_ropein, 1)
            dve.wait_ge(s_rope, 2)

            for l in range(DEPTH):
                split_ahead(("F", l), 1 if l == 0 else 2)
                norm(2 * l, xn1)
                norm_out([("nrm", 2 * l, kp) for kp in range(4)], lambda k: colA[:, c_mix(l) + k:c_mix(l) + k + 1], None, DK)
                split_ahead(("F", l))
                bk = full(dve, ("F", l))
                dve.tensor_scalar(zf[:, :], bk[0:H1, 0:S], fb[:, l:l + 1], None, ALU.add).then_inc(drain_sem(("F", l)), 1)
                emptied(dve, ("F", l))
                link(dve.memset(zero8[:, :], 0.0))
                dve.tensor_scalar(mf[:, :], zf[:, :], 0.0, None, ALU.min).then_inc(s_z, 1)
                dve.wait_ge(s_zt, l + 1)
                link(dve.tensor_tensor(mf[:, :], tf[:, :], mf[:, :], ALU.subtract))
                dve.tensor_tensor_scan(ncum[:, :], mf[:, :], zero8[:, :], 0.0, ALU.add, ALU.add).then_inc(s_cum, 1)
                for i, (nm, c) in enumerate([("Q", 0), ("Q", 1), ("K", 0), ("K", 1)]):
                    split_ahead((nm, l, c))
                    head_norm((nm, l, c), 4 * l + i, sqh[i % 2], qn[i % 2])
                for c in range(2):
                    split_ahead(("V", l, c))
                split_ahead(("PX", l))
                split_ahead(("CX", l))
                split_ahead(("CC", l))
                bk = full(dve, ("CC", l))
                emptied(dve, ("CX", l))
                link(dve.memset(zc[:, :, 0:2], 0.0))
                dve.tensor_tensor(zc[:, :, 2:], bk[:, :].rearrange("p (a s) -> p a s", a=2), cxs[:, :, :], ALU.mult)\
                   .then_inc(drain_sem(("CC", l)), 1)
                split_ahead(("CB", l))
                emptied(dve, ("CC", l))
                for j in range(3):
                    for i in range(2):
                        col = colA[:, c_conv(l, j) + i:c_conv(l, j) + i + 1]
                        if j == 0:
                            link(dve.tensor_scalar(cva[:, i, :], zc[:, i, 0:S], col, None, ALU.mult))
                        else:
                            link(dve.scalar_tensor_tensor(out=(cvb, cva)[j - 1][:, i, :], in0=zc[:, i, j:j + S], scalar=col,
                                                          in1=(cva, cvb)[j - 1][:, i, :], op0=ALU.mult, op1=ALU.add))
                emptied(dve, ("CB", l))
                dve.tensor_tensor(cvb[:, :, :], cva[:, :, :], cbs[:, :, :], ALU.mult).then_inc(s_cv, 1)
                segs = ((0, P), (P, 3 * P))
                g = 0
                for i in range(H1 + 2):
                    if i < H1:
                        u = unit1(l, i)
                        bk = full(dve, ("S", u))
                        if i >= 2:
                            dve.wait_ge(s_exp, 2 * (u - 2) + 2)
                        for t, (a, b) in enumerate(segs):
                            ins = dve.tensor_tensor_reduce(L1[u % 2][:, a:b], bk[:, a:b], causal[:, a:b], 1.0, NEG,
                                                           ALU.add, ALU.max, mx[:, u % 2, t:t + 1])
                            if t == 0:
                                link(ins)
                        ins.then_inc(drain_sem(("S", u)), 1)
                        emptied(dve, ("S", u))
                        dve.tensor_scalar(nmax[:, u % 2, :], mx[:, u % 2, :], -1.0, None, ALU.mult).then_inc(s_nmax, 1)
                    if g < 12:
                        split_ahead(("G", l, g))
                        g += 1
                    if i < H1:
                        if i >= 2:
                            full(dve, ("T", u - 2))
                        probs(u, lambda t, a, b: P1[u % 2][:, a:b], segs)
                    if g < 12 and i % 4 == 0:
                        split_ahead(("G", l, g))
                        g += 1
                    if i >= 2 and i % 2:
                        pair = unit1(l, i - 2) // 2
                        at_low(pair, pair % 4)
                while g < 12:
                    split_ahead(("G", l, g))
                    g += 1
                dve.wait_ge(s_cvhi, l + 1)
                dve.tensor_tensor(aT_lo[:, 4:6, :], cvb[:, :, :], aT_hi[:, 4:6, :].bitcast(F32), ALU.subtract).then_inc(s_cvlo, 1)
                emptied(dve, ("G", l, 11))
                emptied(dve, ("G", l, 10))
                emptied(dve, ("G", l, 9))
                for gi in range(4):
                    bk = full(dve, ("YP", l, gi))
                    for i in range(2):
                        k = 2 * gi + i
                        ins = dve.tensor_scalar(mt[gi % 2][:, i, :], bk[:, S * i:S * i + S],
                                                colA[:, c_psc(l) + k:c_psc(l) + k + 1], None, ALU.mult)
                        if i == 0:
                            link(ins)
                    ins.then_inc(drain_sem(("YP", l, gi)), 1)
                    emptied(dve, ("YP", l, gi))
                    m2 = mg[:, 2 * gi:2 * gi + 2, :]
                    link(dve.scalar_tensor_tensor(out=m2, in0=m2, scalar=1.0, in1=mt[gi % 2][:, :, :], op0=ALU.add, op1=ALU.mult))
                split_ahead(("CO", l))
                for br, what in ((1, "YC"), (0, "YA")):
                    for jp in range(4):
                        nm = (what, l, jp)
                        if what == "YA" and jp % 2 == 0:
                            split_ahead(("AO", l, jp // 2))
                        bk = full(dve, nm)
                        gt = gates[:, DK * br + 2 * jp:DK * br + 2 * jp + 2, :]
                        dve.scalar_tensor_tensor(out=mt[jp % 2][:, :, :], in0=gt, scalar=1.0,
                                                 in1=bk[:, :].rearrange("p (a s) -> p a s", a=2), op0=ALU.add,
                                                 op1=ALU.mult).then_inc(drain_sem(nm), 1)
                        emptied(dve, nm)
                        m2 = mg[:, 2 * jp:2 * jp + 2, :]
                        ins = dve.tensor_tensor(m2, m2, mt[jp % 2][:, :, :], ALU.add)
                        if br:
                            link(ins)
                        else:
                            ins.then_inc(s_mg, 1)
                            h_low(m2, hT_lo[:, 2 * jp:2 * jp + 2, :], hT_hi[:, 2 * jp:2 * jp + 2, :], 0.5)
                for c in range(4):
                    nm = ("WO", l, c)
                    split_ahead(nm)
                    bk = full(dve, nm)
                    xs = x[:, :, 256 * c:256 * c + 256]
                    dve.tensor_tensor(xs, xs, bk[:, :].rearrange("p (t n) -> p t n", t=TT), ALU.add).then_inc(drain_sem(nm), 1)
                norm(2 * l + 1, xnf)
                norm_out([("nrm", 2 * l + 1, kp) for kp in range(4)], lambda k: colA[:, c_ffn(l) + k:c_ffn(l) + k + 1], None, DK)
                dve.wait_ge(s_bin, BIN * (l + 1))
                link(dve.tensor_single_scalar(ihi[:, :], posb[:, :], 16, ALU.arith_shift_right))
                link(dve.tensor_single_scalar(ilo[:, :], posb[:, :], 65535, ALU.bitwise_and))
                link(dve.tensor_copy(hi16[:, :], ihi[:, :]))
                link(dve.tensor_copy(lo16[:, :], ilo[:, :]))
                link(dve.tensor_scalar(relk[:, :], hi16[:, :], hi16[:, 0:1], 65536.0, ALU.subtract, ALU.mult))
                link(dve.tensor_scalar(relq[:, :], lo16[:, :], lo16[:, 0:1], None, ALU.subtract))
                link(dve.tensor_tensor(relk[:, :], relk[:, :], relq[:, :], ALU.add))
                link(dve.tensor_scalar(relq[:, :], relk[:, :], thr[:, 0:1], None, ALU.add))
                bk = full(dve, ("steps", l))
                dve.tensor_copy(dres[:, 0, :], bk[0:96, 0:NG * DH]).then_inc(drain_sem(("steps", l)), 1)
                emptied(dve, ("steps", l))
                for n in range(3):
                    link(dve.tensor_copy(dpart[:, n, :], dres[:, n, :]))
                    if n < 2:
                        link(dve.tensor_tensor(dres[:, n + 1, :], dres[:, n, :], dpart[:, n, :], ALU.subtract))
                    link(dve.tensor_copy(dsel[32 * n:32 * n + 32, :], dpart[32 * n:32 * n + 32, n, :]))
                for c in range(NF1 + 1):
                    if c < NF1:
                        split_ahead(("GT", l, c))
                        split_ahead(("UP", l, c))
                        for u in range(3 * c, min(3 * c + 3, NU)):
                            gu = NU * l + u
                            if u >= 2:
                                full(dve, ("B", l, u - 2))
                            dve.tensor_tensor(Gst[gu % 2][:, :, :],
                                              relk[:, 8 * u:8 * u + 8].unsqueeze(2).broadcast_to([96, 8, P]),
                                              relq[:, P * l:P * l + P].unsqueeze(1).broadcast_to([96, 8, P]), ALU.is_ge)\
                               .then_inc(s_g, 1)
                            if u > 3 * c:
                                bias_out(l, u - 1)
                        emptied(dve, ("GT", l, c))
                        nm = ("UP", l, c)
                        bk = full(dve, nm)
                        dve.tensor_tensor(h32[c % 2][:, :, :], bk[:, :].rearrange("p (a s) -> p a s", a=2), sg[c % 2][:, :, :],
                                          ALU.mult).then_inc(drain_sem(nm), 1)
                        emptied(dve, nm)
                        dve.wait_ge(s_hidhi, NF1 * l + c + 1)
                        sl = 2 * (c % 3)
                        dve.tensor_tensor(aT_lo[:, sl:sl + 2, :], h32[c % 2][:, :, :], aT_hi[:, sl:sl + 2, :].bitcast(F32),
                                          ALU.subtract).then_inc(s_hidlo, 1)
                        bias_out(l, min(3 * c + 2, NU - 1))
                    if c:
                        split_ahead(("DN", l, c - 1))
                for q in range(4):
                    nm = ("DN", l, "sum", q)
                    t, half = divmod(q, 2)
                    bk = full(dve, nm)
                    xs = x[:, t, 512 * half:512 * half + 512]
                    dve.tensor_tensor(xs, xs, bk[:, :], ALU.add).then_inc(drain_sem(nm), 1)
                dve.wait_ge(s_bout, 16 * NG * NU // 4 * (l + 1))
                bk = full(dve, ("mod", l))
                dve.tensor_tensor(mods[:, l, :], bk[:, 0:48], colB[:, b_ada(l):b_ada(l) + 48], ALU.add)\
                   .then_inc(drain_sem(("mod", l)), 1)
                emptied(dve, ("mod", l))
                link(dve.scalar_tensor_tensor(out=gain2[:, l, 0, :], in0=mods[:, l, 8:16], scalar=1.0,
                                              in1=colA[:, c_mix2(l):c_mix2(l) + 8], op0=ALU.add, op1=ALU.mult))
                dve.scalar_tensor_tensor(out=gain2[:, l, 1, :], in0=mods[:, l, 32:40], scalar=1.0,
                                         in1=colA[:, c_mlp2(l):c_mlp2(l) + 8], op0=ALU.add, op1=ALU.mult).then_inc(s_mods, 1)
                dve.wait_ge(s_mods, l + 1)

            def norm2(ev, i, which, xn):
                norm(ev, xn)
                norm_out([("nrm", ev, kp) for kp in range(4)], lambda k: gain2[:, i, which, k:k + 1],
                         lambda k: mods[:, i, 24 * which + k:24 * which + k + 1], DK)

            def wo(i):
                emptied(dve, ("gb", 2 * i, 1))
                emptied(dve, ("gb", 2 * i, 0))
                for c in range(4):
                    nm = ("MO", i, c)
                    split_ahead(nm)
                    bk = full(dve, nm)
                    y = (gy0, gy1)[i][c % 2]
                    rows = (gbc0, gbc)[i]
                    dve.tensor_tensor(y[:, :, :], bk[:, :].rearrange("p (t n) -> p t n", t=TT),
                                      rows[:, 256 * c:256 * c + 256].unsqueeze(1).broadcast_to([P, TT, 256]), ALU.mult)\
                       .then_inc(drain_sem(nm), 1)
                    emptied(dve, nm)
                    xs = x[:, :, 256 * c:256 * c + 256]
                    link(dve.tensor_tensor(xs, xs, y[:, :, :], ALU.add))
                dve.tensor_copy(mx[:, 0, :], mx[:, 0, :]).then_inc(s_x2, 1)

            def mlp(i):
                norm2(5 + 2 * i, i, 1, xnp)
                for c in range(NF2 + 1):
                    if c < NF2:
                        nm = ("M1", i, c)
                        split_ahead(nm)
                        emptied(dve, nm)
                        dve.tensor_tensor(h32[c % 2][:, :, :], rl[c % 2][:, :, :], rl[c % 2][:, :, :], ALU.mult)\
                           .then_inc(s_hid32, 1)
                        dve.wait_ge(s_hidhi, 2 * NF1 + NF2 * i + c + 1)
                        sl = 2 * (c % 3)
                        dve.tensor_tensor(aT_lo[:, sl:sl + 2, :], h32[c % 2][:, :, :], aT_hi[:, sl:sl + 2, :].bitcast(F32),
                                          ALU.subtract).then_inc(s_hidlo, 1)
                    if c:
                        split_ahead(("M2", i, c - 1))
                emptied(dve, ("gb", 2 * i + 1, 1))
                for q in range(4):
                    nm = ("M2", i, "sum", q)
                    t, half = divmod(q, 2)
                    bk = full(dve, nm)
                    dve.tensor_tensor(gy2[:, :], bk[:, :], gbc2[:, 512 * half:512 * half + 512], ALU.mult)\
                       .then_inc(drain_sem(nm), 1)
                    emptied(dve, nm)
                    xs = x[:, t, 512 * half:512 * half + 512]
                    ins = dve.tensor_tensor(xs, xs, gy2[:, :], ALU.add)
                    if i == DEPTH - 1:
                        ins.then_inc(s_final, 1)
                        dve.wait_ge(s_final, q + 1)
                    else:
                        link(ins)
                dve.tensor_copy(mx[:, 0, :], mx[:, 0, :]).then_inc(s_x2, 1)

            norm2(4, 0, 0, xnm)
            for c in range(3):
                split_ahead(("LI", c))
            dve.wait_ge(s_latss, 1)
            for n, wdt in ((0, QL), (1, KVL)):
                link(dve.tensor_scalar(ss[:, 1, n:n + 3:2], ss[:, 0, n:n + 3:2], 1.0 / wdt, None, ALU.mult))
            r = rms(ss[:, 1, 0:4], 4, 1)
            for t in range(TT):
                for n, (a, b) in enumerate(((0, QL), (QL, QL + KVL))):
                    ins = dve.tensor_scalar(latn[:, t, a:b], lat[:, t, a:b], r[:, 2 * t + n:2 * t + n + 1], None, ALU.mult)
                    if (t, n) != (1, 1):
                        link(ins)
            ins.then_inc(s_latn, 1)
            norm_out([("latT", kp) for kp in range(3)],
                     lambda k: colA[:, C_QA + k:C_QA + k + 1], None, 5)

            def rotate(src, dst, heads):
                cb = cosn[:, :, :].unsqueeze(2).broadcast_to([P, TT, heads, 16])
                sbn = sinn[:, :, :].unsqueeze(2).broadcast_to([P, TT, heads, 16])

                def r4(i):
                    return rt[:, i, 0:TT * heads * 16].rearrange("p (t h f) -> p t h f", t=TT, h=heads)

                a, b = src[:, :, :, 0:16], src[:, :, :, 16:32]
                link(dve.tensor_tensor(r4(0), a, cb, ALU.mult))
                link(dve.tensor_tensor(r4(1), b, sbn, ALU.mult))
                link(dve.tensor_tensor(r4(2), b, cb, ALU.mult))
                link(dve.tensor_tensor(r4(3), a, sbn, ALU.mult))
                link(dve.tensor_tensor(dst[:, :, :, 0:16], r4(0), r4(1), ALU.subtract))
                link(dve.tensor_tensor(dst[:, :, :, 16:32], r4(2), r4(3), ALU.add))

            emptied(dve, ("LI", 2))
            rotate(lat[:, :, QL + KVL:].unsqueeze(2), krope[:, :, :].unsqueeze(2), 1)
            for c in range(4):
                split_ahead(("QB", c))
            q4 = q96[:, :, :].rearrange("p t (h n) -> p t h n", h=MH)
            for t in range(TT):
                emptied(dve, ("QB", 3, t))
                emptied(dve, ("QB", 2, t))

            def norm96(n):
                for t in range(TT):
                    dve.wait_ge(s_sq96, 2 * n + t + 1)
                    dve.tensor_reduce(ss[:, 1, MH * t:MH * t + MH], sq96[:, :].rearrange("p (h n) -> p h n", h=MH), AX,
                                      ALU.add).then_inc(s_sum96, 1)
                dve.wait_ge(s_sum96, 2 * n + 2)
                rr = rms(ss[:, 1, :], 32, MQK)
                q3 = q96[:, :, :].rearrange("p t (h n) -> p (t h) n", h=MH)
                dve.tensor_tensor(q3, q3, rr[:, 0:32].unsqueeze(2).broadcast_to([P, 32, MQK]), ALU.mult).then_inc(s_q96, 1)

            rotate(q4[:, :, :, MNOPE:], q4[:, :, :, MNOPE:], MH)
            dve.tensor_copy(mx[:, 1, :], mx[:, 0, :]).then_inc(s_roped, 1)
            norm96(0)
            for c in range(2):
                split_ahead(("KV", c))
            full(dve, ("qT", MH // 2 - 1))
            link(dve.tensor_copy(q4[:, :, :, MNOPE:], krope[:, :, :].unsqueeze(2).broadcast_to([P, TT, MH, MROPE])))
            for c, t, half in ((1, 0, 1), (1, 1, 0), (1, 1, 1)):
                emptied(dve, ("KV", c, t, half))
            dve.tensor_copy(mx[:, 1, :], mx[:, 0, :]).then_inc(s_roped, 1)
            norm96(1)
            for i in range(MH + 2):
                if i < MH:
                    u = unitm(i)
                    bk = full(dve, ("S", u))
                    dve.tensor_reduce(nmax[:, u % 2, :], bk[:, :].rearrange("p (t k) -> p t k", t=TT), AX, ALU.max, negate=True)\
                       .then_inc(s_nmax, 1)
                    dve.wait_ge(s_exp, 2 * u + 2)
                    dve.reciprocal(rz[:, u % 2, :], zsum[:, u % 2, :]).then_inc(drain_sem(("S", u)), 1)
                    emptied(dve, ("S", u))
                    pm = Pm[u % 2]
                    link(dve.tensor_scalar(pm[:, 0, :], pm[:, 0, :], rz[:, u % 2, 0:1], None, ALU.mult))
                    dve.tensor_scalar(pm[:, 1, :], pm[:, 1, :], rz[:, u % 2, 1:2], None, ALU.mult).then_inc(s_prob, 1)
                if i >= 2 and i % 2:
                    pair = unitm(i - 2) // 2
                    at_low(pair, pair % 8)
            wo(0)
            mlp(0)

            norm2(6, 1, 0, xnd)
            for j in range(4):
                for g in range(NG):
                    for m3 in range(3):
                        split_ahead(("D", j, g, m3))
                        if m3 < 2:
                            r = 8 + 6 * j + 2 * g + m3
                            head_norm(("D", j, g, m3), r, sqh2[r % 2], qn2[r % 2])
                for i in range(HB + 1):
                    if i < HB:
                        u = unitd(HB * j + i)
                        bload = u - unitd(0)
                        dve.wait_ge(s_bld[bload % 2], 16 * (bload // 2 + 1))
                        if bload >= 2:
                            full(dve, ("T", u - 2, NG - 1))
                        for g in range(NG):
                            bk = full(dve, ("S", u, g))
                            dve.tensor_tensor(Ld[u % 2][:, :, S * g:S * g + S], bk[:, :].rearrange("p (t k) -> p t k", t=TT),
                                              biasb[bload % 2][:, :, S * g:S * g + S], ALU.add)\
                               .then_inc(drain_sem(("S", u, g)), 1)
                        for g in range(NG):
                            emptied(dve, ("S", u, g))
                        dve.tensor_reduce(nmax[:, u % 2, :], Ld[u % 2][:, :, :], AX, ALU.max, negate=True).then_inc(s_nmax, 1)
                        probs(u, lambda t, a, b: Ld[u % 2][:, t, :], ((0, 0), (0, 0)))
                    if i >= 1 and i % 2 == 0:
                        pair = unitd(HB * j + i - 1) // 2
                        at_low(pair, pair % 8)
            wo(1)
            mlp(1)


NAMES = ["x", "norm_mix_g", "w_in", "forget_b", "q_norm_g", "k_norm_g", "w_attn_out", "conv_w", "w_conv_out", "pool_w",
         "pool_scale", "w_o", "norm_ffn_g", "w_ffn_in", "w_ffn_out", "c_2", "positions_2", "ada_w_2", "ada_b_2",
         "norm_mix_2", "norm_mlp_2", "mlp_w1_2", "mlp_w2_2", "mla_w_in_2", "mla_g_qa_2", "mla_w_qb_2", "mla_g_kva_2",
         "mla_w_kvb_2", "mla_g_q_2", "mla_g_k_2", "mla_w_o_2", "dil_w_in_2", "dil_g_q_2", "dil_g_k_2", "dil_w_o_2",
         "rel_bias_2"]


def kernel(**inputs):
    import numpy as np
    import concourse.bacc as bacc
    from concourse.bass_utils import run_bass_kernel_spmd

    nc = bacc.Bacc("TRN2", target_bir_lowering=False, num_devices=1)
    arrays, aps = {}, {}
    for name, a in [(n, inputs[n]) for n in NAMES] + list(host_constants().items()):
        a = np.ascontiguousarray(a)
        arrays[f"in_{name}"] = a
        aps[name] = nc.dram_tensor(f"in_{name}", a.shape, mybir.dt.from_np(a.dtype), kind="ExternalInput").ap()
    out = nc.dram_tensor("out_0", (1, S, D), F32, kind="ExternalOutput").ap()
    block_pair(nc, aps, out)
    r = run_bass_kernel_spmd(nc, [arrays], core_ids=[0])
    return r.results[0]["out_0"]
```

```python
from contextlib import ExitStack

import concourse.bass as bass
from concourse import mybir

F32 = mybir.dt.float32
F32R = mybir.dt.float32r
BF16 = mybir.dt.bfloat16
I32 = mybir.dt.int32
ALU = mybir.AluOpType
ACT = mybir.ActivationFunctionType
AX = mybir.AxisListType.X

P = 128
S = 256
TT = S // P
D = 1024
DK = D // P
DEPTH = 2
EPS = 1e-6
H1, HD = 8, 64
DA = H1 * HD
DC = D // 4
FF1 = 2816
NF1 = FF1 // 256
FF2 = 4 * D
NF2 = FF2 // 256
MH, MQK, MNOPE, MROPE = 16, 96, 64, 32
QL, KVL = 384, 256
DH = 16
NG = 3
HB = 4
F_AT = 3 * DA
CX_AT = F_AT + H1
CB_AT, CC_AT, PX_AT, G_AT = CX_AT + DC, CX_AT + 2 * DC, CX_AT + 3 * DC, CX_AT + 4 * DC
POOL_WINDOWS = (2, 4, 8, 16)
PAD = 16
DIL = ((128, 1), (512, 4), (2048, 16))
NEG = -1e30

RAW = 3
SPL = 3
WB, AB = 3, 5
AR = 3
AV = 4
NP_ADA = 24
NU = S // 8

_FAR = [15, 27, 50, 91, 166, 305, 559]


def bucket_steps():
    edges = list(range(1, 9)) + _FAR
    steps = [(-1e9, 15)]
    for b in range(14, -1, -1):
        steps.append((float(-(edges[b] - 1)), b))
    for b in range(1, 16):
        steps.append((float(edges[b - 1]), 16 + b))
    return steps


def host_constants():
    import numpy as np
    c = {}
    c["ident"] = np.eye(P, dtype=np.float32)
    q, k = np.arange(P)[:, None], np.arange(S)[None, :]
    tri = np.where(q >= k[:, :P], 0.0, NEG).astype(np.float32)
    c["causal"] = np.concatenate([tri, np.zeros((P, P), np.float32), tri], axis=1)
    i, j = np.arange(S)[:, None], np.arange(S)[None, :]
    dil = np.stack([np.where(((i - j) % r == 0) & (np.abs(i - j) // r <= w // (2 * r)), 0.0, NEG)
                    for w, r in DIL], axis=1).astype(np.float32)
    c["dilmask"] = dil.reshape(TT, P, NG * S)
    inv = np.zeros((P, 2, S), np.float32)
    for g, w in enumerate(POOL_WINDOWS):
        inv[(g % 2) * 64:(g % 2) * 64 + 64, g // 2] = 1.0 / np.minimum(np.arange(S) + 1.0, w)
    c["invcount"] = inv.reshape(P, 2 * S)
    half = MROPE // 2
    c["freq"] = np.tile((1.0 / (10000.0 ** (np.arange(half, dtype=np.float32) / half))).astype(np.float32), (P, 1))
    steps = bucket_steps()
    m = np.zeros((32, 96), np.float32)
    thr = np.full((96, 1), 1e9, np.float32)
    for n, (lo, b) in enumerate(steps):
        for part in range(3):
            m[b, 32 * part + n] += 1.0
            if n:
                m[steps[n - 1][1], 32 * part + n] -= 1.0
            thr[32 * part + n] = lo
    c["stepmat"], c["thr"] = m, thr
    return c


def block_pair(nc, ins, out):
    A = ins
    with ExitStack() as ctx:
        def sem(name):
            return ctx.enter_context(nc.semaphore(name))

        def sb(name, shape, dt=F32, at=None):
            return (at or ctx).enter_context(nc.sbuf_tensor(name, shape, dt))

        bias_dram = nc.dram_tensor("bias_scratch", (TT, DH, P, NG * S), F32, kind="Internal").ap()

        raw = [sb(f"raw{i}", [P, 2048]) for i in range(RAW)]
        whi = [sb(f"whi{i}", [P, 2048], F32R) for i in range(SPL)]
        wlo = [sb(f"wlo{i}", [P, 2048], F32R) for i in range(SPL)]
        x = sb("x", [P, TT, D])
        hT_hi, hT_lo = sb("hT_hi", [P, DK, S], F32R), sb("hT_lo", [P, DK, S], F32R)
        aT_hi, aT_lo = sb("aT_hi", [P, DK, S], F32R), sb("aT_lo", [P, DK, S], F32R)
        h32 = [sb(f"h32_{i}", [P, 2, S]) for i in range(2)]
        ident = sb("ident", [P, P])
        causal = sb("causal", [P, 3 * P])
        invcount = sb("invcount", [P, 2, S])
        ones = sb("ones", [P, 1])
        mhalf = sb("mhalf", [P, 32])
        ss, ms, rstd = (sb(n, [P, 2, 32]) for n in ("ss", "ms", "rstd"))
        NA_ROWS, NB_ROWS = 105, 108
        colA, colB = sb("colA", [P, NA_ROWS]), sb("colB", [P, NB_ROWS])
        fb = sb("fb", [H1, DEPTH])
        csil = sb("csil", [P, DK])
        mods = sb("mods", [P, DEPTH, 48])
        gain2 = sb("gain2", [P, DEPTH, 2, DK])
        cosn, sinn = sb("cosn", [P, TT, 16]), sb("sinn", [P, TT, 16])
        poolw = sb("poolw", [P, 2, S])
        gq8 = sb("gq8", [P, 8])
        nmax, zsum, rz = (sb(n, [P, 2, TT]) for n in ("nmax", "zsum", "rz"))
        mx = sb("mx", [P, 2, TT])

        def c_mix(l): return 8 * l
        def c_ffn(l): return 16 + 8 * l
        def c_psc(l): return 32 + 8 * l
        def c_mix2(l): return 48 + 8 * l
        def c_mlp2(l): return 64 + 8 * l
        def c_conv(l, j): return 80 + 6 * l + 2 * j
        C_COND, C_QA, C_KVA = 92, 100, 103
        def b_ada(l): return 48 * l
        B_Q1, B_K1, B_DQ, B_DK, B_MQ, B_MK = 96, 98, 100, 103, 106, 107

        with ExitStack() as ph:
            rowA, rowB = sb("rowA", [NA_ROWS, P], at=ph), sb("rowB", [NB_ROWS, P], at=ph)
            pos_t = sb("pos_t", [P, TT], I32, ph)
            posf = sb("posf", [P, TT], at=ph)
            freq = sb("freq", [P, 16], at=ph)
            ang = sb("ang", [P, 6, TT * 16], at=ph)
            angi = sb("angi", [P, TT * 16], I32, ph)
            sq1 = sb("sq1", [P, D], at=ph)
            xn1 = sb("xn1", [P, TT, D], at=ph)
        with ExitStack() as ph:
            gates = sb("gates", [P, 24, S], at=ph)
            qT1, kT1 = sb("qT1", [P, 4, S], at=ph), sb("kT1", [P, 4, S], at=ph)
            V1 = sb("V1", [P, TT, DA], at=ph)
            zf, tf = sb("zf", [H1, S], at=ph), sb("tf", [H1, S], at=ph)
            mf, ncum = sb("mf", [H1, S], at=ph), sb("ncum", [H1, S], at=ph)
            zero8 = sb("zero8", [H1, S], at=ph)
            sqh = [sb(f"sqh{i}", [P, 512], at=ph) for i in range(2)]
            qn = [sb(f"qn{i}", [P, TT, 256], at=ph) for i in range(2)]
            cxs, cbs = sb("cxs", [P, 2, S], at=ph), sb("cbs", [P, 2, S], at=ph)
            zc = sb("zc", [P, 2, S + 2], at=ph)
            cva, cvb = sb("cva", [P, 2, S], at=ph), sb("cvb", [P, 2, S], at=ph)
            pu, s2, s4 = (sb(n, [P, 2, S + PAD], at=ph) for n in ("pu", "s2", "s4"))
            s8, s16 = (sb(n, [P, S + PAD], at=ph) for n in ("s8", "s16"))
            pd = sb("pd", [P, 2, S], at=ph)
            L1, P1 = ([sb(f"{n}{i}", [P, 3 * P], at=ph) for i in range(2)] for n in ("L1_", "P1_"))
            PT1 = [sb(f"PT1_{i}", [P, 3 * P], at=ph) for i in range(2)]
            mg = gates[:, 2 * DK:3 * DK, :]
            mt = [sb(f"mt{i}", [P, 2, S], at=ph) for i in range(2)]
        with ExitStack() as ph:
            sqf = sb("sqf", [P, D], at=ph)
            xnf = sb("xnf", [P, TT, D], at=ph)
            ada_raw = [sb(f"ada_raw{i}", [P, D], at=ph) for i in range(AR)]
            ada_tmp = [sb(f"ada_tmp{i}", [P, D], at=ph) for i in range(2)]
            ada_acc = sb("ada_acc", [P, 3 * D], at=ph)
            sg = [sb(f"sg{i}", [P, 2, S], at=ph) for i in range(2)]
            dmask = sb("dmask", [P, NG, S], at=ph)
            posb = sb("posb", [96, S], I32, ph)
            hi16, lo16 = sb("hi16", [96, S], at=ph), sb("lo16", [96, S], at=ph)
            ihi, ilo = sb("ihi", [96, S], I32, ph), sb("ilo", [96, S], I32, ph)
            relk, relq = sb("relk", [96, S], at=ph), sb("relq", [96, S], at=ph)
            thr = sb("thr", [96, 1], at=ph)
            stepmat = sb("stepmat", [32, 96], at=ph)
            relb = sb("relb", [32, NG * DH], at=ph)
            dres = sb("dres", [96, 3, NG * DH], at=ph)
            dpart = sb("dpart", [96, 3, NG * DH], BF16, ph)
            dsel = sb("dsel", [96, NG * DH], BF16, ph)
            Gst = [sb(f"Gst{i}", [96, 8, P], BF16, ph) for i in range(2)]
            stage0 = sb("stage0", [P, NG * DH, 32], at=ph)
            stage = [stage0[:, :, :], xnf[:, :, :].rearrange("p t n -> p (t n)")[:, 0:NG * DH * 32]
                     .rearrange("p (a k) -> p a k", k=32)]
        with ExitStack() as ph:
            sqm = sb("sqm", [P, D], at=ph)
            xnm = sb("xnm", [P, TT, D], at=ph)
        with ExitStack() as ph:
            lat = sb("lat", [P, TT, 672], at=ph)
            latn = sb("latn", [P, TT, 640], at=ph)
            q96, k96 = sb("q96", [P, TT, MH * MQK], at=ph), sb("k96", [P, TT, MH * MQK], at=ph)
            rt = sb("rt", [P, 4, TT * MH * 16], at=ph)
            qTm, kTm = sb("qTm", [MQK, MH, S], at=ph), sb("kTm", [MQK, MH, S], at=ph)
            Vm = sb("Vm", [P, TT, MH * 64], at=ph)
            krope = sb("krope", [P, TT, MROPE], at=ph)
            sq96 = rt[:, :, :].rearrange("p a n -> p (a n)")[:, 0:MH * MQK]
        with ExitStack() as ph:
            Pm = [sb(f"Pm{i}", [P, TT, S], at=ph) for i in range(3)]
            PTm = [sb(f"PTm{i}", [P, TT, S], at=ph) for i in range(2)]
            gbc0 = sb("gbc0", [P, D], at=ph)
            gy0 = [sb(f"gy0_{i}", [P, TT, 256], at=ph) for i in range(2)]
        with ExitStack() as ph:
            sqd = sb("sqd", [P, D], at=ph)
            xnd = sb("xnd", [P, TT, D], at=ph)
        with ExitStack() as ph:
            qTd, kTd = ([sb(f"{n}{i}", [P, NG, 2, S], at=ph) for i in range(2)] for n in ("qTd", "kTd"))
            Vd = [sb(f"Vd{i}", [P, NG, TT, 256], at=ph) for i in range(2)]
            sqh2 = [sb(f"sqh2_{i}", [P, 512], at=ph) for i in range(2)]
            qn2 = [sb(f"qn2_{i}", [P, TT, 256], at=ph) for i in range(2)]
            biasb = [sb(f"biasb{i}", [P, TT, NG * S], at=ph) for i in range(2)]
            Ld = [sb(f"Ld{i}", [P, TT, NG * S], at=ph) for i in range(2)]
            PTd = sb("PTd", [P, NG, TT, S], at=ph)
            gbc = sb("gbc", [P, D], at=ph)
            gy1 = [sb(f"gy1_{i}", [P, TT, 256], at=ph) for i in range(2)]
        with ExitStack() as ph:
            sqp = sb("sqp", [P, D], at=ph)
            xnp = sb("xnp", [P, TT, D], at=ph)
            rl = [sb(f"rl{i}", [P, 2, S], at=ph) for i in range(2)]
            gbc2 = sb("gbc2", [P, D], at=ph)
            gy2 = sb("gy2", [P, 512], at=ph)
            ada_raw2 = [sb(f"ada_raw2_{i}", [P, D], at=ph) for i in range(AR)]
            ada_tmp2 = [sb(f"ada_tmp2_{i}", [P, D], at=ph) for i in range(2)]
            ada_acc2 = [sb(f"ada_acc2_{i}", [P, 3 * D], at=ph) for i in range(2)]
            ada_rawv = [sb(f"ada_rawv{i}", [P, D], at=ph) for i in range(AV)]

        bank = [ctx.enter_context(nc.psum_tensor(f"bank{i}", [P, 512], F32)) for i in range(WB + AB)]

        s_raw = [sem(f"raw_arrived{i}") for i in range(RAW)]
        s_hi, s_lo = sem("high_part_ready"), sem("low_part_ready")
        s_w, s_a, s_acc = sem("projection_summed"), sem("attention_summed"), sem("down_chunk_added")
        drained = [sem(f"bank_drained{i}") for i in range(WB + AB)]
        s_rows, s_const, s_set = sem("rows_loaded"), sem("constants_loaded"), sem("memsets_done")
        s_ropein, s_rope = sem("angles_ready"), sem("rope_ready")
        s_x = sem("x_loaded")
        s_ss, s_ms, s_rstd, s_xn = sem("squares_summed"), sem("mean_square_ready"), sem("rstd_ready"), sem("x_normed")
        s_hhi, s_hlo = sem("h_high_ready"), sem("h_low_ready")
        s_sq = sem("head_squares_ready")
        s_z, s_zt, s_cum = sem("forget_logit_ready"), sem("forget_softplus_ready"), sem("forget_sum_ready")
        s_cv, s_cvhi, s_cvlo = sem("conv_ready"), sem("conv_high_ready"), sem("conv_low_ready")
        s_pd = sem("pool_ready")
        s_nmax, s_exp, s_rz = sem("row_max_ready"), sem("exp_ready"), sem("row_sum_inverted")
        s_athi = sem("attn_high_ready")
        s_hidhi, s_hidlo = sem("hidden_high_ready"), sem("hidden_low_ready")
        s_ada = [sem(f"ada_arrived{i}") for i in range(AR)]
        s_adaused, s_adasum, s_csil = sem("ada_piece_used"), sem("ada_summed"), sem("cond_ready")
        s_bin, s_g = sem("bias_inputs_loaded"), sem("steps_built")
        s_bout, s_bld = [sem(f"bias_stored{i}") for i in range(2)], [sem(f"bias_loaded{i}") for i in range(2)]
        s_mods, s_latn, s_q96, s_sq96 = sem("mods_ready"), sem("latent_normed"), sem("heads_normed"), sem("head96_squares")
        s_poolw, s_set0, s_freq = sem("pool_weights_loaded"), sem("rows_cleared"), sem("frequencies_loaded")
        s_final, s_latss, s_hn = sem("result_ready"), sem("latent_squares_summed"), sem("head_squares_summed")
        s_roped, s_sum96, s_hid32 = sem("heads_rotated"), sem("head96_squares_summed"), sem("hidden_ready")
        s_adav = [sem(f"ada_arrived_vector{i}") for i in range(AV)]
        s_adastep = sem("ada_vector_step")
        s_x2, s_mg = sem("x_updated"), sem("branches_merged")
        s_dc, s_ac, s_pc = sem("vector_step"), sem("scalar_step"), sem("pool_step")
        s_out = sem("out_stored")

        chunks, chunk_at, names = [], {}, []

        def chunk(name, src):
            chunk_at[name] = len(chunks)
            names.append(name)
            chunks.append(src)

        def kmajor(w, c0, n):
            return w[:, c0:c0 + n].rearrange("(k p) n -> p k n", p=P)

        for l in range(DEPTH):
            w_in = A["w_in"][l]
            chunk(("F", l), kmajor(w_in, F_AT, P))
            for n, c0 in (("Q", 0), ("K", DA), ("V", 2 * DA)):
                for c in range(2):
                    chunk((n, l, c), kmajor(w_in, c0 + 256 * c, 256))
            for n, c0 in (("PX", PX_AT), ("CX", CX_AT), ("CC", CC_AT), ("CB", CB_AT)):
                chunk((n, l), kmajor(w_in, c0, 256))
            for c in range(12):
                chunk(("G", l, c), kmajor(w_in, G_AT + 256 * c, 256))
            chunk(("CO", l), kmajor(A["w_conv_out"][l], 0, D))
            for c in range(2):
                chunk(("AO", l, c), kmajor(A["w_attn_out"][l], 512 * c, 512))
            for c in range(4):
                chunk(("WO", l, c), kmajor(A["w_o"][l], 256 * c, 256))
            for c in range(NF1 + 1):
                if c < NF1:
                    chunk(("GT", l, c), kmajor(A["w_ffn_in"][l], 256 * c, 256))
                    chunk(("UP", l, c), kmajor(A["w_ffn_in"][l], FF1 + 256 * c, 256))
                if c:
                    chunk(("DN", l, c - 1), kmajor(A["w_ffn_out"][l][256 * (c - 1):256 * c, :], 0, D))
        for i in range(DEPTH):
            if i == 0:
                for c in range(3):
                    chunk(("LI", c), kmajor(A["mla_w_in_2"][0], 256 * c, min(256, 672 - 256 * c)))
                for c in range(4):
                    chunk(("QB", c), kmajor(A["mla_w_qb_2"][0], 384 * c, 384))
                for c in range(2):
                    chunk(("KV", c), kmajor(A["mla_w_kvb_2"][0], D * c, D))
                for c in range(4):
                    chunk(("MO", 0, c), kmajor(A["mla_w_o_2"][0], 256 * c, 256))
            else:
                for j in range(4):
                    for g in range(NG):
                        for n in range(3):
                            chunk(("D", j, g, n), kmajor(A["dil_w_in_2"][0], (3 * g + n) * D + 256 * j, 256))
                for c in range(4):
                    chunk(("MO", 1, c), kmajor(A["dil_w_o_2"][0], 256 * c, 256))
            for c in range(NF2 + 1):
                if c < NF2:
                    chunk(("M1", i, c), kmajor(A["mlp_w1_2"][i], 256 * c, 256))
                if c:
                    chunk(("M2", i, c - 1), kmajor(A["mlp_w2_2"][i][256 * (c - 1):256 * c, :], 0, D))

        def view(buf, c):
            kk, n = chunks[c].shape[1:]
            return buf[:, 0:kk * n].rearrange("p (k n) -> p k n", k=kk)

        h_done, n_pairs = {}, 0
        for name, k in ((("nrm", 0), 4), (("mg", 0), 4), (("nrm", 1), 4), (("nrm", 2), 4), (("mg", 1), 4),
                        (("nrm", 3), 4), (("nrm", 4), 4), (("lat",), 3), (("nrm", 5), 4), (("nrm", 6), 4),
                        (("nrm", 7), 4)):
            n_pairs += k
            h_done[name] = n_pairs

        CONSTS, BIN, N_ROWS_DMA = 16 * 4, 16 * 5, 27
        jobs, chunk_done = {}, []
        def unit1(l, h): return 8 * l + h
        def unitm(h): return 16 + h
        def unitd(h): return 32 + h

        def full(eng, name):
            s, n, b, _ = jobs[name]
            eng.wait_ge(s, n)
            return bank[b]

        def drain_sem(name):
            return drained[jobs[name][2]]

        def emptied(eng, name):
            _, _, b, k = jobs[name]
            eng.wait_ge(drained[b], k)

        def idle(*_):
            pass

        def dilated(project, scores, exps, turn_probs, values, turn_pair, ready):
            left = [("D", j, g, m3) for j in range(DH // HB) for g in range(NG) for m3 in range(3)]

            def ahead(j, n=1):
                for _ in range(n):
                    if left and left[0][1] <= j:
                        project(left.pop(0))

            ahead(0, 3 * NG)
            for j in range(DH // HB):
                ready(j)
                for i in range(HB + 1):
                    if i < HB:
                        scores(j, i)
                    if i == 3:
                        turn_pair(j, 0)
                    if i < HB:
                        ahead(j + 1)
                        exps(j, i)
                    if i:
                        turn_probs(j, i - 1)
                        ahead(j + 1)
                        values(j, i - 1)
                ahead(j + 1, 3 * NG)
                turn_pair(j, 1)

        block = ctx.enter_context(nc.Block())

        @block.tensor
        def _(pe):
            n = {"w": 0, "a": 0, "acc": 0, "c": 0}
            ended = {"w": 0, "a": 0}

            def begin(kind, name):
                j, nb = n[kind], (WB if kind == "w" else AB)
                n[kind] += 1
                b = j % nb + (WB if kind == "a" else 0)
                if j >= nb:
                    pe.wait_ge(drained[b], j // nb)
                jobs[name] = (kind, None, b, j // nb + 1)
                return bank[b]

            def end(ins, name):
                kind, _, b, k = jobs[name]
                s = s_w if kind == "w" else s_a
                ins.then_inc(s, 1)
                ended[kind] += 1
                jobs[name] = (s, ended[kind], b, k)

            def weights(name):
                c = chunk_at[name]
                assert c == n["c"], (name, c, n["c"])
                n["c"] += 1
                pe.wait_ge(s_lo, c + 1)
                return view(whi[c % SPL], c), view(wlo[c % SPL], c)

            def used(name):
                chunk_done.append(jobs[name][:2])

            def mm3(dst, lh, ll, rh, rl, start, stop):
                pe.matmul(dst, lh, rh, start=start, stop=False)
                pe.matmul(dst, lh, rl, start=False, stop=False)
                return pe.matmul(dst, ll, rh, start=False, stop=stop)

            def await_pair(what, t, k):
                if what and t == 0 and k % 2 == 0:
                    pe.wait_ge(s_hlo, h_done[what] - DK // 2 + k // 2 + 1)

            def feature_major(name, w, cols, a_hi, a_lo, k0, kk, first_of=None):
                bk = begin("w", name)
                for t, c0 in enumerate(cols):
                    for k in range(kk):
                        await_pair(first_of, t, k)
                        m = mm3(bk[:, S * t:S * t + S], w[0][:, k, c0:c0 + P], w[1][:, k, c0:c0 + P],
                                a_hi[:, k0 + k, :], a_lo[:, k0 + k, :], k == 0, k == kk - 1)
                end(m, name)

            def token_major(name, w, c0, nc_, a_hi, a_lo, k0, kk, toks=(0, 1), first_of=None):
                bk = begin("w", name)
                for i, t in enumerate(toks):
                    for k in range(kk):
                        await_pair(first_of, i, k)
                        m = mm3(bk[:, 256 * i:256 * i + nc_], a_hi[:, k0 + k, P * t:P * t + P],
                                a_lo[:, k0 + k, P * t:P * t + P], w[0][:, k, c0:c0 + nc_], w[1][:, k, c0:c0 + nc_],
                                k == 0, k == kk - 1)
                end(m, name)

            def turn(name, src, nblk, w=P):
                bk = begin("w", name)
                for i in range(nblk):
                    for t in range(TT):
                        m = pe.transpose(bk[0:w, S * i + P * t:S * i + P * t + P], src(i, t), ident[:, :])
                end(m, name)

            def norm(e, xn):
                pe.wait_ge(s_xn, 2 * e + 2)
                for kp in range(DK // 2):
                    turn(("nrm", e, kp), lambda i, t: xn[:, t, P * (2 * kp + i):P * (2 * kp + i) + P], 2)

            def qk_turn(r, job, buf):
                emptied(pe, job)
                turn(("qkT", r), lambda i, t: buf[:, t, P * i:P * i + P], 2)

            pe.wait_ge(s_const, CONSTS)
            pe.wait_ge(s_rows, 16 * N_ROWS_DMA)
            pe.wait_ge(s_set, 1)
            bk = begin("w", "colA")
            end(pe.transpose(bk[:, 0:NA_ROWS], rowA[:, :], ident[0:NA_ROWS, 0:NA_ROWS]), "colA")
            bk = begin("w", "colB")
            end(pe.transpose(bk[:, 0:NB_ROWS], rowB[:, :], ident[0:NB_ROWS, 0:NB_ROWS]), "colB")

            def head_out(u, v, pt, tiles):
                bk = begin("w", ("O", u))
                for t in range(TT):
                    for i, kt in enumerate(tiles[t]):
                        m = pe.matmul(bk[:, HD * t:HD * t + HD], pt(kt, t), v(kt), start=i == 0, stop=i == len(tiles[t]) - 1)
                end(m, ("O", u))

            def turn_pair(pair):
                emptied(pe, ("O", 2 * pair))
                emptied(pe, ("O", 2 * pair + 1))
                turn(("OT", pair), lambda i, t: h32[pair % 2][:, 0, P * t:P * t + P], 1)

            def ffn_down(key, c, accs, nf, hid0):
                w = weights((key[0], key[1], c))
                pe.wait_ge(s_hidlo, hid0 + c + 1)
                sl = 2 * (c % 3)
                for t in range(TT):
                    for half in range(2):
                        for k in range(2):
                            m = mm3(accs[2 * t + half][:, :], aT_hi[:, sl + k, P * t:P * t + P],
                                    aT_lo[:, sl + k, P * t:P * t + P], w[0][:, k, 512 * half:512 * half + 512],
                                    w[1][:, k, 512 * half:512 * half + 512], c == 0 and k == 0, c == nf - 1 and k == 1)
                        if c == nf - 1 or (t, half) == (1, 1):
                            n["acc"] += 1
                            m.then_inc(s_acc, 1)
                        if c == nf - 1:
                            nm = (key[0], key[1], "sum", 2 * t + half)
                            jobs[nm] = (s_acc, n["acc"]) + jobs[nm][2:]
                chunk_done.append((s_acc, n["acc"]))

            def mod_columns(h, acc):
                bk = begin("w", ("mod", h))
                for k in range(24):
                    m = pe.matmul(bk[:, k:k + 1], acc[:, P * k:P * k + P], ones[:, :], start=True, stop=True)
                end(m, ("mod", h))

            for l in range(DEPTH):
                norm(2 * l, xn1)
                w = weights(("F", l))
                bk = begin("w", ("F", l))
                for k in range(DK):
                    await_pair(("nrm", 2 * l), 0, k)
                    m = mm3(bk[:, 0:S], w[0][:, k, :], w[1][:, k, :], hT_hi[:, k, :], hT_lo[:, k, :], k == 0, k == DK - 1)
                end(m, ("F", l))
                used(("F", l))
                order = [("Q", 0), ("Q", 1), ("K", 0), ("K", 1), ("V", 0), ("V", 1)]
                for i, (nm, c) in enumerate(order):
                    w = weights((nm, l, c))
                    token_major((nm, l, c), w, 0, 256, hT_hi, hT_lo, 0, DK)
                    used((nm, l, c))
                    if 1 <= i <= 4:
                        r = 4 * l + i - 1
                        qk_turn(r, (order[i - 1][0], l, order[i - 1][1]), qn[r % 2])
                for nm in ("PX", "CX", "CC", "CB"):
                    w = weights((nm, l))
                    feature_major((nm, l), w, (0, P), hT_hi, hT_lo, 0, DK)
                    used((nm, l))

                def gate(c):
                    w = weights(("G", l, c))
                    feature_major(("G", l, c), w, (0, P), hT_hi, hT_lo, 0, DK)
                    used(("G", l, c))

                emptied(pe, ("qkT", 4 * l + 3))
                emptied(pe, ("V", l, 1))
                emptied(pe, ("qkT", 4 * l + 2))
                emptied(pe, ("qkT", 4 * l + 1))
                pe.wait_ge(s_cum, l + 1)
                g = 0
                for i in range(H1 + 3):
                    if i < H1:
                        u = unit1(l, i)
                        bk = begin("a", ("S", u))
                        r0, t = 64 * (i % 2), i // 2
                        for q0, q1, c0 in ((0, P, 0), (P, S, P)):
                            pe.matmul(bk[:, c0:c0 + q1], qT1[r0:r0 + 64, t, q0:q1], kT1[r0:r0 + 64, t, 0:q1],
                                      start=True, stop=False)
                            m = pe.matmul(bk[:, c0:c0 + q1], ident[0:H1, i:i + 1].broadcast_to([H1, P]),
                                          ncum[:, 0:q1], start=False, stop=True)
                        end(m, ("S", u))
                    if g < 12:
                        gate(g)
                        g += 1
                    if 1 <= i <= H1:
                        u = unit1(l, i - 1)
                        pe.wait_ge(s_exp, 2 * u + 2)
                        bk = begin("a", ("T", u))
                        pr = P1[u % 2]
                        pe.transpose(bk[:, 0:P], pr[:, 0:P], ident[:, :])
                        pe.transpose(bk[:, P:2 * P], pr[:, P:2 * P], ident[:, :])
                        end(pe.transpose(bk[:, 2 * P:3 * P], pr[:, 2 * P:3 * P], ident[:, :]), ("T", u))
                    if g < 12 and i % 4 == 0:
                        gate(g)
                        g += 1
                    if 2 <= i < H1 + 2:
                        u = unit1(l, i - 2)
                        emptied(pe, ("T", u))
                        head_out(u, lambda kt, h=i - 2: V1[:, kt, HD * h:HD * h + HD],
                                 lambda kt, t, pt=PT1[u % 2]: pt[:, P * (t + kt):P * (t + kt) + P], ((0,), (0, 1)))
                    if i >= 4 and i % 2 == 0:
                        turn_pair(unit1(l, i - 4) // 2)
                while g < 12:
                    gate(g)
                    g += 1
                pe.wait_ge(s_poolw, 16 * (l + 1))
                pe.wait_ge(s_pd, l + 1)
                for gi in range(4):
                    bk = begin("w", ("YP", l, gi))
                    r0 = 64 * (gi % 2)
                    for half in range(2):
                        m = pe.matmul(bk[:, S * half:S * half + S], poolw[r0:r0 + 64, gi // 2, P * half:P * half + P],
                                      pd[r0:r0 + 64, gi // 2, :], start=True, stop=True)
                    end(m, ("YP", l, gi))
                w = weights(("CO", l))
                pe.wait_ge(s_cvlo, l + 1)
                for jp in range(4):
                    feature_major(("YC", l, jp), w, (256 * jp, 256 * jp + P), aT_hi, aT_lo, 4, 2)
                used(("YC", l, 3))
                for h in range(0, H1, 2):
                    emptied(pe, ("OT", unit1(l, h) // 2))
                for c in range(2):
                    w = weights(("AO", l, c))
                    for jp in range(2):
                        feature_major(("YA", l, 2 * c + jp), w, (256 * jp, 256 * jp + P), aT_hi, aT_lo, 0, 4)
                    used(("YA", l, 2 * c + 1))
                for c in range(4):
                    w = weights(("WO", l, c))
                    token_major(("WO", l, c), w, 0, 256, hT_hi, hT_lo, 0, DK, first_of=None if c else ("mg", l))
                    used(("WO", l, c))
                norm(2 * l + 1, xnf)
                accs = None

                def biases(u):
                    if u >= NU:
                        return
                    pe.wait_ge(s_g, NU * l + u + 1)
                    bk = begin("w", ("B", l, u))
                    gb = Gst[(NU * l + u) % 2]
                    for k in range(8):
                        m = pe.matmul(bk[:, 48 * k:48 * k + 48], gb[:, k, :], dsel[:, :], start=True, stop=True)
                    end(m, ("B", l, u))

                for c in range(NF1 + 1):
                    if c < NF1:
                        for i, nm in enumerate(("GT", "UP")):
                            w = weights((nm, l, c))
                            feature_major((nm, l, c), w, (0, P), hT_hi, hT_lo, 0, DK,
                                          first_of=None if c or i else ("nrm", 2 * l + 1))
                            used((nm, l, c))
                            if (c, i) == (0, 0):
                                pe.wait_ge(s_bin, BIN * (l + 1))
                                bk = begin("w", ("steps", l))
                                end(pe.matmul(bk[0:96, 0:NG * DH], stepmat[:, :], relb[:, :], start=True, stop=True),
                                    ("steps", l))
                            if c:
                                biases(3 * c + i)
                        if c == 0:
                            biases(0)
                            biases(1)
                    if c:
                        if c == 1:
                            accs = [begin("a", ("DN", l, "sum", q)) for q in range(4)]
                        if c == NF1:
                            pe.wait_ge(s_adasum, l + 1)
                            mod_columns(l, ada_acc)
                        ffn_down(("DN", l), c - 1, accs, NF1, NF1 * l)
                    if c < NF1:
                        biases(3 * c + 2)

            def gate_rows(e, col0, i):
                pe.wait_ge(s_mods, 2 * i + (2 if col0 >= 24 else 1))
                for half in range(2):
                    bk = begin("w", ("gb", e, half))
                    for k in range(4):
                        kk = col0 + 4 * half + k
                        m = pe.matmul(bk[:, P * k:P * k + P], mods[:, i, kk:kk + 1].broadcast_to([P, P]), ident[:, :],
                                      start=True, stop=True)
                    end(m, ("gb", e, half))

            def wo(i):
                gate_rows(2 * i, 16, i)
                for h in range(0, MH, 2):
                    emptied(pe, ("OT", (unitm, unitd)[i](h) // 2))
                for c in range(4):
                    w = weights(("MO", i, c))
                    token_major(("MO", i, c), w, 0, 256, aT_hi, aT_lo, 0, DK)
                    used(("MO", i, c))

            def mlp(i):
                norm(5 + 2 * i, xnp)
                gate_rows(2 * i + 1, 40, i)
                accs = None
                for c in range(NF2 + 1):
                    if c < NF2:
                        w = weights(("M1", i, c))
                        feature_major(("M1", i, c), w, (0, P), hT_hi, hT_lo, 0, DK,
                                      first_of=None if c else ("nrm", 5 + 2 * i))
                        used(("M1", i, c))
                    if c:
                        if c == 1:
                            accs = [begin("a", ("M2", i, "sum", q)) for q in range(4)]
                        if i == 0 and c == NF2:
                            pe.wait_ge(s_adastep, NP_ADA)
                            mod_columns(3, ada_acc2[1])
                            pe.wait_ge(s_adasum, 3)
                            mod_columns(2, ada_acc2[0])
                        ffn_down(("M2", i), c - 1, accs, NF2, 2 * NF1 + NF2 * i)

            norm(4, xnm)
            for c in range(3):
                w = weights(("LI", c))
                token_major(("LI", c), w, 0, min(256, 672 - 256 * c), hT_hi, hT_lo, 0, DK,
                            first_of=None if c else ("nrm", 4))
                used(("LI", c))
            pe.wait_ge(s_latn, 1)
            for kp in range(3):
                turn(("latT", kp), lambda i, t: latn[:, t, P * (2 * kp + i):P * (2 * kp + i) + P], 2 if kp < 2 else 1)
            pe.wait_ge(s_hlo, h_done[("lat",)])
            for c in range(4):
                w = weights(("QB", c))
                for t in range(TT):
                    token_major(("QB", c, t), w, 0, 384, hT_hi, hT_lo, 0, 3, (t,))
                used(("QB", c, 1))
            for c in range(2):
                w = weights(("KV", c))
                for t in range(TT):
                    for half in range(2):
                        token_major(("KV", c, t, half), w, 512 * half, 512, hT_hi, hT_lo, 3, 2, (t,))
                used(("KV", c, 1, 1))
            pe.wait_ge(s_q96, 1)
            for hp in range(MH // 2):
                turn(("qT", hp), lambda i, t: q96[:, t, MQK * (2 * hp + i):MQK * (2 * hp + i) + MQK], 2, MQK)
            pe.wait_ge(s_q96, 2)
            for hp in range(MH // 2):
                turn(("kT", hp), lambda i, t: k96[:, t, MQK * (2 * hp + i):MQK * (2 * hp + i) + MQK], 2, MQK)
            for hp in range(MH // 2 - 3, MH // 2):
                emptied(pe, ("kT", hp))
            for i in range(MH + 4):
                if i < MH:
                    u = unitm(i)
                    bk = begin("a", ("S", u))
                    for t in range(TT):
                        m = pe.matmul(bk[:, S * t:S * t + S], qTm[:, i, P * t:P * t + P], kTm[:, i, :],
                                      start=True, stop=True)
                    end(m, ("S", u))
                if 2 <= i < MH + 2:
                    u = unitm(i - 2)
                    pe.wait_ge(s_exp, 2 * u + 2)
                    bk = begin("a", ("T", u))
                    for kt in range(TT):
                        for t in range(TT):
                            m = pe.transpose(bk[:, S * kt + P * t:S * kt + P * t + P],
                                             Pm[u % 3][:, t, P * kt:P * kt + P], ident[:, :])
                    end(m, ("T", u))
                if 3 <= i < MH + 3:
                    u = unitm(i - 3)
                    emptied(pe, ("T", u))
                    head_out(u, lambda kt, h=i - 3: Vm[:, kt, HD * h:HD * h + HD],
                             lambda kt, t, pt=PTm[u % 2]: pt[:, kt, P * t:P * t + P], ((0, 1), (0, 1)))
                if i >= 5 and i % 2:
                    turn_pair(unitm(i - 5) // 2)
            wo(0)
            mlp(0)

            norm(6, xnd)
            todo = []

            def project(chunk_name):
                _, j, g, m3 = chunk_name
                w = weights(chunk_name)
                token_major(chunk_name, w, 0, 256, hT_hi, hT_lo, 0, DK,
                            first_of=("nrm", 6) if chunk_name == ("D", 0, 0, 0) else None)
                used(chunk_name)
                if todo:
                    r, job = todo.pop(0)
                    qk_turn(r, job, qn2[r % 2])
                if m3 < 2:
                    todo.append((8 + 6 * j + 2 * g + m3, chunk_name))

            def scores(j, i):
                u = unitd(HB * j + i)
                r0, pr = 64 * (i % 2), i // 2
                for g in range(NG):
                    bk = begin("a", ("S", u, g))
                    for t in range(TT):
                        m = pe.matmul(bk[:, S * t:S * t + S], qTd[j % 2][r0:r0 + 64, g, pr, P * t:P * t + P],
                                      kTd[j % 2][r0:r0 + 64, g, pr, :], start=True, stop=True)
                    end(m, ("S", u, g))

            def turn_probs(j, i):
                u = unitd(HB * j + i)
                pe.wait_ge(s_exp, 2 * u + 2)
                for g in range(NG):
                    bk = begin("a", ("T", u, g))
                    for kt in range(TT):
                        for t in range(TT):
                            c0 = S * g + P * kt
                            m = pe.transpose(bk[:, S * kt + P * t:S * kt + P * t + P],
                                             Ld[u % 2][:, t, c0:c0 + P], ident[:, :])
                    end(m, ("T", u, g))

            def values(j, i):
                u = unitd(HB * j + i)
                for g in range(NG):
                    emptied(pe, ("T", u, g))
                head_out(u, lambda kt: Vd[j % 2][:, kt // 2, kt % 2, HD * i:HD * i + HD],
                         lambda kt, t: PTd[:, kt // 2, kt % 2, P * t:P * t + P], (range(2 * NG),) * 2)

            def ready(j):
                for g in range(NG):
                    emptied(pe, ("qkT", 8 + 6 * j + 2 * g))
                    emptied(pe, ("qkT", 8 + 6 * j + 2 * g + 1))
                    emptied(pe, ("D", j, g, 2))

            dilated(project, scores, idle, turn_probs, values, lambda j, p: turn_pair(unitd(HB * j + 2 * p) // 2), ready)
            wo(1)
            mlp(1)
            assert n["c"] == len(chunks)

        def rows_of(v):
            return v.rearrange("(r c) -> r c", c=P)

        row_loads = []
        for l in range(DEPTH):
            row_loads += [(rowA[c_mix(l):c_mix(l) + 8, :], rows_of(A["norm_mix_g"][l])),
                          (rowA[c_ffn(l):c_ffn(l) + 8, :], rows_of(A["norm_ffn_g"][l])),
                          (rowA[c_psc(l):c_psc(l) + 8, :], rows_of(A["pool_scale"][l])),
                          (rowA[c_mix2(l):c_mix2(l) + 8, :], rows_of(A["norm_mix_2"][l])),
                          (rowA[c_mlp2(l):c_mlp2(l) + 8, :], rows_of(A["norm_mlp_2"][l])),
                          (rowA[c_conv(l, 0):c_conv(l, 0) + 6, :], A["conv_w"][l].rearrange("j (r c) -> (j r) c", c=P)),
                          (rowB[b_ada(l):b_ada(l) + 48, :], rows_of(A["ada_b_2"][l]))]
        row_loads += [(rowA[C_COND:C_COND + 8, :], rows_of(A["c_2"][0])),
                      (rowA[C_QA:C_QA + 3, :], rows_of(A["mla_g_qa_2"][0])),
                      (rowA[C_KVA:C_KVA + 2, :], rows_of(A["mla_g_kva_2"][0])),
                      (rowB[B_MQ:B_MQ + 1, 0:MQK], A["mla_g_q_2"][0:1, :]),
                      (rowB[B_MK:B_MK + 1, 0:MQK], A["mla_g_k_2"][0:1, :])]
        for half in (0, 64):
            row_loads += [(rowB[B_Q1:B_Q1 + 2, half:half + 64], A["q_norm_g"]),
                          (rowB[B_K1:B_K1 + 2, half:half + 64], A["k_norm_g"]),
                          (rowB[B_DQ:B_DQ + 3, half:half + 64], A["dil_g_q_2"][0]),
                          (rowB[B_DK:B_DK + 3, half:half + 64], A["dil_g_k_2"][0])]
        assert len(row_loads) == N_ROWS_DMA
        N_ROWS_ACT = N_ROWS_DMA // 3

        @block.sync
        def _(sp):
            sp.dma_start(x[:, :, :], A["x"][0].rearrange("(t p) d -> p t d", p=P)).then_inc(s_x, 16)

            def ada_src(h, q):
                k, cb = divmod(q, 3)
                return A["ada_w_2"][h // 2, P * k:P * k + P, D * (3 * (h % 2) + cb):D * (3 * (h % 2) + cb) + D]

            def ada_piece(n):
                if n >= AR:
                    sp.wait_ge(s_adaused, n - AR + 1)
                h, q = divmod(n, NP_ADA)
                sp.dma_start((ada_raw2 if h == 2 else ada_raw)[n % AR][:, :], ada_src(h, q)).then_inc(s_ada[n % AR], 16)

            def ada_piece_v(q):
                if q >= AV:
                    sp.wait_ge(s_adastep, q - AV + 1)
                sp.dma_start(ada_rawv[q % AV][:, :], ada_src(3, q)).then_inc(s_adav[q % AV], 16)

            ada_next = 0
            for c, src in enumerate(chunks):
                name = names[c]
                if c >= RAW:
                    sp.wait_ge(s_lo, c - RAW + 1)
                sp.dma_start(view(raw[c % RAW], c), src).then_inc(s_raw[c % RAW], 16)
                if c == 1:
                    sp.wait_ge(s_set0, 1)
                    for dst, row in row_loads[N_ROWS_ACT:]:
                        sp.dma_start(dst, row).then_inc(s_rows, 16)
                if name[0] == "PX":
                    l = name[1]
                    if l:
                        sp.wait_ge(jobs[("YP", l - 1, 3)][0], jobs[("YP", l - 1, 3)][1])
                    sp.dma_start(poolw[:, :, :], A["pool_w"][l].rearrange("(a b) c d -> (b c) a d", b=2))\
                      .then_inc(s_poolw, 16)
                if name[0] == "UP" and name[2] == 0:
                    l = name[1]
                    sp.wait_ge(s_xn, 2 * (2 * l + 1) + 2)
                    for dst, a in ((posb[:, :], A["positions_2"][0:1, :].broadcast_to([96, S])), (thr[:, :], A["thr"]),
                                   (stepmat[:, :], A["stepmat"]), (relb[:, :], A["rel_bias_2"]),
                                   (dmask[:, :, :], A["dilmask"][l].rearrange("p (g s) -> p g s", g=NG))):
                        sp.dma_start(dst, a).then_inc(s_bin, 16)
                if name[0] in ("GT", "UP", "DN") and name[2] + (name[0] == "DN") >= 1:
                    l = name[1]
                    if ada_next < NP_ADA * (l + 1):
                        ada_piece(ada_next)
                        ada_next += 1
                if name[:2] in (("M1", 0), ("M2", 0)):
                    m2 = name[0] == "M2"
                    r = name[2] + m2
                    if name == ("M1", 0, 1):
                        sp.wait_ge(s_xn, 2 * 5 + 2)
                    if r >= 1 and ada_next < 3 * NP_ADA:
                        ada_piece(ada_next)
                        ada_next += 1
                    q = 2 * (r - 3) + m2
                    if 0 <= q < NP_ADA:
                        ada_piece_v(q)
            sp.wait_ge(s_final, 4)
            sp.dma_start(out[0].rearrange("(t p) d -> p t d", p=P), x[:, :, :]).then_inc(s_out, 16)
            sp.wait_ge(s_out, 16)

        @block.gpsimd
        def _(pool):
            steps = [0]

            def link(ins):
                steps[0] += 1
                ins.then_inc(s_pc, 1)
                pool.wait_ge(s_pc, steps[0])

            pool.memset(rowB[:, :], 0.0).then_inc(s_set0, 1)
            pool.memset(ones[:, :], 1.0).then_inc(s_set, 1)
            pool.memset(mhalf[:, :], -0.5).then_inc(s_set, 1)
            pool.wait_ge(s_set, 2)
            e = [0]

            def rsqrt(w):
                i = e[0]
                e[0] += 1
                pool.wait_ge(s_ms, i + 1)
                pool.tensor_tensor(rstd[:, i % 2, 0:w], ms[:, i % 2, 0:w], mhalf[:, 0:w], ALU.pow).then_inc(s_rstd, 1)

            def ada_half(h, raws, tmps, accs):
                for q in range(NP_ADA):
                    n = NP_ADA * h + q
                    k, cb = divmod(q, 3)
                    pool.wait_ge(s_ada[n % AR], 16 * (n // AR + 1))
                    acc = accs[:, D * cb:D * cb + D]
                    w = raws[n % AR]
                    if k == 0:
                        pool.tensor_scalar(acc, w[:, :], csil[:, k:k + 1], None, ALU.mult).then_inc(s_adaused, 1)
                        continue
                    t = tmps[q % 2]
                    pool.tensor_scalar(t[:, :], w[:, :], csil[:, k:k + 1], None, ALU.mult).then_inc(s_adaused, 1)
                    pool.wait_ge(s_adaused, n + 1)
                    ins = pool.tensor_tensor(acc, acc, t[:, :], ALU.add)
                    if q < NP_ADA - 1:
                        link(ins)
                    else:
                        ins.then_inc(s_adasum, 1)

            for l in range(DEPTH):
                rsqrt(TT)
                for _ in range(4):
                    rsqrt(TT * 4)
                emptied(pool, ("PX", l))
                for b in (pu, s2, s4):
                    link(pool.memset(b[:, :, 0:PAD], 0.0))
                for b in (s8, s16):
                    link(pool.memset(b[:, 0:PAD], 0.0))
                n = S + PAD
                link(pool.tensor_tensor(s2[:, :, 1:n], pu[:, :, 1:n], pu[:, :, 0:n - 1], ALU.add))
                link(pool.tensor_tensor(s4[:, :, 2:n], s2[:, :, 2:n], s2[:, :, 0:n - 2], ALU.add))
                link(pool.tensor_tensor(s8[:, 4:n], s4[:, 1, 4:n], s4[:, 1, 0:n - 4], ALU.add))
                link(pool.tensor_tensor(s16[:, 8:n], s8[:, 8:n], s8[:, 0:n - 8], ALU.add))
                for dst, src, i, p0 in ((pd, s2[:, 0, :], 0, 0), (pd, s4[:, 0, :], 0, 64),
                                        (pd, s8[:, :], 1, 0), (pd, s16[:, :], 1, 64)):
                    link(pool.tensor_tensor(dst[p0:p0 + 64, i, :], src[p0:p0 + 64, PAD:], invcount[p0:p0 + 64, i, :], ALU.mult))
                pool.tensor_tensor(pd[:, :, :], pd[:, :, :], pu[:, :, PAD:], ALU.subtract).then_inc(s_pd, 1)
                rsqrt(TT)
                if l == 0:
                    pool.wait_ge(s_csil, 1)
                else:
                    full(pool, ("mod", 0))
                ada_half(l, ada_raw, ada_tmp, ada_acc)
            rsqrt(TT)
            rsqrt(4)
            rsqrt(32)
            rsqrt(32)
            rsqrt(TT)
            ada_half(2, ada_raw2, ada_tmp2, ada_acc2[0])
            rsqrt(TT)
            for _ in range(24):
                rsqrt(TT * 4)
            rsqrt(TT)

        @block.scalar
        def _(act):
            steps, split_next = [0], [0]

            def link(ins):
                steps[0] += 1
                ins.then_inc(s_ac, 1)
                act.wait_ge(s_ac, steps[0])

            def split_ahead(name, ahead=2):
                while split_next[0] <= min(chunk_at[name] + ahead, len(chunks) - 1):
                    c = split_next[0]
                    split_next[0] += 1
                    act.wait_ge(s_raw[c % RAW], 16 * (c // RAW + 1))
                    if c >= SPL:
                        act.wait_ge(*chunk_done[c - SPL])
                    act.activation(view(whi[c % SPL], c), view(raw[c % RAW], c), ACT.Copy).then_inc(s_hi, 1)

            act.dma_start(pos_t[:, :], A["positions_2"][0].rearrange("(t p) -> p t", p=P), allow_slow_non_contiguous=True).then_inc(s_freq, 16)
            act.dma_start(freq[:, :], A["freq"]).then_inc(s_freq, 16)
            act.dma_start(ident[:, :], A["ident"]).then_inc(s_const, 16)
            act.dma_start(causal[:, :], A["causal"]).then_inc(s_const, 16)
            act.dma_start(invcount[:, :, :], A["invcount"].rearrange("p (a s) -> p a s", a=2)).then_inc(s_const, 16)
            act.dma_start(fb[:, :], A["forget_b"].rearrange("l h -> h l"), allow_slow_non_contiguous=True).then_inc(s_const, 16)
            act.wait_ge(s_set0, 1)
            for dst, src in row_loads[:N_ROWS_ACT]:
                act.dma_start(dst, src).then_inc(s_rows, 16)

            def norm_sums(e, sq):
                for t in range(TT):
                    if e == 0:
                        act.wait_ge(s_x, 16)
                    elif e <= 4:
                        emptied(act, ("WO", e // 2, 3) if e % 2 else ("DN", e // 2 - 1, "sum", 2 * t + 1))
                    else:
                        act.wait_ge(s_x2, {5: 1, 6: 2 + t, 7: 4}[e])
                    if e or t:
                        act.wait_ge(s_ss, 2 * e + t)
                    act.activation(sq[:, :], x[:, t, :], ACT.Square, accum_out=ss[:, 0, t:t + 1]).then_inc(s_ss, 1)

            def h_high(src, dst, scale=1.0):
                act.activation(dst, src, ACT.Copy, scale=scale).then_inc(s_hhi, 1)

            def norm_high(e, what="nrm", pairs=DK // 2):
                for kp in range(pairs):
                    nm = (what, e, kp) if what == "nrm" else (what, kp)
                    emptied(act, nm)
                    w = 2 if not (what == "latT" and kp == 2) else 1
                    h_high(h32[kp % 2][:, 0:w, :], hT_hi[:, 2 * kp:2 * kp + w, :])

            def head_squares(job, r, buf):
                bk = full(act, job)
                if r >= 2:
                    act.wait_ge(s_hn, r - 1)
                act.activation(buf[:, :], bk[:, :], ACT.Square).then_inc(s_sq, 1)

            def exps(u, src, dst):
                act.wait_ge(s_nmax, u + 1)
                if u >= 2:
                    act.wait_ge(s_rz, u - 1)
                for t in range(TT):
                    act.activation(dst(t), src(t), ACT.Exp, bias=nmax[:, u % 2, t:t + 1],
                                   accum_out=zsum[:, u % 2, t:t + 1]).then_inc(s_exp, 1)

            def at_high(pair, k):
                bk = full(act, ("OT", pair))
                act.activation(aT_hi[:, k, :], bk[:, 0:S], ACT.Copy).then_inc(s_athi, 1)

            norm_sums(0, sq1)
            split_ahead(("F", 0), 1)
            full(act, "colA")
            act.activation(colA[:, :], bank[jobs["colA"][2]][:, 0:NA_ROWS], ACT.Copy).then_inc(drain_sem("colA"), 1)
            full(act, "colB")
            act.activation(colB[:, :], bank[jobs["colB"][2]][:, 0:NB_ROWS], ACT.Copy).then_inc(drain_sem("colB"), 1)

            for l in range(DEPTH):
                if l:
                    split_ahead(("F", l))
                    norm_sums(2 * l, sq1)
                norm_high(2 * l)
                split_ahead(("F", l))
                if l == 0:
                    emptied(act, "colA")
                    act.activation(csil[:, :], colA[:, C_COND:C_COND + 8], ACT.Silu).then_inc(s_csil, 1)
                    act.wait_ge(s_ropein, 1)
                    act.activation(cosn[:, :, :], ang[:, 4, :].rearrange("p (t f) -> p t f", t=TT), ACT.Sin).then_inc(s_rope, 1)
                    act.activation(sinn[:, :, :], ang[:, 3, :].rearrange("p (t f) -> p t f", t=TT), ACT.Sin).then_inc(s_rope, 1)
                    act.wait_ge(s_rope, 2)
                act.wait_ge(s_z, l + 1)
                link(act.activation(tf[:, :], zf[:, :], ACT.Abs))
                link(act.activation(tf[:, :], tf[:, :], ACT.Exp, scale=-1.0))
                act.activation(tf[:, :], tf[:, :], ACT.Ln, bias=1.0).then_inc(s_zt, 1)
                order = [("Q", 0), ("Q", 1), ("K", 0), ("K", 1)]

                def qk_out(i):
                    nm, c = order[i]
                    r = 4 * l + i
                    dst, col = (qT1, gq8[:, l:l + 1]) if nm == "Q" else (kT1, colB[:, B_K1 + l:B_K1 + l + 1])
                    bk = full(act, ("qkT", r))
                    act.activation(dst[:, 2 * c:2 * c + 2, :], bk[:, :].rearrange("p (a s) -> p a s", a=2), ACT.Copy,
                                   scale=col).then_inc(drain_sem(("qkT", r)), 1)

                for i, (nm, c) in enumerate(order):
                    split_ahead((nm, l, c))
                    head_squares((nm, l, c), 4 * l + i, sqh[i % 2])
                    if i:
                        qk_out(i - 1)
                for c in range(2):
                    split_ahead(("V", l, c))
                    bk = full(act, ("V", l, c))
                    act.activation(V1[:, :, 256 * c:256 * c + 256], bk[:, :].rearrange("p (t n) -> p t n", t=TT), ACT.Copy)\
                       .then_inc(drain_sem(("V", l, c)), 1)
                    if c == 0:
                        qk_out(3)
                for nm in ("PX", "CX", "CC", "CB"):
                    split_ahead((nm, l))
                    if nm == "CC":
                        continue
                    dst = {"PX": pu[:, :, PAD:], "CX": cxs[:, :, :], "CB": cbs[:, :, :]}[nm]
                    bk = full(act, (nm, l))
                    act.activation(dst, bk[:, :].rearrange("p (a s) -> p a s", a=2), ACT.Copy)\
                       .then_inc(drain_sem((nm, l)), 1)
                g = 0

                def gate(c):
                    split_ahead(("G", l, c))
                    bk = full(act, ("G", l, c))
                    act.activation(gates[:, 2 * c:2 * c + 2, :], bk[:, :].rearrange("p (a s) -> p a s", a=2), ACT.Tanh,
                                   scale=0.5).then_inc(drain_sem(("G", l, c)), 1)

                segs = ((0, P), (P, 3 * P))
                for i in range(H1 + 3):
                    if i < H1:
                        u = unit1(l, i)
                        if i >= 2:
                            full(act, ("T", u - 2))
                        exps(u, lambda t: L1[u % 2][:, segs[t][0]:segs[t][1]], lambda t: P1[u % 2][:, segs[t][0]:segs[t][1]])
                    if g < 12:
                        gate(g)
                        g += 1
                    if 1 <= i <= H1:
                        u = unit1(l, i - 1)
                        bk = full(act, ("T", u))
                        act.activation(PT1[u % 2][:, :], bk[:, 0:3 * P], ACT.Copy).then_inc(drain_sem(("T", u)), 1)
                    if g < 12 and i % 4 == 0:
                        gate(g)
                        g += 1
                    if i >= 4 and i % 2 == 0:
                        at_high(unit1(l, i - 4) // 2, (i - 4) // 2)
                while g < 12:
                    gate(g)
                    g += 1
                act.wait_ge(s_cv, l + 1)
                act.activation(aT_hi[:, 4:6, :], cvb[:, :, :], ACT.Copy).then_inc(s_cvhi, 1)
                split_ahead(("CO", l))
                split_ahead(("AO", l, 0))
                split_ahead(("AO", l, 1))
                for kp in range(4):
                    act.wait_ge(s_mg, 4 * l + kp + 1)
                    h_high(mg[:, 2 * kp:2 * kp + 2, :], hT_hi[:, 2 * kp:2 * kp + 2, :], 0.5)
                for c in range(4):
                    split_ahead(("WO", l, c))
                norm_sums(2 * l + 1, sqf)
                norm_high(2 * l + 1)
                def store_biases(units):
                    for u in units:
                        if u >= 0 and u % 4 == 3:
                            emptied(act, ("B", l, u))
                            k0 = 32 * (u // 4)
                            for g in range(NG):
                                act.dma_start(bias_dram[l, :, :, S * g + k0:S * g + k0 + 32].rearrange("h p k -> p h k"),
                                              stage[(NU * l + u) // 4 % 2][:, DH * g:DH * g + DH, :])\
                                   .then_inc(s_bout[(NU * l + u) // 4 % 2], 16)

                for c in range(NF1 + 1):
                    store_biases([3 * c - 2])
                    if c < NF1:
                        split_ahead(("GT", l, c))
                        bk = full(act, ("GT", l, c))
                        if c >= 2:
                            emptied(act, ("UP", l, c - 2))
                        act.activation(sg[c % 2][:, :, :], bk[:, :].rearrange("p (a s) -> p a s", a=2), ACT.Silu)\
                           .then_inc(drain_sem(("GT", l, c)), 1)
                        store_biases([3 * c - 1])
                        split_ahead(("UP", l, c))
                        store_biases([3 * c])
                        emptied(act, ("UP", l, c))
                        if c >= 3:
                            act.wait_ge(*chunk_done[chunk_at[("DN", l, c - 3)]])
                        act.activation(aT_hi[:, 2 * (c % 3):2 * (c % 3) + 2, :], h32[c % 2][:, :, :], ACT.Copy)\
                           .then_inc(s_hidhi, 1)
                    if c:
                        split_ahead(("DN", l, c - 1))
                for i in range(2):
                    act.wait_ge(s_bout[i], 16 * NG * NU // 8 * (l + 1))

            def gate_rows(e, dst):
                for half in range(2):
                    bk = full(act, ("gb", e, half))
                    act.activation(dst[:, 512 * half:512 * half + 512], bk[:, :], ACT.Copy)\
                       .then_inc(drain_sem(("gb", e, half)), 1)

            def wo(i):
                for c in range(4):
                    split_ahead(("MO", i, c))

            def mlp(i):
                norm_sums(5 + 2 * i, sqp)
                norm_high(5 + 2 * i)
                gate_rows(2 * i + 1, gbc2)
                for c in range(NF2 + 1):
                    if c < NF2:
                        split_ahead(("M1", i, c))
                        bk = full(act, ("M1", i, c))
                        if c >= 2:
                            act.wait_ge(s_hid32, NF2 * i + c - 1)
                        act.activation(rl[c % 2][:, :, :], bk[:, :].rearrange("p (a s) -> p a s", a=2), ACT.Relu)\
                           .then_inc(drain_sem(("M1", i, c)), 1)
                        act.wait_ge(s_hid32, NF2 * i + c + 1)
                        if c >= 3:
                            act.wait_ge(*chunk_done[chunk_at[("M2", i, c - 3)]])
                        act.activation(aT_hi[:, 2 * (c % 3):2 * (c % 3) + 2, :], h32[c % 2][:, :, :], ACT.Copy)\
                           .then_inc(s_hidhi, 1)
                    if c:
                        split_ahead(("M2", i, c - 1))

            norm_sums(4, sqm)
            norm_high(4)
            for c in range(3):
                split_ahead(("LI", c))
                w = min(256, 672 - 256 * c)
                bk = full(act, ("LI", c))
                act.activation(lat[:, :, 256 * c:256 * c + w], bk[:, :].rearrange("p (t n) -> p t n", t=TT)[:, :, 0:w],
                               ACT.Copy).then_inc(drain_sem(("LI", c)), 1)
            emptied(act, ("LI", 0))
            emptied(act, ("LI", 1))
            for t in range(TT):
                for n, (a, b) in enumerate(((0, QL), (QL, QL + KVL))):
                    ins = act.activation(sq96[:, a:b], lat[:, t, a:b], ACT.Square,
                                         accum_out=ss[:, 0, 2 * t + n:2 * t + n + 1])
                    if (t, n) == (1, 1):
                        ins.then_inc(s_latss, 1)
                    else:
                        link(ins)
            norm_high(0, "latT", 3)
            for c in range(4):
                split_ahead(("QB", c))
                for t in range(TT):
                    bk = full(act, ("QB", c, t))
                    act.activation(q96[:, t, 384 * c:384 * c + 384], bk[:, 0:384], ACT.Copy)\
                       .then_inc(drain_sem(("QB", c, t)), 1)

            def squares96(n, buf):
                act.wait_ge(s_roped, n + 1)
                for t in range(TT):
                    if n or t:
                        act.wait_ge(s_sum96, 2 * n + t)
                    act.activation(sq96[:, :], buf[:, t, :], ACT.Square).then_inc(s_sq96, 1)

            def turned96(what, dst, col):
                for hp in range(MH // 2):
                    bk = full(act, (what, hp))
                    act.activation(dst[:, 2 * hp:2 * hp + 2, :], bk[0:MQK, :].rearrange("p (a s) -> p a s", a=2),
                                   ACT.Copy, scale=col).then_inc(drain_sem((what, hp)), 1)

            for c in range(2):
                split_ahead(("KV", c))
                for t in range(TT):
                    for half in range(2):
                        nm = ("KV", c, t, half)
                        bk = full(act, nm)
                        v = bk[:, :].rearrange("p (h n) -> p h n", h=4)
                        h0 = 8 * c + 4 * half
                        act.activation(k96[:, t, :].rearrange("p (h n) -> p h n", h=MH)[:, h0:h0 + 4, 0:MNOPE],
                                       v[:, :, 0:MNOPE], ACT.Copy)
                        act.activation(Vm[:, t, 64 * h0:64 * h0 + 256].rearrange("p (h n) -> p h n", h=4),
                                       v[:, :, MNOPE:P], ACT.Copy).then_inc(drain_sem(nm), 1)
                if c == 0:
                    squares96(0, q96)
            turned96("qT", qTm, gq8[0:MQK, 5:6])
            for t, half in ((0, 1), (1, 0), (1, 1)):
                emptied(act, ("KV", 1, t, half))
            squares96(1, k96)
            turned96("kT", kTm, colB[0:MQK, B_MK:B_MK + 1])
            for i in range(MH + 4):
                if 1 <= i <= MH:
                    u = unitm(i - 1)
                    bk = full(act, ("S", u))
                    if i > 3:
                        full(act, ("T", u - 3))
                    exps(u, lambda t: bk[:, S * t:S * t + S], lambda t: Pm[u % 3][:, t, :])
                if 2 <= i < MH + 2:
                    u = unitm(i - 2)
                    bt = full(act, ("T", u))
                    act.activation(PTm[u % 2][:, :, :], bt[:, :].rearrange("p (a s) -> p a s", a=2), ACT.Copy)\
                       .then_inc(drain_sem(("T", u)), 1)
                if i >= 5 and i % 2:
                    at_high(unitm(i - 5) // 2, (i - 5) // 2)
            gate_rows(0, gbc0)
            wo(0)
            mlp(0)

            norm_sums(6, sqd)
            norm_high(6)

            def bias_load(n):
                if n >= 2:
                    act.wait_ge(s_nmax, unitd(n - 2) + 1)
                act.dma_start(biasb[n % 2][:, :, :], bias_dram[:, n, :, :].rearrange("t p k -> p t k"))\
                   .then_inc(s_bld[n % 2], 16)

            todo = []

            def qk_out(j, g, m3):
                r = 8 + 6 * j + 2 * g + m3
                bk = full(act, ("qkT", r))
                dst, col = (qTd[j % 2], gq8[:, 2 + g:3 + g]) if m3 == 0 else (kTd[j % 2], colB[:, B_DK + g:B_DK + g + 1])
                act.activation(dst[:, g, :, :], bk[:, :].rearrange("p (a s) -> p a s", a=2), ACT.Copy,
                               scale=col).then_inc(drain_sem(("qkT", r)), 1)

            def project(chunk_name):
                _, j, g, m3 = chunk_name
                split_ahead(chunk_name)
                if m3 < 2:
                    r = 8 + 6 * j + 2 * g + m3
                    head_squares(chunk_name, r, sqh2[r % 2])
                else:
                    bk = full(act, chunk_name)
                    act.activation(Vd[j % 2][:, g, :, :], bk[:, :].rearrange("p (t n) -> p t n", t=TT), ACT.Copy)\
                       .then_inc(drain_sem(chunk_name), 1)
                if todo:
                    qk_out(*todo.pop(0))
                if m3 < 2:
                    todo.append((j, g, m3))

            def head_exps(j, i):
                u = unitd(HB * j + i)
                exps(u, lambda t: Ld[u % 2][:, t, :], lambda t: Ld[u % 2][:, t, :])
                if HB * j + i + 2 < DH:
                    bias_load(HB * j + i + 2)

            def turn_probs(j, i):
                u = unitd(HB * j + i)
                for g in range(NG):
                    bk = full(act, ("T", u, g))
                    act.activation(PTd[:, g, :, :], bk[:, :].rearrange("p (a s) -> p a s", a=2), ACT.Copy)\
                       .then_inc(drain_sem(("T", u, g)), 1)

            for n in range(2):
                bias_load(n)
            dilated(project, idle, head_exps, turn_probs, idle,
                    lambda j, p: at_high(unitd(HB * j + 2 * p) // 2, 2 * j + p), idle)
            gate_rows(2, gbc)
            wo(1)
            mlp(1)

        @block.vector
        def _(dve):
            steps, split_next, e = [0], [0], [0]

            def link(ins):
                steps[0] += 1
                ins.then_inc(s_dc, 1)
                dve.wait_ge(s_dc, steps[0])

            def split_ahead(name, ahead=2):
                while split_next[0] <= min(chunk_at[name] + ahead, len(chunks) - 1):
                    c = split_next[0]
                    split_next[0] += 1
                    dve.wait_ge(s_hi, c + 1)
                    dve.tensor_tensor(view(wlo[c % SPL], c), view(raw[c % RAW], c), view(whi[c % SPL], c).bitcast(F32),
                                      ALU.subtract).then_inc(s_lo, 1)

            def mean_square(src, width, n):
                i = e[0]
                e[0] += 1
                dve.tensor_scalar(ms[:, i % 2, 0:width], src, 1.0 / n, EPS, ALU.mult, ALU.add).then_inc(s_ms, 1)
                return i

            def rms(src, width, n):
                i = mean_square(src, width, n)
                dve.wait_ge(s_rstd, i + 1)
                return rstd[:, i % 2, :]

            def norm(ev, xn):
                dve.wait_ge(s_ss, 2 * ev + 2)
                r = rms(ss[:, 0, 0:TT], TT, D)
                for t in range(TT):
                    dve.tensor_scalar(xn[:, t, :], x[:, t, :], r[:, t:t + 1], None, ALU.mult).then_inc(s_xn, 1)

            def bias_out(l, u):
                nm = ("B", l, u)
                bk = full(dve, nm)
                m = (NU * l + u) // 4
                if u % 4 == 0 and m >= 2:
                    dve.wait_ge(s_bout[m % 2], 16 * NG * (m // 2))
                k0 = 8 * (u % 4)
                dve.tensor_tensor(stage[m % 2][:, :, k0:k0 + 8].rearrange("p (g h) k -> p g h k", g=NG),
                                  bk[:, 0:8 * NG * DH].rearrange("p (k g h) -> p g h k", k=8, g=NG),
                                  dmask[:, :, 8 * u:8 * u + 8].unsqueeze(2).broadcast_to([P, NG, DH, 8]), ALU.add)\
                   .then_inc(drain_sem(nm), 1)

            hc = [0]

            def h_low(src, dst_lo, dst_hi, scale=None):
                hc[0] += 1
                dve.wait_ge(s_hhi, hc[0])
                if scale is None:
                    dve.tensor_tensor(dst_lo, src, dst_hi.bitcast(F32), ALU.subtract).then_inc(s_hlo, 1)
                else:
                    dve.scalar_tensor_tensor(out=dst_lo, in0=src, scalar=scale, in1=dst_hi.bitcast(F32), op0=ALU.mult,
                                             op1=ALU.subtract).then_inc(s_hlo, 1)

            def norm_out(names, gain, shift, tiles):
                def low(kp, w):
                    h_low(h32[kp % 2][:, 0:w, :], hT_lo[:, 2 * kp:2 * kp + w, :], hT_hi[:, 2 * kp:2 * kp + w, :])

                for kp, nm in enumerate(names):
                    w = min(2, tiles - 2 * kp)
                    bk = full(dve, nm)
                    if kp >= 2:
                        dve.wait_ge(s_hlo, hc[0])
                    for i in range(w):
                        k = 2 * kp + i
                        b = bk[:, S * i:S * i + S]
                        if shift is None:
                            ins = dve.tensor_scalar(h32[kp % 2][:, i, :], b, gain(k), None, ALU.mult)
                        else:
                            ins = dve.tensor_scalar(h32[kp % 2][:, i, :], b, gain(k), shift(k), ALU.mult, ALU.add)
                        if i < w - 1:
                            link(ins)
                    ins.then_inc(drain_sem(nm), 1)
                    if kp:
                        low(kp - 1, 2)
                low(kp, w)

            unfinished = []

            def finish_head_norm():
                if not unfinished:
                    return
                i, job, r, buf = unfinished.pop(0)
                dve.wait_ge(s_rstd, i + 1)
                rr = rstd[:, i % 2, :]
                bk = full(dve, job)
                if r >= 2:
                    full(dve, ("qkT", r - 2))
                dve.tensor_tensor(buf[:, :, :].rearrange("p t (h n) -> p (t h) n", n=HD),
                                  bk[:, :].rearrange("p (a n) -> p a n", n=HD),
                                  rr[:, 0:8].unsqueeze(2).broadcast_to([P, 8, HD]), ALU.mult)\
                   .then_inc(drain_sem(job), 1)

            def begin_head_norm(job, r, sqbuf, buf):
                dve.wait_ge(s_sq, r + 1)
                dve.tensor_reduce(ss[:, 1, 0:8], sqbuf[:, :].rearrange("p (a n) -> p a n", n=HD), AX, ALU.add)\
                   .then_inc(s_hn, 1)
                dve.wait_ge(s_hn, r + 1)
                unfinished.append((mean_square(ss[:, 1, 0:8], 8, HD), job, r, buf))

            def invert_sums(u):
                dve.wait_ge(s_exp, 2 * u + 2)
                if u >= 2:
                    emptied(dve, ("O", u - 2))
                dve.reciprocal(rz[:, u % 2, :], zsum[:, u % 2, :]).then_inc(s_rz, 1)

            def scale_out(u):
                bk = full(dve, ("O", u))
                dve.wait_ge(s_rz, u + 1)
                dve.tensor_tensor(h32[u // 2 % 2][:, 0, :].rearrange("p (t n) -> p t n", t=TT)[:, :, HD * (u % 2):HD * (u % 2) + HD],
                                  bk[:, 0:TT * HD].rearrange("p (t n) -> p t n", t=TT),
                                  rz[:, u % 2, :].unsqueeze(2).broadcast_to([P, TT, HD]), ALU.mult)\
                   .then_inc(drain_sem(("O", u)), 1)

            def at_low(pair, k):
                bk = full(dve, ("OT", pair))
                dve.wait_ge(s_athi, pair + 1)
                dve.tensor_tensor(aT_lo[:, k, :], bk[:, 0:S], aT_hi[:, k, :].bitcast(F32), ALU.subtract)\
                   .then_inc(drain_sem(("OT", pair)), 1)

            dve.wait_ge(s_freq, 32)
            link(dve.tensor_copy(posf[:, :], pos_t[:, :]))
            link(dve.tensor_tensor(ang[:, 0, :].rearrange("p (t f) -> p t f", t=TT),
                                   posf[:, :].unsqueeze(2).broadcast_to([P, TT, 16]),
                                   freq[:, :].unsqueeze(1).broadcast_to([P, TT, 16]), ALU.mult))
            two_pi = 6.283185307179586
            c1 = 6.28125
            c2 = 0.0019350051879882812
            c3 = two_pi - c1 - c2
            link(dve.tensor_scalar(ang[:, 1, :], ang[:, 0, :], 1.0 / two_pi, None, ALU.mult))
            link(dve.tensor_copy(angi[:, :], ang[:, 1, :]))
            link(dve.tensor_copy(ang[:, 1, :], angi[:, :]))
            link(dve.scalar_tensor_tensor(out=ang[:, 2, :], in0=ang[:, 1, :], scalar=-c1, in1=ang[:, 0, :], op0=ALU.mult, op1=ALU.add))
            link(dve.scalar_tensor_tensor(out=ang[:, 0, :], in0=ang[:, 1, :], scalar=-c2, in1=ang[:, 2, :], op0=ALU.mult, op1=ALU.add))
            link(dve.scalar_tensor_tensor(out=ang[:, 2, :], in0=ang[:, 1, :], scalar=-c3, in1=ang[:, 0, :], op0=ALU.mult, op1=ALU.add))

            def wrap(dst, src):
                link(dve.tensor_scalar(ang[:, 5, :], src, two_pi / 2, -two_pi, ALU.is_gt, ALU.mult))
                link(dve.tensor_tensor(ang[:, 5, :], ang[:, 5, :], src, ALU.add))
                link(dve.tensor_scalar(dst, ang[:, 5, :], -two_pi / 2, two_pi, ALU.is_lt, ALU.mult))
                link(dve.tensor_tensor(dst, dst, ang[:, 5, :], ALU.add))
                link(dve.tensor_scalar(dst, dst, 3.1415925, -3.1415925, ALU.min, ALU.max))

            wrap(ang[:, 3, :], ang[:, 2, :])
            link(dve.tensor_scalar(ang[:, 0, :], ang[:, 2, :], two_pi / 4, None, ALU.add))
            wrap(ang[:, 4, :], ang[:, 0, :])
            dve.tensor_copy(ang[:, 5, 0:1], ang[:, 4, 0:1]).then_inc(s_ropein, 1)

            def mods_half(h):
                i, which = divmod(h, 2)
                bk = full(dve, ("mod", h))
                c0 = 24 * which
                dve.tensor_tensor(mods[:, i, c0:c0 + 24], bk[:, 0:24], colB[:, b_ada(i) + c0:b_ada(i) + c0 + 24], ALU.add)\
                   .then_inc(drain_sem(("mod", h)), 1)
                emptied(dve, ("mod", h))
                c1 = (c_mix2, c_mlp2)[which](i)
                dve.scalar_tensor_tensor(out=gain2[:, i, which, :], in0=mods[:, i, c0 + 8:c0 + 16], scalar=1.0,
                                         in1=colA[:, c1:c1 + 8], op0=ALU.add, op1=ALU.mult).then_inc(s_mods, 1)
                dve.wait_ge(s_mods, h + 1)

            for l in range(DEPTH):
                if l:
                    split_ahead(("F", l))
                norm(2 * l, xn1)
                if l == 0:
                    split_ahead(("F", 0), 1)
                    emptied(dve, "colA")
                    emptied(dve, "colB")
                    link(dve.tensor_scalar(gq8[:, 0:2], colB[:, B_Q1:B_Q1 + 2], HD ** -0.5, None, ALU.mult))
                    link(dve.tensor_scalar(gq8[:, 2:5], colB[:, B_DQ:B_DQ + 3], HD ** -0.5, None, ALU.mult))
                    link(dve.tensor_scalar(gq8[:, 5:6], colB[:, B_MQ:B_MQ + 1], MQK ** -0.5, None, ALU.mult))
                norm_out([("nrm", 2 * l, kp) for kp in range(4)], lambda k: colA[:, c_mix(l) + k:c_mix(l) + k + 1], None, DK)
                split_ahead(("F", l))
                bk = full(dve, ("F", l))
                dve.wait_ge(s_rope, 2)
                dve.tensor_scalar(zf[:, :], bk[0:H1, 0:S], fb[:, l:l + 1], None, ALU.add).then_inc(drain_sem(("F", l)), 1)
                emptied(dve, ("F", l))
                link(dve.memset(zero8[:, :], 0.0))
                dve.tensor_scalar(mf[:, :], zf[:, :], 0.0, None, ALU.min).then_inc(s_z, 1)
                dve.wait_ge(s_zt, l + 1)
                link(dve.tensor_tensor(mf[:, :], tf[:, :], mf[:, :], ALU.subtract))
                dve.tensor_tensor_scan(ncum[:, :], mf[:, :], zero8[:, :], 0.0, ALU.add, ALU.add).then_inc(s_cum, 1)
                for i, (nm, c) in enumerate([("Q", 0), ("Q", 1), ("K", 0), ("K", 1)]):
                    finish_head_norm()
                    split_ahead((nm, l, c))
                    begin_head_norm((nm, l, c), 4 * l + i, sqh[i % 2], qn[i % 2])
                for c in range(2):
                    finish_head_norm()
                    split_ahead(("V", l, c))
                split_ahead(("PX", l))
                split_ahead(("CX", l))
                split_ahead(("CC", l))
                bk = full(dve, ("CC", l))
                emptied(dve, ("CX", l))
                link(dve.memset(zc[:, :, 0:2], 0.0))
                dve.tensor_tensor(zc[:, :, 2:], bk[:, :].rearrange("p (a s) -> p a s", a=2), cxs[:, :, :], ALU.mult)\
                   .then_inc(drain_sem(("CC", l)), 1)
                split_ahead(("CB", l))
                emptied(dve, ("CC", l))
                for j in range(3):
                    for i in range(2):
                        col = colA[:, c_conv(l, j) + i:c_conv(l, j) + i + 1]
                        if j == 0:
                            link(dve.tensor_scalar(cva[:, i, :], zc[:, i, 0:S], col, None, ALU.mult))
                        else:
                            link(dve.scalar_tensor_tensor(out=(cvb, cva)[j - 1][:, i, :], in0=zc[:, i, j:j + S], scalar=col,
                                                          in1=(cva, cvb)[j - 1][:, i, :], op0=ALU.mult, op1=ALU.add))
                emptied(dve, ("CB", l))
                dve.tensor_tensor(cvb[:, :, :], cva[:, :, :], cbs[:, :, :], ALU.mult).then_inc(s_cv, 1)
                segs = ((0, P), (P, 3 * P))
                g = 0
                for i in range(H1 + 3):
                    if i < H1:
                        u = unit1(l, i)
                        bk = full(dve, ("S", u))
                        if i >= 2:
                            dve.wait_ge(s_exp, 2 * (u - 2) + 2)
                        for t, (a, b) in enumerate(segs):
                            ins = dve.tensor_tensor_reduce(L1[u % 2][:, a:b], bk[:, a:b], causal[:, a:b], 1.0, NEG,
                                                           ALU.add, ALU.max, mx[:, u % 2, t:t + 1])
                            if t == 0:
                                link(ins)
                        ins.then_inc(drain_sem(("S", u)), 1)
                        emptied(dve, ("S", u))
                        dve.tensor_scalar(nmax[:, u % 2, :], mx[:, u % 2, :], -1.0, None, ALU.mult).then_inc(s_nmax, 1)
                    if g < 12:
                        split_ahead(("G", l, g))
                        g += 1
                    if 1 <= i <= H1:
                        invert_sums(unit1(l, i - 1))
                    if g < 12 and i % 4 == 0:
                        split_ahead(("G", l, g))
                        g += 1
                    if 2 <= i < H1 + 2:
                        scale_out(unit1(l, i - 2))
                    if i >= 4 and i % 2 == 0:
                        at_low(unit1(l, i - 4) // 2, (i - 4) // 2)
                while g < 12:
                    split_ahead(("G", l, g))
                    g += 1
                dve.wait_ge(s_cvhi, l + 1)
                dve.tensor_tensor(aT_lo[:, 4:6, :], cvb[:, :, :], aT_hi[:, 4:6, :].bitcast(F32), ALU.subtract).then_inc(s_cvlo, 1)
                emptied(dve, ("G", l, 11))
                emptied(dve, ("G", l, 10))
                emptied(dve, ("G", l, 9))
                for gi in range(4):
                    bk = full(dve, ("YP", l, gi))
                    for i in range(2):
                        k = 2 * gi + i
                        ins = dve.tensor_scalar(mt[gi % 2][:, i, :], bk[:, S * i:S * i + S],
                                                colA[:, c_psc(l) + k:c_psc(l) + k + 1], None, ALU.mult)
                        if i == 0:
                            link(ins)
                    ins.then_inc(drain_sem(("YP", l, gi)), 1)
                    emptied(dve, ("YP", l, gi))
                    m2 = mg[:, 2 * gi:2 * gi + 2, :]
                    link(dve.scalar_tensor_tensor(out=m2, in0=m2, scalar=1.0, in1=mt[gi % 2][:, :, :], op0=ALU.add, op1=ALU.mult))
                split_ahead(("CO", l))
                for br, what in ((1, "YC"), (0, "YA")):
                    for jp in range(4):
                        nm = (what, l, jp)
                        if what == "YA" and jp % 2 == 0:
                            split_ahead(("AO", l, jp // 2))
                        bk = full(dve, nm)
                        gt = gates[:, DK * br + 2 * jp:DK * br + 2 * jp + 2, :]
                        dve.scalar_tensor_tensor(out=mt[jp % 2][:, :, :], in0=gt, scalar=1.0,
                                                 in1=bk[:, :].rearrange("p (a s) -> p a s", a=2), op0=ALU.add,
                                                 op1=ALU.mult).then_inc(drain_sem(nm), 1)
                        emptied(dve, nm)
                        m2 = mg[:, 2 * jp:2 * jp + 2, :]
                        ins = dve.tensor_tensor(m2, m2, mt[jp % 2][:, :, :], ALU.add)
                        if br:
                            link(ins)
                        else:
                            ins.then_inc(s_mg, 1)
                            h_low(m2, hT_lo[:, 2 * jp:2 * jp + 2, :], hT_hi[:, 2 * jp:2 * jp + 2, :], 0.5)
                for c in range(4):
                    nm = ("WO", l, c)
                    split_ahead(nm)
                    bk = full(dve, nm)
                    xs = x[:, :, 256 * c:256 * c + 256]
                    dve.tensor_tensor(xs, xs, bk[:, :].rearrange("p (t n) -> p t n", t=TT), ALU.add).then_inc(drain_sem(nm), 1)
                norm(2 * l + 1, xnf)
                norm_out([("nrm", 2 * l + 1, kp) for kp in range(4)], lambda k: colA[:, c_ffn(l) + k:c_ffn(l) + k + 1], None, DK)
                dve.wait_ge(s_bin, BIN * (l + 1))
                link(dve.tensor_single_scalar(ihi[:, :], posb[:, :], 16, ALU.arith_shift_right))
                link(dve.tensor_single_scalar(ilo[:, :], posb[:, :], 65535, ALU.bitwise_and))
                link(dve.tensor_copy(hi16[:, :], ihi[:, :]))
                link(dve.tensor_copy(lo16[:, :], ilo[:, :]))
                link(dve.tensor_scalar(relk[:, :], hi16[:, :], hi16[:, 0:1], 65536.0, ALU.subtract, ALU.mult))
                link(dve.tensor_scalar(relq[:, :], lo16[:, :], lo16[:, 0:1], None, ALU.subtract))
                link(dve.tensor_tensor(relk[:, :], relk[:, :], relq[:, :], ALU.add))
                link(dve.tensor_scalar(relq[:, :], relk[:, :], thr[:, 0:1], None, ALU.add))
                bk = full(dve, ("steps", l))
                dve.tensor_copy(dres[:, 0, :], bk[0:96, 0:NG * DH]).then_inc(drain_sem(("steps", l)), 1)
                emptied(dve, ("steps", l))
                for n in range(3):
                    link(dve.tensor_copy(dpart[:, n, :], dres[:, n, :]))
                    if n < 2:
                        link(dve.tensor_tensor(dres[:, n + 1, :], dres[:, n, :], dpart[:, n, :], ALU.subtract))
                    link(dve.tensor_copy(dsel[32 * n:32 * n + 32, :], dpart[32 * n:32 * n + 32, n, :]))

                def steps_of(u):
                    if u >= NU:
                        return
                    if u >= 2:
                        full(dve, ("B", l, u - 2))
                    dve.tensor_tensor(Gst[(NU * l + u) % 2][:, :, :],
                                      relk[:, 8 * u:8 * u + 8].unsqueeze(2).broadcast_to([96, 8, P]),
                                      relq[:, P * l:P * l + P].unsqueeze(1).broadcast_to([96, 8, P]), ALU.is_ge)\
                       .then_inc(s_g, 1)

                steps_of(0)
                for c in range(NF1 + 1):
                    if c < NF1:
                        split_ahead(("GT", l, c))
                        steps_of(3 * c + 1)
                        if c:
                            bias_out(l, 3 * c - 1)
                        split_ahead(("UP", l, c))
                        steps_of(3 * c + 2)
                        bias_out(l, 3 * c)
                        emptied(dve, ("GT", l, c))
                        nm = ("UP", l, c)
                        bk = full(dve, nm)
                        dve.tensor_tensor(h32[c % 2][:, :, :], bk[:, :].rearrange("p (a s) -> p a s", a=2), sg[c % 2][:, :, :],
                                          ALU.mult).then_inc(drain_sem(nm), 1)
                        emptied(dve, nm)
                        dve.wait_ge(s_hidhi, NF1 * l + c + 1)
                        sl = 2 * (c % 3)
                        dve.tensor_tensor(aT_lo[:, sl:sl + 2, :], h32[c % 2][:, :, :], aT_hi[:, sl:sl + 2, :].bitcast(F32),
                                          ALU.subtract).then_inc(s_hidlo, 1)
                    if c:
                        split_ahead(("DN", l, c - 1))
                    if c < NF1:
                        steps_of(3 * c + 3)
                        bias_out(l, 3 * c + 1)
                for q in range(4):
                    nm = ("DN", l, "sum", q)
                    t, half = divmod(q, 2)
                    bk = full(dve, nm)
                    xs = x[:, t, 512 * half:512 * half + 512]
                    dve.tensor_tensor(xs, xs, bk[:, :], ALU.add).then_inc(drain_sem(nm), 1)
                for i in range(2):
                    dve.wait_ge(s_bout[i], 16 * NG * NU // 8 * (l + 1))
                mods_half(l)

            def norm2(ev, i, which, xn):
                norm(ev, xn)
                norm_out([("nrm", ev, kp) for kp in range(4)], lambda k: gain2[:, i, which, k:k + 1],
                         lambda k: mods[:, i, 24 * which + k:24 * which + k + 1], DK)

            def wo(i):
                emptied(dve, ("gb", 2 * i, 1))
                emptied(dve, ("gb", 2 * i, 0))
                for c in range(4):
                    nm = ("MO", i, c)
                    split_ahead(nm)
                    bk = full(dve, nm)
                    y = (gy0, gy1)[i][c % 2]
                    rows = (gbc0, gbc)[i]
                    dve.tensor_tensor(y[:, :, :], bk[:, :].rearrange("p (t n) -> p t n", t=TT),
                                      rows[:, 256 * c:256 * c + 256].unsqueeze(1).broadcast_to([P, TT, 256]), ALU.mult)\
                       .then_inc(drain_sem(nm), 1)
                    emptied(dve, nm)
                    xs = x[:, :, 256 * c:256 * c + 256]
                    ins = dve.tensor_tensor(xs, xs, y[:, :, :], ALU.add)
                    if c < 3:
                        link(ins)
                    else:
                        ins.then_inc(s_x2, 1)

            def ada_step(q):
                k, cb = divmod(q, 3)
                dve.wait_ge(s_adav[q % AV], 16 * (q // AV + 1))
                acc, w = ada_acc2[1][:, D * cb:D * cb + D], ada_rawv[q % AV][:, :]
                if q >= 3:
                    dve.wait_ge(s_adastep, q - 2)
                    ins = dve.scalar_tensor_tensor(out=acc, in0=w, scalar=csil[:, k:k + 1], in1=acc, op0=ALU.mult, op1=ALU.add)
                else:
                    ins = dve.tensor_scalar(acc, w, csil[:, k:k + 1], None, ALU.mult)
                ins.then_inc(s_adastep, 1)

            def mlp(i):
                norm2(5 + 2 * i, i, 1, xnp)
                for c in range(NF2 + 1):
                    if c < NF2:
                        nm = ("M1", i, c)
                        split_ahead(nm)
                        emptied(dve, nm)
                        dve.tensor_tensor(h32[c % 2][:, :, :], rl[c % 2][:, :, :], rl[c % 2][:, :, :], ALU.mult)\
                           .then_inc(s_hid32, 1)
                        dve.wait_ge(s_hidhi, 2 * NF1 + NF2 * i + c + 1)
                        sl = 2 * (c % 3)
                        dve.tensor_tensor(aT_lo[:, sl:sl + 2, :], h32[c % 2][:, :, :], aT_hi[:, sl:sl + 2, :].bitcast(F32),
                                          ALU.subtract).then_inc(s_hidlo, 1)
                    if c:
                        split_ahead(("M2", i, c - 1))
                    if i == 0 and c >= 2:
                        for q in range(2 * (c - 2), min(2 * (c - 2) + 2, NP_ADA)):
                            ada_step(q)
                emptied(dve, ("gb", 2 * i + 1, 1))
                for q in range(4):
                    nm = ("M2", i, "sum", q)
                    t, half = divmod(q, 2)
                    bk = full(dve, nm)
                    dve.tensor_tensor(gy2[:, :], bk[:, :], gbc2[:, 512 * half:512 * half + 512], ALU.mult)\
                       .then_inc(drain_sem(nm), 1)
                    emptied(dve, nm)
                    xs = x[:, t, 512 * half:512 * half + 512]
                    ins = dve.tensor_tensor(xs, xs, gy2[:, :], ALU.add)
                    if i == DEPTH - 1:
                        ins.then_inc(s_final, 1)
                        dve.wait_ge(s_final, q + 1)
                    elif half:
                        ins.then_inc(s_x2, 1)
                        dve.wait_ge(s_x2, 2 + t)
                    else:
                        link(ins)

            norm2(4, 0, 0, xnm)
            for c in range(3):
                split_ahead(("LI", c))
            dve.wait_ge(s_latss, 1)
            for n, wdt in ((0, QL), (1, KVL)):
                link(dve.tensor_scalar(ss[:, 1, n:n + 3:2], ss[:, 0, n:n + 3:2], 1.0 / wdt, None, ALU.mult))
            r = rms(ss[:, 1, 0:4], 4, 1)
            for t in range(TT):
                for n, (a, b) in enumerate(((0, QL), (QL, QL + KVL))):
                    ins = dve.tensor_scalar(latn[:, t, a:b], lat[:, t, a:b], r[:, 2 * t + n:2 * t + n + 1], None, ALU.mult)
                    if (t, n) != (1, 1):
                        link(ins)
            ins.then_inc(s_latn, 1)
            norm_out([("latT", kp) for kp in range(3)],
                     lambda k: colA[:, C_QA + k:C_QA + k + 1], None, 5)

            def rotate(src, dst, heads):
                cb = cosn[:, :, :].unsqueeze(2).broadcast_to([P, TT, heads, 16])
                sbn = sinn[:, :, :].unsqueeze(2).broadcast_to([P, TT, heads, 16])

                def r4(i):
                    return rt[:, i, 0:TT * heads * 16].rearrange("p (t h f) -> p t h f", t=TT, h=heads)

                a, b = src[:, :, :, 0:16], src[:, :, :, 16:32]
                link(dve.tensor_tensor(r4(0), a, cb, ALU.mult))
                link(dve.tensor_tensor(r4(1), b, sbn, ALU.mult))
                link(dve.tensor_tensor(r4(2), b, cb, ALU.mult))
                link(dve.tensor_tensor(r4(3), a, sbn, ALU.mult))
                link(dve.tensor_tensor(dst[:, :, :, 0:16], r4(0), r4(1), ALU.subtract))
                return dve.tensor_tensor(dst[:, :, :, 16:32], r4(2), r4(3), ALU.add)

            emptied(dve, ("LI", 2))
            link(rotate(lat[:, :, QL + KVL:].unsqueeze(2), krope[:, :, :].unsqueeze(2), 1))
            for c in range(4):
                split_ahead(("QB", c))
            q4 = q96[:, :, :].rearrange("p t (h n) -> p t h n", h=MH)
            for t in range(TT):
                emptied(dve, ("QB", 3, t))
                emptied(dve, ("QB", 2, t))

            def norm96(n, buf):
                for t in range(TT):
                    dve.wait_ge(s_sq96, 2 * n + t + 1)
                    dve.tensor_reduce(ss[:, 1, MH * t:MH * t + MH], sq96[:, :].rearrange("p (h n) -> p h n", h=MH), AX,
                                      ALU.add).then_inc(s_sum96, 1)
                dve.wait_ge(s_sum96, 2 * n + 2)
                rr = rms(ss[:, 1, :], 32, MQK)
                q3 = buf[:, :, :].rearrange("p t (h n) -> p (t h) n", h=MH)
                dve.tensor_tensor(q3, q3, rr[:, 0:32].unsqueeze(2).broadcast_to([P, 32, MQK]), ALU.mult).then_inc(s_q96, 1)

            rotate(q4[:, :, :, MNOPE:], q4[:, :, :, MNOPE:], MH).then_inc(s_roped, 1)
            k4 = k96[:, :, :].rearrange("p t (h n) -> p t h n", h=MH)
            dve.tensor_copy(k4[:, :, :, MNOPE:], krope[:, :, :].unsqueeze(2).broadcast_to([P, TT, MH, MROPE]))\
               .then_inc(s_roped, 1)
            dve.wait_ge(s_roped, 2)
            norm96(0, q96)
            for c in range(2):
                split_ahead(("KV", c))
            for c, t, half in ((1, 0, 1), (1, 1, 0), (1, 1, 1)):
                emptied(dve, ("KV", c, t, half))
            norm96(1, k96)
            for i in range(MH + 4):
                if 2 <= i < MH + 2:
                    u = unitm(i - 2)
                    dve.wait_ge(s_exp, 2 * u + 2)
                    emptied(dve, ("O", u - 2))
                    dve.reciprocal(rz[:, u % 2, 0:1], zsum[:, u % 2, 0:1]).then_inc(drain_sem(("S", u)), 1)
                    dve.reciprocal(rz[:, u % 2, 1:2], zsum[:, u % 2, 1:2]).then_inc(s_rz, 1)
                    emptied(dve, ("S", u))
                if i < MH:
                    u = unitm(i)
                    bk = full(dve, ("S", u))
                    dve.tensor_reduce(nmax[:, u % 2, :], bk[:, :].rearrange("p (t k) -> p t k", t=TT), AX, ALU.max, negate=True)\
                       .then_inc(s_nmax, 1)
                if 3 <= i < MH + 3:
                    scale_out(unitm(i - 3))
                if i >= 5 and i % 2:
                    at_low(unitm(i - 5) // 2, (i - 5) // 2)
            wo(0)
            mlp(0)
            mods_half(2)
            mods_half(3)

            norm2(6, 1, 0, xnd)

            def project(chunk_name):
                _, j, g, m3 = chunk_name
                finish_head_norm()
                split_ahead(chunk_name)
                if m3 < 2:
                    r = 8 + 6 * j + 2 * g + m3
                    begin_head_norm(chunk_name, r, sqh2[r % 2], qn2[r % 2])

            def scores(j, i):
                n = HB * j + i
                u = unitd(n)
                dve.wait_ge(s_bld[n % 2], 16 * (n // 2 + 1))
                if n >= 2:
                    full(dve, ("T", u - 2, NG - 1))
                for g in range(NG):
                    bk = full(dve, ("S", u, g))
                    dve.tensor_tensor(Ld[u % 2][:, :, S * g:S * g + S], bk[:, :].rearrange("p (t k) -> p t k", t=TT),
                                      biasb[n % 2][:, :, S * g:S * g + S], ALU.add).then_inc(drain_sem(("S", u, g)), 1)
                for g in range(NG):
                    emptied(dve, ("S", u, g))
                dve.tensor_reduce(nmax[:, u % 2, :], Ld[u % 2][:, :, :], AX, ALU.max, negate=True).then_inc(s_nmax, 1)

            def values(j, i):
                finish_head_norm()
                invert_sums(unitd(HB * j + i))
                scale_out(unitd(HB * j + i))

            dilated(project, scores, idle, idle, values,
                    lambda j, p: at_low(unitd(HB * j + 2 * p) // 2, 2 * j + p), idle)
            wo(1)
            mlp(1)


NAMES = ["x", "norm_mix_g", "w_in", "forget_b", "q_norm_g", "k_norm_g", "w_attn_out", "conv_w", "w_conv_out", "pool_w",
         "pool_scale", "w_o", "norm_ffn_g", "w_ffn_in", "w_ffn_out", "c_2", "positions_2", "ada_w_2", "ada_b_2",
         "norm_mix_2", "norm_mlp_2", "mlp_w1_2", "mlp_w2_2", "mla_w_in_2", "mla_g_qa_2", "mla_w_qb_2", "mla_g_kva_2",
         "mla_w_kvb_2", "mla_g_q_2", "mla_g_k_2", "mla_w_o_2", "dil_w_in_2", "dil_g_q_2", "dil_g_k_2", "dil_w_o_2",
         "rel_bias_2"]


def kernel(**inputs):
    import numpy as np
    import concourse.bacc as bacc
    from concourse.bass_utils import run_bass_kernel_spmd

    nc = bacc.Bacc("TRN2", target_bir_lowering=False, num_devices=1)
    arrays, aps = {}, {}
    for name, a in [(n, inputs[n]) for n in NAMES] + list(host_constants().items()):
        a = np.ascontiguousarray(a)
        arrays[f"in_{name}"] = a
        aps[name] = nc.dram_tensor(f"in_{name}", a.shape, mybir.dt.from_np(a.dtype), kind="ExternalInput").ap()
    out = nc.dram_tensor("out_0", (1, S, D), F32, kind="ExternalOutput").ap()
    block_pair(nc, aps, out)
    r = run_bass_kernel_spmd(nc, [arrays], core_ids=[0])
    return r.results[0]["out_0"]
```
